# Optimizing a Trainium2 kernel written in Bass

```python
import jax, jax.numpy as jnp
from jax import lax
import numpy as np
import math

D_MODEL = 1024
BATCH = 1
SEQ = 256
DEPTH = 1

GRID_W = 64
CTX_LEN = 256
CONV_WIDTH = D_MODEL // 2
RET_HEADS = 4
RET_HEAD_DIM = (D_MODEL - CONV_WIDTH) // RET_HEADS
RET_WIDTH = RET_HEADS * RET_HEAD_DIM
MIX_WIDTH = CONV_WIDTH + RET_WIDTH
RET_CHUNK = 128
ROPE_BASE = 10000.0
N_EXPERTS = 16
EC_CAPACITY_FACTOR = 2
D_EXPERT = 2 * D_MODEL
RMS_EPS = 1e-6
GN_EPS = 1e-6
SPLITS = (CONV_WIDTH, CONV_WIDTH, CONV_WIDTH, RET_WIDTH, RET_WIDTH, RET_WIDTH, RET_WIDTH)
IN_COLS = sum(SPLITS)
SPLIT_IDX = tuple(int(s) for s in np.cumsum(SPLITS)[:-1])


def _rms_norm(x, g):
    xf = x.astype(jnp.float32)
    y = xf * lax.rsqrt(jnp.mean(xf * xf, axis=-1, keepdims=True) + RMS_EPS)
    return (y * g.astype(jnp.float32)).astype(x.dtype)

def _modulation(cond, w_ada, b_ada):
    m = jax.nn.silu(cond) @ w_ada + b_ada
    return jnp.split(m[:, None, :], 6, axis=-1)

def _rotary(t, pos):
    half = t.shape[-1] // 2
    inv = 1.0 / (ROPE_BASE ** (jnp.arange(half, dtype=jnp.float32) / half))
    ang = pos[:, None] * inv[None, :]
    cos = jnp.cos(ang)[None, :, None, :]
    sin = jnp.sin(ang)[None, :, None, :]
    t1, t2 = t[..., :half], t[..., half:]
    return jnp.concatenate([t1 * cos - t2 * sin, t1 * sin + t2 * cos], axis=-1)

def _ret_qkv(q, k, v, pos):
    b, n, _ = q.shape
    shp = (b, n, RET_HEADS, RET_HEAD_DIM)
    q = _rotary(q.reshape(shp).astype(jnp.float32), pos)
    k = _rotary(k.reshape(shp).astype(jnp.float32), pos) * (RET_HEAD_DIM ** -0.5)
    v = v.reshape(shp).astype(jnp.float32)
    return q, k, v

def _retention_scan(q, k, v, log_g, s0, include_self):
    b, n, h, d = q.shape
    nc = n // RET_CHUNK
    qc = q.reshape(b, nc, RET_CHUNK, h, d)
    kc = k.reshape(b, nc, RET_CHUNK, h, d)
    vc = v.reshape(b, nc, RET_CHUNK, h, d)
    idx = jnp.arange(RET_CHUNK, dtype=jnp.float32)
    rel = idx[:, None] - idx[None, :]
    mask = (rel >= 0) if include_self else (rel > 0)
    decay = jnp.where(mask[None], jnp.exp(log_g[:, None, None] * jnp.where(mask, rel, 0.0)[None]), 0.0)
    scores = jnp.einsum('bcihd,bcjhd->bchij', qc, kc) * decay[None, None]
    intra = jnp.einsum('bchij,bcjhd->bcihd', scores, vc)
    zeta = jnp.exp(log_g[None, :] * (RET_CHUNK - 1.0 - idx)[:, None])
    u = jnp.einsum('bcjhd,bcjhe->bchde', kc * zeta[None, None, :, :, None], vc)
    g_chunk = jnp.exp(log_g * RET_CHUNK)[None, :, None, None]

    def step(s, u_c):
        return g_chunk * s + u_c, s

    s_final, s_prev = lax.scan(step, s0, jnp.moveaxis(u, 1, 0))
    s_prev = jnp.moveaxis(s_prev, 0, 1)
    xi = jnp.exp(log_g[None, :] * (idx + 1.0)[:, None])
    inter = jnp.einsum('bcihd,bchde->bcihe', qc, s_prev) * xi[None, None, :, :, None]
    return (intra + inter).reshape(b, n, h, d), s_final

def _bidir_retention(q, k, v, log_gf, log_gb, s0_f, s0_b):
    y_f, s_f = _retention_scan(q, k, v, log_gf, s0_f, True)
    flip = lambda t: jnp.flip(t, axis=1)
    y_b, s_b = _retention_scan(flip(q), flip(k), flip(v), log_gb, s0_b, False)
    return y_f + flip(y_b), s_f, s_b

def _context_states(k, v, log_gf, log_gb):
    n = k.shape[1]
    pos = jnp.arange(n, dtype=jnp.float32)
    wf = jnp.exp(log_gf[None, :] * (n - 1.0 - pos)[:, None])
    wb = jnp.exp(log_gb[None, :] * pos[:, None])
    s_f = jnp.einsum('bnhd,nh,bnhe->bhde', k, wf, v)
    s_b = jnp.einsum('bnhd,nh,bnhe->bhde', k, wb, v)
    return s_f, s_b

def _ret_out(y, g, norm_g):
    b, n, _, _ = y.shape
    mu = jnp.mean(y, axis=-1, keepdims=True)
    var = jnp.mean(jnp.square(y - mu), axis=-1, keepdims=True)
    yn = ((y - mu) * lax.rsqrt(var + GN_EPS)).reshape(b, n, RET_WIDTH) * norm_g.astype(jnp.float32)
    return (jax.nn.silu(g.astype(jnp.float32)) * yn).astype(g.dtype)

def _conv_branch(gate_b, gate_c, u_in, w, bias, rows, width):
    bsz, n, ch = u_in.shape
    u = (gate_c * u_in).reshape(bsz, rows, width, ch)
    up = jnp.pad(u, ((0, 0), (0, 0), (1, 1), (0, 0)))
    y = up[:, :, :-2] * w[0] + up[:, :, 1:-1] * w[1] + up[:, :, 2:] * w[2] + bias
    return gate_b * y.reshape(bsz, n, ch)

def _expert_choice_ffn(h, w_router, b_router, w_gate, w_up, w_down):
    b, n, d = h.shape
    cap = max(1, EC_CAPACITY_FACTOR * n // N_EXPERTS)
    logits = h.astype(jnp.float32) @ w_router.astype(jnp.float32) + b_router.astype(jnp.float32)
    aff = jax.nn.softmax(logits, axis=-1)
    gate, idx = lax.top_k(jnp.swapaxes(aff, 1, 2), cap)
    xs = jax.vmap(lambda hb, ib: hb[ib])(h, idx)
    a = jnp.einsum('becd,edf->becf', xs, w_gate)
    u = jnp.einsum('becd,edf->becf', xs, w_up)
    y = jnp.einsum('becf,efd->becd', jax.nn.silu(a) * u, w_down) * gate[..., None].astype(h.dtype)
    return jax.vmap(lambda yb, ib: jnp.zeros((n, d), yb.dtype).at[ib.reshape(-1)].add(yb.reshape(-1, d)))(y, idx)

def first_inputs(seed: int = 0) -> dict:
    key = jax.random.key(seed)
    ks = jax.random.split(key, 22)
    f32 = jnp.float32

    def nrm(k, shape, scale):
        return jax.random.normal(k, shape, f32) * scale

    decay_base = jnp.log(2.0 ** (5.0 + jnp.arange(RET_HEADS, dtype=f32)) - 1.0)
    return {
        "x": nrm(ks[0], (BATCH, SEQ, D_MODEL), 1.0),
        "c": nrm(ks[1], (BATCH, D_MODEL), 1.0),
        "ctx": nrm(ks[2], (BATCH, CTX_LEN, D_MODEL), 1.0),
        "c_ctx": nrm(ks[3], (D_MODEL,), 1.0),
        "w_ada": nrm(ks[4], (DEPTH, D_MODEL, 6 * D_MODEL), 0.5 * D_MODEL ** -0.5),
        "b_ada": nrm(ks[5], (DEPTH, 6 * D_MODEL), 0.02),
        "pre_mix_g": 1.0 + nrm(ks[6], (DEPTH, D_MODEL), 0.05),
        "post_mix_g": 1.0 + nrm(ks[7], (DEPTH, D_MODEL), 0.05),
        "pre_ffn_g": 1.0 + nrm(ks[8], (DEPTH, D_MODEL), 0.05),
        "post_ffn_g": 1.0 + nrm(ks[9], (DEPTH, D_MODEL), 0.05),
        "w_in": nrm(ks[10], (DEPTH, D_MODEL, IN_COLS), D_MODEL ** -0.5),
        "conv_w": nrm(ks[11], (DEPTH, 3, CONV_WIDTH), 3.0 ** -0.5),
        "conv_b": nrm(ks[12], (DEPTH, CONV_WIDTH), 0.02),
        "ret_decay_logit": decay_base[None, None, :] + nrm(ks[13], (DEPTH, 2, RET_HEADS), 0.1),
        "ret_norm_g": 1.0 + nrm(ks[14], (DEPTH, RET_WIDTH), 0.05),
        "w_out": nrm(ks[15], (DEPTH, MIX_WIDTH, D_MODEL), MIX_WIDTH ** -0.5),
        "w_router": nrm(ks[16], (DEPTH, D_MODEL, N_EXPERTS), D_MODEL ** -0.5),
        "b_router": nrm(ks[17], (DEPTH, N_EXPERTS), 0.01),
        "w_gate": nrm(ks[18], (DEPTH, N_EXPERTS, D_MODEL, D_EXPERT), D_MODEL ** -0.5),
        "w_up": nrm(ks[19], (DEPTH, N_EXPERTS, D_MODEL, D_EXPERT), D_MODEL ** -0.5),
        "w_down": nrm(ks[20], (DEPTH, N_EXPERTS, D_EXPERT, D_MODEL), D_EXPERT ** -0.5),
    }

def first_block(x, c, ctx, c_ctx, w_ada, b_ada, pre_mix_g, post_mix_g, pre_ffn_g, post_ffn_g,
              w_in, conv_w, conv_b, ret_decay_logit, ret_norm_g, w_out,
              w_router, b_router, w_gate, w_up, w_down):
    n_lat = x.shape[1]
    ctx_len = ctx.shape[1]
    rows = n_lat // GRID_W
    pos_ctx = jnp.arange(ctx_len, dtype=jnp.float32)
    pos_lat = ctx_len + jnp.arange(n_lat, dtype=jnp.float32)
    bsz = x.shape[0]
    zero_state = jnp.zeros((bsz, RET_HEADS, RET_HEAD_DIM, RET_HEAD_DIM), jnp.float32)

    for i in range(DEPTH):
        last = i == DEPTH - 1
        sh1, sc1, g1, sh2, sc2, g2 = _modulation(c, w_ada[i], b_ada[i])
        csh1, csc1, cg1, csh2, csc2, cg2 = _modulation(c_ctx[None, :], w_ada[i], b_ada[i])
        log_gf = jax.nn.log_sigmoid(ret_decay_logit[i, 0].astype(jnp.float32))
        log_gb = jax.nn.log_sigmoid(ret_decay_logit[i, 1].astype(jnp.float32))

        hc = _rms_norm(ctx, pre_mix_g[i]) * (1.0 + csc1) + csh1
        c_b, c_c, c_x, c_q, c_k, c_v, c_g = jnp.split(hc @ w_in[i], SPLIT_IDX, axis=-1)
        qc, kc, vc = _ret_qkv(c_q, c_k, c_v, pos_ctx)
        if last:
            s_f, s_b = _context_states(kc, vc, log_gf, log_gb)
            ctx_next = ctx
        else:
            yc, s_f, s_b = _bidir_retention(qc, kc, vc, log_gf, log_gb, zero_state, zero_state)
            mix_c = jnp.concatenate([
                _conv_branch(c_b, c_c, c_x, conv_w[i], conv_b[i], 1, ctx_len),
                _ret_out(yc, c_g, ret_norm_g[i])], axis=-1) @ w_out[i]
            ctx_mid = ctx + cg1 * _rms_norm(mix_c, post_mix_g[i])
            hc2 = _rms_norm(ctx_mid, pre_ffn_g[i]) * (1.0 + csc2) + csh2
            ffn_c = _expert_choice_ffn(hc2, w_router[i], b_router[i], w_gate[i], w_up[i], w_down[i])
            ctx_next = ctx_mid + cg2 * _rms_norm(ffn_c, post_ffn_g[i])

        hx = _rms_norm(x, pre_mix_g[i]) * (1.0 + sc1) + sh1
        x_b, x_c, x_x, x_q, x_k, x_v, x_g = jnp.split(hx @ w_in[i], SPLIT_IDX, axis=-1)
        qx, kx, vx = _ret_qkv(x_q, x_k, x_v, pos_lat)
        yx, _, _ = _bidir_retention(qx, kx, vx, log_gf, log_gb, s_f, s_b)
        mix_x = jnp.concatenate([
            _conv_branch(x_b, x_c, x_x, conv_w[i], conv_b[i], rows, GRID_W),
            _ret_out(yx, x_g, ret_norm_g[i])], axis=-1) @ w_out[i]
        x = x + g1 * _rms_norm(mix_x, post_mix_g[i])
        hx2 = _rms_norm(x, pre_ffn_g[i]) * (1.0 + sc2) + sh2
        ffn_x = _expert_choice_ffn(hx2, w_router[i], b_router[i], w_gate[i], w_up[i], w_down[i])
        x = x + g2 * _rms_norm(ffn_x, post_ffn_g[i])
        ctx = ctx_next
    return x


CHUNK = 64
SSM_INNER = 1024
SSM_HEAD_DIM = 64
SSM_HEADS = SSM_INNER // SSM_HEAD_DIM
SSM_GROUPS = 2
SSM_STATE = 128
SSM_CONV = 4
SSM_CONV_DIM = SSM_INNER + 2 * SSM_GROUPS * SSM_STATE
LRU_WIDTH = 1024
LRU_BLOCKS = 16
LRU_BLOCK = LRU_WIDTH // LRU_BLOCKS
LRU_CONV = 4
LRU_C = 8.0
FFN_DIM = 3072
FFN_CONV = 3
N_BRANCHES = 2
IN_SPLITS = (
    SSM_INNER,
    SSM_INNER + SSM_CONV_DIM,
    SSM_INNER + SSM_CONV_DIM + SSM_HEADS,
    SSM_INNER + SSM_CONV_DIM + SSM_HEADS + LRU_WIDTH,
    SSM_INNER + SSM_CONV_DIM + SSM_HEADS + 2 * LRU_WIDTH,
)
N_IN = SSM_INNER + SSM_CONV_DIM + SSM_HEADS + 2 * LRU_WIDTH + N_BRANCHES * D_MODEL


def rmsnorm(x, w):
    xf = x.astype(jnp.float32)
    y = xf * lax.rsqrt(jnp.mean(xf * xf, axis=-1, keepdims=True) + RMS_EPS)
    return (y * w.astype(jnp.float32)).astype(x.dtype)

def causal_dwconv(x, w, b):
    k = w.shape[0]
    out = lax.conv_general_dilated(
        x, w[:, None, :].astype(x.dtype), window_strides=(1,), padding=[(k - 1, 0)],
        dimension_numbers=("NWC", "WIO", "NWC"), feature_group_count=x.shape[-1])
    return out + b

def ssd_chunked(xh, dt, a, bm, cm):
    b, s = xh.shape[:2]
    c = s // CHUNK
    e = SSM_HEADS // SSM_GROUPS
    x = xh.reshape(b, c, CHUNK, SSM_GROUPS, e, SSM_HEAD_DIM)
    dtc = dt.reshape(b, c, CHUNK, SSM_GROUPS, e)
    bc = bm.reshape(b, c, CHUNK, SSM_GROUPS, SSM_STATE)
    cc = cm.reshape(b, c, CHUNK, SSM_GROUPS, SSM_STATE)
    a_dt = (dtc * a.reshape(SSM_GROUPS, e)).transpose(0, 3, 4, 1, 2)
    a_cs = jnp.cumsum(a_dt, axis=-1)
    xdt = x * dtc[..., None]
    causal = jnp.tril(jnp.ones((CHUNK, CHUNK), dtype=bool))
    seg = a_cs[..., :, None] - a_cs[..., None, :]
    decay = jnp.exp(jnp.where(causal, seg, -jnp.inf))
    cb = jnp.einsum("bclgn,bcsgn->bgcls", cc, bc)
    y_diag = jnp.einsum("bgcls,bgecls,bcsgep->bclgep", cb, decay, xdt)
    decay_states = jnp.exp(a_cs[..., -1:] - a_cs)
    states = jnp.einsum("bclgn,bgecl,bclgep->cbgepn", bc, decay_states, xdt)
    chunk_decay = jnp.exp(a_cs[..., -1]).transpose(3, 0, 1, 2)

    def step(h, inp):
        st, dec = inp
        return h * dec[..., None, None] + st, h

    h0 = jnp.zeros(states.shape[1:], states.dtype)
    _, prev = lax.scan(step, h0, (states, chunk_decay))
    y_off = jnp.einsum("bclgn,cbgepn,bgecl->bclgep", cc, prev, jnp.exp(a_cs))
    return (y_diag + y_off).reshape(b, s, SSM_HEADS, SSM_HEAD_DIM)

def ssd_mixer(u_z, u_xbc, u_dt, conv_w, conv_b, dt_bias, a_log, d_skip, norm_w):
    b, s = u_z.shape[:2]
    xbc = jax.nn.silu(causal_dwconv(u_xbc, conv_w, conv_b)).astype(jnp.float32)
    xs, bm, cm = jnp.split(xbc, [SSM_INNER, SSM_INNER + SSM_GROUPS * SSM_STATE], axis=-1)
    dt = jax.nn.softplus(u_dt.astype(jnp.float32) + dt_bias.astype(jnp.float32))
    a = -jnp.exp(a_log.astype(jnp.float32))
    xh = xs.reshape(b, s, SSM_HEADS, SSM_HEAD_DIM)
    y = ssd_chunked(xh, dt, a,
                    bm.reshape(b, s, SSM_GROUPS, SSM_STATE),
                    cm.reshape(b, s, SSM_GROUPS, SSM_STATE))
    y = y + d_skip.astype(jnp.float32)[:, None] * xh
    yg = (y.reshape(b, s, SSM_INNER) * jax.nn.silu(u_z.astype(jnp.float32)))
    yg = yg.reshape(b, s, SSM_GROUPS, SSM_INNER // SSM_GROUPS)
    yg = yg * lax.rsqrt(jnp.mean(yg * yg, axis=-1, keepdims=True) + RMS_EPS)
    yg = yg.reshape(b, s, SSM_INNER) * norm_w.astype(jnp.float32)
    return yg.astype(u_z.dtype)

def rglru_mixer(u_y, u_x, conv_w, conv_b, wr, br, wi, bi, lam):
    b, s = u_x.shape[:2]
    gate = jax.nn.gelu(u_y, approximate=True)
    xc = causal_dwconv(u_x, conv_w, conv_b)
    xb = xc.reshape(b, s, LRU_BLOCKS, LRU_BLOCK)
    r = jax.nn.sigmoid(jnp.einsum("bshi,hij->bshj", xb, wr) + br).reshape(b, s, LRU_WIDTH)
    i = jax.nn.sigmoid(jnp.einsum("bshi,hij->bshj", xb, wi) + bi).reshape(b, s, LRU_WIDTH)
    log_a = -LRU_C * r.astype(jnp.float32) * jax.nn.softplus(-lam.astype(jnp.float32))
    a = jnp.exp(log_a)
    mult = jnp.sqrt(-jnp.expm1(2.0 * log_a))
    bx = mult * i.astype(jnp.float32) * xc.astype(jnp.float32)

    def combine(lhs, rhs):
        a1, b1 = lhs
        a2, b2 = rhs
        return a1 * a2, a2 * b1 + b2

    _, h = lax.associative_scan(combine, (a, bx), axis=1)
    return (h.astype(u_x.dtype) * gate)

def second_inputs(seed: int = 0) -> dict:
    key = jax.random.key(seed)
    ks = jax.random.split(key, 32)
    L = DEPTH
    f32 = jnp.float32

    def nrm(k, shape, scale):
        return jax.random.normal(k, shape, f32) * scale

    def gain(k, shape):
        return 1.0 + 0.05 * jax.random.normal(k, shape, f32)

    dt0 = jnp.exp(jax.random.uniform(ks[8], (L, SSM_HEADS), f32, np.log(1e-3), np.log(1e-1)))
    a_c = jax.random.uniform(ks[16], (L, LRU_WIDTH), f32, 0.9, 0.999)
    a0 = a_c ** (1.0 / LRU_C)
    return {
        "x": nrm(ks[0], (BATCH, SEQ, D_MODEL), 1.0),
        "mix_pre_norm": gain(ks[1], (L, D_MODEL)),
        "mix_post_norm": gain(ks[2], (L, D_MODEL)),
        "w_in": nrm(ks[3], (L, D_MODEL, N_IN), D_MODEL ** -0.5),
        "ssm_conv_w": nrm(ks[4], (L, SSM_CONV, SSM_CONV_DIM), SSM_CONV ** -0.5),
        "ssm_conv_b": nrm(ks[5], (L, SSM_CONV_DIM), 0.02),
        "ssm_dt_bias": dt0 + jnp.log(-jnp.expm1(-dt0)),
        "ssm_a_log": jnp.log(jax.random.uniform(ks[6], (L, SSM_HEADS), f32, 1.0, 16.0)),
        "ssm_d": 1.0 + 0.1 * jax.random.normal(ks[7], (L, SSM_HEADS), f32),
        "ssm_norm": gain(ks[9], (L, SSM_INNER)),
        "w_proj_ssm": nrm(ks[10], (L, SSM_INNER, D_MODEL), SSM_INNER ** -0.5),
        "lru_conv_w": nrm(ks[11], (L, LRU_CONV, LRU_WIDTH), LRU_CONV ** -0.5),
        "lru_conv_b": nrm(ks[12], (L, LRU_WIDTH), 0.02),
        "lru_wr": nrm(ks[13], (L, LRU_BLOCKS, LRU_BLOCK, LRU_BLOCK), LRU_BLOCK ** -0.5),
        "lru_br": nrm(ks[14], (L, LRU_BLOCKS, LRU_BLOCK), 0.02),
        "lru_wi": nrm(ks[15], (L, LRU_BLOCKS, LRU_BLOCK, LRU_BLOCK), LRU_BLOCK ** -0.5),
        "lru_bi": nrm(ks[17], (L, LRU_BLOCKS, LRU_BLOCK), 0.02),
        "lru_lambda": jnp.log(a0) - jnp.log1p(-a0),
        "w_proj_lru": nrm(ks[18], (L, LRU_WIDTH, D_MODEL), LRU_WIDTH ** -0.5),
        "gate_b": nrm(ks[19], (L, N_BRANCHES, D_MODEL), 0.02),
        "w_out": nrm(ks[20], (L, D_MODEL, D_MODEL), D_MODEL ** -0.5),
        "ffn_pre_norm": gain(ks[21], (L, D_MODEL)),
        "ffn_post_norm": gain(ks[22], (L, D_MODEL)),
        "w_ffn_up": nrm(ks[23], (L, D_MODEL, 2 * FFN_DIM), D_MODEL ** -0.5),
        "ffn_conv_w": nrm(ks[24], (L, FFN_CONV, 2 * FFN_DIM), FFN_CONV ** -0.5),
        "ffn_conv_b": nrm(ks[25], (L, 2 * FFN_DIM), 0.02),
        "w_ffn_down": nrm(ks[26], (L, FFN_DIM, D_MODEL), FFN_DIM ** -0.5),
    }

def second_block(x, mix_pre_norm, mix_post_norm, w_in, ssm_conv_w, ssm_conv_b, ssm_dt_bias,
              ssm_a_log, ssm_d, ssm_norm, w_proj_ssm, lru_conv_w, lru_conv_b, lru_wr, lru_br,
              lru_wi, lru_bi, lru_lambda, w_proj_lru, gate_b, w_out, ffn_pre_norm,
              ffn_post_norm, w_ffn_up, ffn_conv_w, ffn_conv_b, w_ffn_down):
    b, s, _ = x.shape
    for l in range(DEPTH):
        h = rmsnorm(x, mix_pre_norm[l])
        u = h @ w_in[l]
        u_z, u_xbc, u_dt, u_ly, u_lx, u_g = jnp.split(u, list(IN_SPLITS), axis=-1)
        y_a = ssd_mixer(u_z, u_xbc, u_dt, ssm_conv_w[l], ssm_conv_b[l], ssm_dt_bias[l],
                        ssm_a_log[l], ssm_d[l], ssm_norm[l])
        y_b = rglru_mixer(u_ly, u_lx, lru_conv_w[l], lru_conv_b[l], lru_wr[l], lru_br[l],
                          lru_wi[l], lru_bi[l], lru_lambda[l])
        g = jax.nn.sigmoid(u_g.reshape(b, s, N_BRANCHES, D_MODEL) + gate_b[l])
        merged = g[:, :, 0, :] * (y_a @ w_proj_ssm[l]) + g[:, :, 1, :] * (y_b @ w_proj_lru[l])
        x = x + rmsnorm(merged @ w_out[l], mix_post_norm[l])
        h = rmsnorm(x, ffn_pre_norm[l])
        up = causal_dwconv(h @ w_ffn_up[l], ffn_conv_w[l], ffn_conv_b[l])
        f_gate, f_val = jnp.split(up, 2, axis=-1)
        f = (jax.nn.gelu(f_gate, approximate=True) * f_val) @ w_ffn_down[l]
        x = x + rmsnorm(f, ffn_post_norm[l])
    return x


DEPTH_3 = 2

REL_BUCKETS = 32
REL_MAX_EXACT = 16
REL_MAX_DIST = 128
ATTN_HEADS = 8

GLA_HEADS = 4
GLA_DK = 64
GLA_DV = 128
GLA_RANK = 16
GLA_TAU = 16.0
GLA_CHUNK = 64

SWA_HEADS = ATTN_HEADS
SWA_KV_HEADS = 2
SWA_DH = 64
SWA_WINDOW = 128

MOBA_HEADS = ATTN_HEADS
MOBA_KV_HEADS = 2
MOBA_DH = 128
MOBA_BLOCK = 256
MOBA_TOPK = 3
MOBA_Q_CHUNK = 32

EPS = 1e-6

A_WIDTH = GLA_HEADS * GLA_DV
B_WIDTH = SWA_HEADS * SWA_DH
C_WIDTH = MOBA_HEADS * MOBA_DH
EVEN_WIDTH = A_WIDTH + B_WIDTH
EVEN_SPLITS = (GLA_HEADS * GLA_DK, GLA_HEADS * GLA_DK, A_WIDTH, GLA_RANK, A_WIDTH,
               B_WIDTH, SWA_KV_HEADS * SWA_DH, SWA_KV_HEADS * SWA_DH, B_WIDTH)
EVEN_COLS = 2832
ODD_SPLITS = (C_WIDTH, MOBA_KV_HEADS * MOBA_DH, MOBA_KV_HEADS * MOBA_DH, C_WIDTH)
ODD_COLS = 2560
N_EVEN = (DEPTH_3 + 1) // 2
N_ODD = DEPTH_3 // 2


def rmsnorm_3(x, g):
    xf = x.astype(jnp.float32)
    y = xf * lax.rsqrt(jnp.mean(xf * xf, axis=-1, keepdims=True) + EPS)
    return (y * g.astype(jnp.float32)).astype(x.dtype)

def split_cols(h, sizes):
    idx = np.cumsum(np.array(sizes))[:-1].tolist()
    return jnp.split(h, idx, axis=-1)

def t5_bucket(dist):
    n = jnp.maximum(dist, 0)
    nf = jnp.maximum(n, 1).astype(jnp.float32)
    large = REL_MAX_EXACT + (jnp.log(nf / REL_MAX_EXACT) / math.log(REL_MAX_DIST / REL_MAX_EXACT)
                             * (REL_BUCKETS - REL_MAX_EXACT)).astype(jnp.int32)
    large = jnp.minimum(large, REL_BUCKETS - 1)
    return jnp.where(n < REL_MAX_EXACT, n, large)

def gla_chunked(q, k, v, log_a):
    B_, S_, H_, DK = q.shape
    DV = v.shape[-1]
    N = S_ // GLA_CHUNK

    def chunks(t):
        return t.astype(jnp.float32).reshape(B_, N, GLA_CHUNK, H_, t.shape[-1]).transpose(0, 3, 1, 2, 4)

    qc, kc, vc, gc = chunks(q), chunks(k), chunks(v), chunks(log_a)
    b = jnp.cumsum(gc, axis=3)
    b_last = b[:, :, :, -1:, :]
    q_e = qc * jnp.exp(b) * (DK ** -0.5)
    k_e = kc * jnp.exp(-b)
    causal = jnp.tril(jnp.ones((GLA_CHUNK, GLA_CHUNK), dtype=bool))
    att = jnp.where(causal, jnp.einsum('bhncd,bhnsd->bhncs', q_e, k_e), 0.0)
    o_intra = jnp.einsum('bhncs,bhnse->bhnce', att, vc)
    kv_chunk = jnp.einsum('bhncd,bhnce->bhnde', kc * jnp.exp(b_last - b), vc)
    decay = jnp.exp(b_last[:, :, :, 0, :])

    def step(state, inp):
        dec, kv = inp
        return dec[..., None] * state + kv, state

    s0 = jnp.zeros((B_, H_, DK, DV), jnp.float32)
    _, s_before = lax.scan(step, s0, (jnp.moveaxis(decay, 2, 0), jnp.moveaxis(kv_chunk, 2, 0)))
    s_before = jnp.moveaxis(s_before, 0, 2)
    o = o_intra + jnp.einsum('bhncd,bhnde->bhnce', q_e, s_before)
    return o.transpose(0, 2, 3, 1, 4).reshape(B_, S_, H_, DV).astype(v.dtype)

def swa_attention(q, k, v, sinks, rel_bias):
    B_, S_, H_, DH = q.shape
    KVH = k.shape[2]
    G = H_ // KVH
    W = SWA_WINDOW
    NB = S_ // W
    qb = q.reshape(B_, NB, W, KVH, G, DH).transpose(0, 3, 4, 1, 2, 5)

    def band(t):
        tb = t.reshape(B_, NB, W, KVH, DH).transpose(0, 3, 1, 2, 4)
        prev = jnp.pad(tb[:, :, :-1], ((0, 0), (0, 0), (1, 0), (0, 0), (0, 0)))
        return jnp.concatenate([prev, tb], axis=3)

    kb, vb = band(k), band(v)
    qi = jnp.arange(W)[:, None]
    kj = jnp.arange(2 * W)[None, :]
    dist = qi + W - kj
    in_win = (dist >= 0) & (dist < W)
    blk = jnp.arange(NB)[:, None, None]
    mask = in_win[None] & ((blk > 0) | (kj[None] >= W))
    bias = rel_bias[t5_bucket(dist)].astype(jnp.float32)
    bias = bias.transpose(2, 0, 1).reshape(KVH, G, 1, W, 2 * W)
    logits = jnp.einsum('bkgnqd,bknsd->bkgnqs', qb, kb).astype(jnp.float32) * (DH ** -0.5) + bias
    logits = jnp.where(mask, logits, -jnp.inf)
    sink = jnp.broadcast_to(sinks.astype(jnp.float32).reshape(KVH, G, 1, 1, 1), logits.shape[:-1] + (1,))
    probs = jax.nn.softmax(jnp.concatenate([logits, sink], axis=-1), axis=-1)[..., :-1]
    o = jnp.einsum('bkgnqs,bknsd->bkgnqd', probs.astype(v.dtype), vb)
    return o.transpose(0, 3, 4, 1, 2, 5).reshape(B_, S_, H_ * DH)

def moba_attention(q, k, v, rel_bias):
    B_, S_, H_, DH = q.shape
    G = H_ // k.shape[2]
    S_pad = -(-S_ // MOBA_BLOCK) * MOBA_BLOCK
    pad = ((0, 0), (0, S_pad - S_), (0, 0), (0, 0))
    qh = jnp.pad(q, pad).transpose(0, 2, 1, 3)
    kh = jnp.repeat(jnp.pad(k, pad), G, axis=2).transpose(0, 2, 1, 3)
    vh = jnp.repeat(jnp.pad(v, pad), G, axis=2).transpose(0, 2, 1, 3)
    NBLK = S_pad // MOBA_BLOCK
    kblk = kh.reshape(B_, H_, NBLK, MOBA_BLOCK, DH)
    vblk = vh.reshape(B_, H_, NBLK, MOBA_BLOCK, DH)
    kmean = kblk.mean(axis=3)
    k_sel = min(MOBA_TOPK, NBLK)
    bi = jnp.arange(B_)[:, None, None, None]
    hi = jnp.arange(H_)[None, :, None, None]
    offs = jnp.arange(MOBA_BLOCK)
    blk_ids = jnp.arange(NBLK)
    scale = DH ** -0.5

    def one_chunk(c):
        start = c * MOBA_Q_CHUNK
        qc = lax.dynamic_slice_in_dim(qh, start, MOBA_Q_CHUNK, axis=2)
        tpos = start + jnp.arange(MOBA_Q_CHUNK)
        own = start // MOBA_BLOCK
        gate = jnp.einsum('bhqd,bhnd->bhqn', qc, kmean).astype(jnp.float32)
        gate = jnp.where(blk_ids < own, gate, -jnp.inf)
        _, idx = lax.top_k(gate, k_sel)
        kg = kblk[bi, hi, idx].reshape(B_, H_, MOBA_Q_CHUNK, k_sel * MOBA_BLOCK, DH)
        vg = vblk[bi, hi, idx].reshape(B_, H_, MOBA_Q_CHUNK, k_sel * MOBA_BLOCK, DH)
        kpos = (idx[..., None] * MOBA_BLOCK + offs).reshape(B_, H_, MOBA_Q_CHUNK, k_sel * MOBA_BLOCK)
        valid = jnp.broadcast_to((idx < own)[..., None], idx.shape + (MOBA_BLOCK,)).reshape(kpos.shape)
        bias_sel = rel_bias[t5_bucket(tpos[None, None, :, None] - kpos), hi].astype(jnp.float32)
        logit_sel = jnp.einsum('bhqd,bhqsd->bhqs', qc, kg).astype(jnp.float32) * scale + bias_sel
        logit_sel = jnp.where(valid, logit_sel, -jnp.inf)
        ko = lax.dynamic_slice_in_dim(kh, own * MOBA_BLOCK, MOBA_BLOCK, axis=2)
        vo = lax.dynamic_slice_in_dim(vh, own * MOBA_BLOCK, MOBA_BLOCK, axis=2)
        dist_own = tpos[:, None] - (own * MOBA_BLOCK + offs)[None, :]
        bias_own = rel_bias[t5_bucket(dist_own)].astype(jnp.float32).transpose(2, 0, 1)
        logit_own = jnp.einsum('bhqd,bhsd->bhqs', qc, ko).astype(jnp.float32) * scale + bias_own
        logit_own = jnp.where(dist_own >= 0, logit_own, -jnp.inf)
        probs = jax.nn.softmax(jnp.concatenate([logit_sel, logit_own], axis=-1), axis=-1)
        p_sel = probs[..., :k_sel * MOBA_BLOCK]
        p_own = probs[..., k_sel * MOBA_BLOCK:]
        o = jnp.einsum('bhqs,bhqsd->bhqd', p_sel, vg) + jnp.einsum('bhqs,bhsd->bhqd', p_own, vo)
        return o.astype(v.dtype)

    out = lax.map(one_chunk, jnp.arange(S_pad // MOBA_Q_CHUNK))
    out = out.transpose(1, 0, 3, 2, 4).reshape(B_, S_pad, H_ * DH)
    return out[:, :S_]

def even_layer(hn, w_in, gla_w_up, gla_b_up, gla_gain, sinks, w_out, rel_bias):
    B_, S_, _ = hn.shape
    proj = hn @ w_in
    aq, ak, av, a_down, a_gate, bq, bk, bv, b_gate = split_cols(proj, EVEN_SPLITS)
    log_a = jax.nn.log_sigmoid((a_down @ gla_w_up + gla_b_up).astype(jnp.float32)) / GLA_TAU
    oa = gla_chunked(aq.reshape(B_, S_, GLA_HEADS, GLA_DK), ak.reshape(B_, S_, GLA_HEADS, GLA_DK),
                     av.reshape(B_, S_, GLA_HEADS, GLA_DV), log_a.reshape(B_, S_, GLA_HEADS, GLA_DK))
    oa = rmsnorm_3(oa, gla_gain).reshape(B_, S_, A_WIDTH) * jax.nn.silu(a_gate)
    ob = swa_attention(bq.reshape(B_, S_, SWA_HEADS, SWA_DH), bk.reshape(B_, S_, SWA_KV_HEADS, SWA_DH),
                       bv.reshape(B_, S_, SWA_KV_HEADS, SWA_DH), sinks, rel_bias) * jax.nn.silu(b_gate)
    return jnp.concatenate([oa, ob], axis=-1) @ w_out

def odd_layer(hn, w_in, w_out, rel_bias):
    B_, S_, _ = hn.shape
    cq, ck, cv, c_gate = split_cols(hn @ w_in, ODD_SPLITS)
    oc = moba_attention(cq.reshape(B_, S_, MOBA_HEADS, MOBA_DH), ck.reshape(B_, S_, MOBA_KV_HEADS, MOBA_DH),
                        cv.reshape(B_, S_, MOBA_KV_HEADS, MOBA_DH), rel_bias)
    return (oc * jax.nn.silu(c_gate)) @ w_out

def third_inputs(seed: int = 0) -> dict:
    key = jax.random.key(seed)
    ks = jax.random.split(key, 12)
    f32 = jnp.float32
    x = jax.random.normal(ks[0], (BATCH, SEQ, D_MODEL), f32)
    norm_gain = 1.0 + 0.02 * jax.random.normal(ks[1], (DEPTH_3, D_MODEL), f32)
    final_gain = 1.0 + 0.02 * jax.random.normal(ks[2], (D_MODEL,), f32)
    rel_bias = 0.2 * jax.random.normal(ks[3], (REL_BUCKETS, ATTN_HEADS), f32)
    w_in_even = jax.random.normal(ks[4], (N_EVEN, D_MODEL, EVEN_COLS), f32) * D_MODEL ** -0.5
    gla_w_up = jax.random.normal(ks[5], (N_EVEN, GLA_RANK, GLA_HEADS * GLA_DK), f32) * GLA_RANK ** -0.5
    gla_b_up = 0.1 * jax.random.normal(ks[6], (N_EVEN, GLA_HEADS * GLA_DK), f32)
    gla_norm_gain = 1.0 + 0.02 * jax.random.normal(ks[7], (N_EVEN, GLA_DV), f32)
    swa_sinks = 0.5 * jax.random.normal(ks[8], (N_EVEN, SWA_HEADS), f32)
    w_out_even = jax.random.normal(ks[9], (N_EVEN, EVEN_WIDTH, D_MODEL), f32) * EVEN_WIDTH ** -0.5
    w_in_odd = jax.random.normal(ks[10], (N_ODD, D_MODEL, ODD_COLS), f32) * D_MODEL ** -0.5
    w_out_odd = jax.random.normal(ks[11], (N_ODD, C_WIDTH, D_MODEL), f32) * C_WIDTH ** -0.5
    return {"x": x, "norm_gain": norm_gain, "final_gain": final_gain, "rel_bias": rel_bias,
            "w_in_even": w_in_even, "gla_w_up": gla_w_up, "gla_b_up": gla_b_up,
            "gla_norm_gain": gla_norm_gain, "swa_sinks": swa_sinks, "w_out_even": w_out_even,
            "w_in_odd": w_in_odd, "w_out_odd": w_out_odd}

def third_block(x, norm_gain, final_gain, rel_bias, w_in_even, gla_w_up, gla_b_up, gla_norm_gain,
              swa_sinks, w_out_even, w_in_odd, w_out_odd):
    h = x
    for layer in range(DEPTH_3):
        hn = rmsnorm_3(h, norm_gain[layer])
        if layer % 2 == 0:
            i = layer // 2
            h = h + even_layer(hn, w_in_even[i], gla_w_up[i], gla_b_up[i], gla_norm_gain[i],
                               swa_sinks[i], w_out_even[i], rel_bias)
        else:
            i = layer // 2
            h = h + odd_layer(hn, w_in_odd[i], w_out_odd[i], rel_bias)
    return rmsnorm_3(h, final_gain)


def setup_inputs(seed=0):
    out = dict(first_inputs(seed))
    for name, value in second_inputs(seed + 1).items():
        if name != "x":
            out[name + "_2"] = value
    for name, value in third_inputs(seed + 2).items():
        if name != "x":
            out[name + "_3"] = value
    return out


def reference(
    x, c, ctx, c_ctx, w_ada, b_ada, pre_mix_g, post_mix_g, pre_ffn_g, post_ffn_g, w_in, conv_w,
    conv_b, ret_decay_logit, ret_norm_g, w_out, w_router, b_router, w_gate, w_up, w_down,
    mix_pre_norm_2, mix_post_norm_2, w_in_2, ssm_conv_w_2, ssm_conv_b_2, ssm_dt_bias_2,
    ssm_a_log_2, ssm_d_2, ssm_norm_2, w_proj_ssm_2, lru_conv_w_2, lru_conv_b_2, lru_wr_2,
    lru_br_2, lru_wi_2, lru_bi_2, lru_lambda_2, w_proj_lru_2, gate_b_2, w_out_2, ffn_pre_norm_2,
    ffn_post_norm_2, w_ffn_up_2, ffn_conv_w_2, ffn_conv_b_2, w_ffn_down_2, norm_gain_3,
    final_gain_3, rel_bias_3, w_in_even_3, gla_w_up_3, gla_b_up_3, gla_norm_gain_3, swa_sinks_3,
    w_out_even_3, w_in_odd_3, w_out_odd_3,
):
    x = first_block(
        x, c, ctx, c_ctx, w_ada, b_ada, pre_mix_g, post_mix_g, pre_ffn_g, post_ffn_g, w_in,
        conv_w, conv_b, ret_decay_logit, ret_norm_g, w_out, w_router, b_router, w_gate, w_up,
        w_down,
    )
    x = second_block(
        x, mix_pre_norm_2, mix_post_norm_2, w_in_2, ssm_conv_w_2, ssm_conv_b_2, ssm_dt_bias_2,
        ssm_a_log_2, ssm_d_2, ssm_norm_2, w_proj_ssm_2, lru_conv_w_2, lru_conv_b_2, lru_wr_2,
        lru_br_2, lru_wi_2, lru_bi_2, lru_lambda_2, w_proj_lru_2, gate_b_2, w_out_2,
        ffn_pre_norm_2, ffn_post_norm_2, w_ffn_up_2, ffn_conv_w_2, ffn_conv_b_2, w_ffn_down_2,
    )
    return third_block(
        x, norm_gain_3, final_gain_3, rel_bias_3, w_in_even_3, gla_w_up_3, gla_b_up_3,
        gla_norm_gain_3, swa_sinks_3, w_out_even_3, w_in_odd_3, w_out_odd_3,
    )


_drawn_inputs = setup_inputs


def setup_inputs(seed=0):
    import zlib

    import numpy as np

    out = dict(_drawn_inputs(seed))
    spreads = {}
    factors = {'ssm_conv_b_2': 2.713,
     'lru_br_2': 8.0,
     'lru_bi_2': 8.0,
     'gate_b_2': 8.0,
     'ffn_conv_b_2': 3.191,
     'norm_gain_3': 5.452,
     'final_gain_3': 2.838,
     'rel_bias_3': 4.76,
     'gla_b_up_3': 5.438,
     'gla_norm_gain_3': 8.0,
     'swa_sinks_3': 8.0}
    for name, (base, spread) in spreads.items():
        noise = np.random.default_rng([zlib.crc32(name.encode()), seed]).standard_normal(out[name].shape)
        drawn = base * np.exp(spread * noise) if base else spread * noise
        out[name] = __import__('jax').numpy.asarray(drawn.astype(out[name].dtype))
    for name, factor in factors.items():
        out[name] = (out[name] * factor).astype(out[name].dtype)
    return out
```

```python
import math
from contextlib import ExitStack
from collections import namedtuple

import numpy as np

import concourse.bass as bass
from concourse import mybir
from concourse.alu_op_type import AluOpType as ALU

F32 = mybir.dt.float32
U32 = mybir.dt.uint32
ACT = mybir.ActivationFunctionType
AXX = mybir.AxisListType.X

P = 128
SEQ = 256
DM = 1024
KT = DM // P
TT = SEQ // P
EPS = 1e-6
HEADS1 = 4
EXPERTS = 16
CAP = 2 * SEQ // EXPERTS
DEXP = 2 * DM
SSM_H, SSM_P, CHUNK = 16, 64, 64
FFN = 3072
FT = FFN // P
REL_BUCKETS, REL_EXACT, REL_DIST = 32, 16, 128
AH = 8
TOEP = 383
TPITCH = 384

RING = 4
BLK = 4096
UNITS = 4
ADA_BLOCKS = 12
D1_UNITS = 28 + 8
D1_BLOCKS = D1_UNITS // UNITS
EXP_BLOCKS = 12
IN2, OUT2 = 53, 8
EVEN3, ODD3 = 23, 20
D2_LAYERS = (IN2, 8, 8, 8, 2 * FT, 8 * 3, EVEN3, 8, ODD3, 8)
D2_UNITS = sum(D2_LAYERS)
D2_BLOCKS = D2_UNITS // UNITS
D1_BLOCK0 = ADA_BLOCKS
EXP_BLOCK0 = D1_BLOCK0 + D1_BLOCKS
D2_BLOCK0 = EXP_BLOCK0 + EXPERTS * EXP_BLOCKS

PARAMS = [("cc", 16), ("b_ada", 48), ("pre_mix_g", 8), ("post_mix_g", 8), ("pre_ffn_g", 8), ("post_ffn_g", 8),
          ("conv_w", 12), ("conv_b", 4), ("decay", 8), ("ret_norm_g", 4), ("b_router", 16), ("w_router", 128),
          ("mix_pre", 8), ("mix_post", 8), ("ssm_conv_w", 48), ("ssm_conv_b", 12), ("dt_bias", 1), ("a_log", 1),
          ("ssm_d", 8), ("ssm_norm", 8), ("lru_conv_w", 32), ("lru_conv_b", 8), ("lru_br", 8), ("lru_bi", 8),
          ("lru_lam", 8), ("gate_b", 16), ("ffn_pre", 8), ("ffn_post", 8), ("ffn_conv_w", 144), ("ffn_conv_b", 48),
          ("norm_gain", 16), ("final_gain", 8), ("gla_b_up", 2), ("gla_gain", 1), ("sinks", 8), ("rel", 8),
          ("gla_w_up", 256)]
CONSTS = [("ident", 128), ("swap", 128), ("cos_c", 256), ("sin_c", 256), ("cos_t", 128), ("sin_t", 128),
          ("ahead", 512), ("behind", 512), ("row1", 256), ("row_rev", 256), ("row", 256), ("tok", 2), ("tok_rev", 2),
          ("own_expert", 512), ("ssd_reset", 256), ("chunk_rows", 256), ("head_rows", 16), ("causal", 384),
          ("gla_reset", 256), ("gla_mask", 128), ("half", 2), ("buckets", 2 * TOEP)]


def offsets(entries):
    at, out = 0, {}
    for name, n in entries:
        out[name] = (at, n)
        at += n
    return out, at


P_AT, P_COLS = offsets(PARAMS)
C_AT, C_COLS = offsets(CONSTS)

SEMS = """dense_sb ring_used dense_mm h_ready xc_ready lru_in ri_sig ri_mm cs_ready ssd_tr xbc_silu cb_mm ssd_sb cb_ready
xs_tr lmask_ready seg_ready bc_mm xdt_ready m_ready ya_pair ssd_y yb_ready ya_sq ya_sum ya_ready mg_ready f_ready
x2_ready dt_in dt_soft a_exp lam_soft xbc_conv lam_ready th_ready ly_gelu z_silu seg_exp lru_neg lru_root g_sig
ya_gated ya_inv ya_rstd conv_step ffn_gelu toep_stored lg_sb bias_in gl_mm kp_ready kp_tr att_mm kpt_ready kv_mm
att_ready st_ready o_mm o_sq o_sb o_sum lg_mm lg_ready pt_sb pt_tr ao_ready ao_mm oa_var bqh_ready gl_in gl_soft
gl_b gl_exp gl_left eg_silu o_rstd lg_shift lg_exp out_ready toep_sb out_stored norm_squared norm_inverted
norm_summed consts_in ones_ready rel_ready toep_mm c_ready ada_sb mod_ready ada_tr hc_ready hx_ready rot_mm
kw_ready qk_rot state_mm state_sb score_mm qfb_ready sd_ready y_mm y_sb mean_mm ysq_ready var_mm mix_ready
h2_ready router_mm ht_tr aff_ready aff_tr topk_ready slot_mm sel_ready ht_sb xs_sb xs_mm slots_ready xse_ready
hid_ready hid_tr hidt_sb selt_ready y_low y_high acc_done act_step norm_scale params_in ctx_in x_in zeros_ready
decay_soft ramp_ready dmat_ready xi_ready g_silu yc_ready yvar_ready yrstd_ready x1_ready logit_shift aff_exp
silu_sb ffn_sb dve_step decay_ready""".split()


DENSE1 = ([(u, a, a == "ctx" or u >= 4) for u in range(8) for a in ("x", "ctx")]
          + [(u, "x", False) for u in range(8, 28)])
SCORE_BANK = (6, 7, 4, 5)


def block_ends(unit, act="ctx"):
    return unit % UNITS == UNITS - 1 and (unit >= 8 or act == "ctx")


def conv_taps(dve, nc, link, out, src, w, bias, taps):
    link(nc.vector.tensor_scalar(out, src, w[:, taps - 1:taps], bias, ALU.mult, ALU.add))
    for s in range(1, taps):
        last = nc.vector.scalar_tensor_tensor(out=out[:, s:SEQ], in0=src[:, 0:SEQ - s], scalar=w[:, taps - 1 - s:taps - s],
                                              in1=out[:, s:SEQ], op0=ALU.mult, op1=ALU.add)
        if s < taps - 1:
            link(last)
    return last


def spread(ap, axis, n):
    a = ap.unsqueeze(axis)
    shape = list(a.shape)
    shape[axis] = n
    return a.broadcast_to(shape)


def program(nc, d, out):
    ctx = ExitStack()
    with ctx:
        def sb(name, shape, dt=F32):
            return ctx.enter_context(nc.sbuf_tensor(name, shape, dt))

        s = namedtuple("Semaphores", SEMS)(*[ctx.enter_context(nc.semaphore(n)) for n in SEMS])
        ring_loaded = [ctx.enter_context(nc.semaphore(f"ring_loaded{i}")) for i in range(RING)]
        B = [ctx.enter_context(nc.psum_tensor(f"bank{i}", [P, 512], F32)) for i in range(8)]

        ring = sb("ring", [P, RING, BLK])
        params = sb("params", [P, P_COLS])
        consts = sb("consts", [P, C_COLS])
        lru_w = sb("lru_w", [P, 2, KT, P])
        X = sb("x_resid", [P, KT, SEQ])
        H = sb("h_normed", [P, KT, SEQ])
        SQ = sb("squares", [P, KT, SEQ])
        RS = sb("rstd", [P, 2, SEQ])
        U = sb("work", [P, 80 * SEQ])
        ones = sb("ones", [P, P])
        sm = sb("small", [P, 1024])
        idx_u = sb("topk_index", [EXPERTS, CAP], U32)

        def par(name, a=None, b=None):
            at, n = P_AT[name]
            return params[:, at + (0 if a is None else a):at + (n if b is None else b)]

        def con(name):
            at, n = C_AT[name]
            return consts[:, at:at + n]

        def tiles(a, n):
            return U[:, a * SEQ:(a + n) * SEQ]

        def tiles3(a, n):
            return tiles(a, n).rearrange("p (n t) -> p n t", t=SEQ)

        def small(at, n):
            return sm[:, at:at + n]

        ident = con("ident")
        flat = lambda ap: ap[:, :, :].rearrange("p k t -> p (k t)")

        def weights(block, sub, k):
            at = (sub * KT + k) * P
            return ring[:, block % RING, at:at + P]

        def uses(block):
            return 16 * (block // RING + 1)

        C2 = small(0, KT * 32).rearrange("p (k m) -> p k m", m=32)
        MOD = small(256, 96).rearrange("p (n s) -> p n s", s=2)
        A1 = small(352, 16).rearrange("p (s k) -> p s k", s=2)
        A2 = small(368, 8)
        G1P = small(376, 8)
        G2P = small(384, 8)
        LG = small(392, 8)
        LT = small(400, 8)
        WFB = small(408, 16).rearrange("p (t h) -> p t h", t=TT)
        LOGIT = small(424, 32).rearrange("p (t e) -> p t e", t=TT)
        RMAX = small(456, 2)
        RSUM = small(458, 2)
        SLOT_TOK = small(460, 16)
        SLOT_GATE = small(476, 16)
        VAL = small(492, 32)
        IDXF = small(524, 32)
        IDX4 = small(556, 128)
        VAL4 = small(684, 128)
        NEGA = small(812, 1)
        TOT = small(813, 1)
        LSH = small(814, 32).rearrange("p (t h) -> p t h", t=TT)
        LAMC = small(846, 8)
        LAMT = small(854, 8)
        DEC = small(862, 8).rearrange("p (t c) -> p t c", t=2)
        AMAX = small(870, 16).rearrange("p (h b) -> p h b", b=2)
        ASUM = small(886, 16).rearrange("p (h b) -> p h b", b=2)
        ASNK = small(902, 16).rearrange("p (h b) -> p h b", b=2)

        CTXR, HC = tiles3(0, 8), tiles3(8, 8)
        KQ = tiles3(16, 8)
        VX = tiles(24, 4).rearrange("p (t c) -> p t c", t=TT)
        KC = tiles(28, 4).rearrange("p (t h c) -> p t h c", t=TT, h=HEADS1)
        VC = tiles(32, 4).rearrange("p (t c) -> p t c", t=TT)
        G_, B_, C_, XI_ = tiles3(36, 4), tiles3(40, 4), tiles3(44, 4), tiles3(48, 4)
        KQR = tiles3(52, 8)
        DM_ = tiles(60, 8).rearrange("p (h m n) -> p h m n", h=HEADS1, m=TT)
        QFB = tiles3(68, 8)
        ROT = tiles(76, 4)
        KW = SQ[:, :, :].rearrange("p (s t x) n -> p s t (x n)", s=2, t=TT)
        SFB = tiles(76, 4).rearrange("p (s h c) -> p s h c", s=2, h=HEADS1)
        TW = tiles(28, 24).rearrange("p (h j) -> p h j", j=TPITCH)
        RELB = tiles(76, 4).rearrange("p (h j) -> p h j", h=AH)
        ADA = tiles(52, 2)
        Y, YC = tiles3(16, 4), tiles3(20, 4)
        MIX, MO = tiles3(8, 8), tiles3(28, 8)
        R4 = tiles3(52, 4)
        HT = tiles(0, 8).rearrange("p (t c) -> p t c", t=TT)
        XS = tiles(8, 17).rearrange("p (k j) -> p k j", k=KT)
        SEL = tiles(25, 4).rearrange("p (t j) -> p t j", t=TT)
        R16 = tiles(36, 2)
        AT = tiles(38, 1)
        XSE = tiles(39, 1).rearrange("p (k m) -> p k m", k=KT)
        SG, HID, HIDT = tiles(40, 2), tiles(42, 2), tiles(44, 2)
        YE = tiles(46, 4)
        SELT = tiles(50, 1)
        ZERO = tiles(51, 2)
        FO = tiles3(60, 8)

        RAW = tiles3(0, IN2)
        XC = tiles3(0, 8)
        TH, LY, Z, GATE = tiles3(13, 8), tiles3(21, 8), tiles3(29, 8), tiles3(37, 16)
        XBC = tiles3(53, 12)
        YA = tiles3(53, 8)
        DT, ADT, LCUM = tiles(65, 1), tiles(66, 1), tiles(67, 1)
        CBM = tiles(68, 3).rearrange("p (g l) -> p g l", g=2)
        SEG = tiles(71, 3).rearrange("p (b l) -> p b l", b=2)
        LMASK = tiles3(74, 2)
        I_OF = (8, 9, 10, 11, 76, 77, 78, 79)
        XDT = SQ[:, :, :].rearrange("p (t x) n -> p t (x n)", t=TT)
        DTT = small(924, 32).rearrange("p (t h) -> p t h", t=TT)
        LRU_T = tiles(12, 1)
        PA, PB, MO2 = tiles3(29, 8), tiles3(21, 8), tiles3(13, 8)
        UP, FV = tiles3(0, 48), tiles3(48, FT)
        DO = tiles3(0, 8)
        PU2 = 44
        MID2 = 35
        L_LRU, L_SSM, L_OUT2, L_UP, L_DOWN, L_EVEN, L_OE, L_ODD, L_OO = (
            sum(D2_LAYERS[:n]) for n in range(1, len(D2_LAYERS)))
        PU3 = PU2 + L_DOWN + 8 - L_EVEN
        ROUND = RING * UNITS
        SSD_LEN = 3 * P

        def d2_block(unit):
            return D2_BLOCK0 + unit // UNITS

        def tensor_dense2(pe, arrived, dense_unit, unit, act, pu, tokens_out=False):
            pe.wait_ge(s.dense_sb, pu - 3)
            arrived(d2_block(unit))
            dense_unit(d2_block(unit), unit % UNITS, B[pu % 4], act, tokens_out).then_inc(
                s.ring_used if block_ends(unit) else s.dense_mm, 1)

        def tensor_loop2(pe, dense_unit, first, rounds, act):
            with pe.Fori(0, rounds) as r:
                for j in range(ROUND):
                    unit = first + j
                    pe.wait_ge(s.dense_sb, r * ROUND + (PU2 + unit - 3))
                    blk = d2_block(unit)
                    pe.wait_ge(ring_loaded[blk % RING], r * 16 + uses(blk))
                    dense_unit(blk, unit % UNITS, B[(PU2 + unit) % 4], act).then_inc(
                        s.ring_used if block_ends(unit) else s.dense_mm, 1)

        def tensor_block2(pe, mm, arrived, dense_unit, column_sums):
            def unit2(unit, act):
                tensor_dense2(pe, arrived, dense_unit, unit, act, PU2 + unit)

            column_sums(5)
            pe.wait_ge(s.h_ready, 1)
            tensor_loop2(pe, dense_unit, 0, 2, H)
            unit2(32, H), unit2(33, H)
            pe.wait_ge(s.xc_ready, 1)
            pe.wait_ge(s.lru_in, 16)
            for k in range(KT):
                if k >= 4:
                    pe.wait_ge(s.ri_sig, k - 3)
                for n in range(2):
                    last = mm(B[4 + k % 4][:, n * SEQ:(n + 1) * SEQ], lru_w[:, n, k, :], XC[:, k, :])
                last.then_inc(s.ri_mm, 1)
            unit2(34, H), unit2(35, H)
            pe.wait_ge(s.ri_sig, KT)
            pe.wait_ge(s.cs_ready, 1)
            for t in range(TT):
                nc.tensor.transpose(B[4][:, t * P:(t + 1) * P], LCUM[:, t * P:(t + 1) * P], ident)
                last = nc.tensor.transpose(B[5][:, t * P:(t + 1) * P], DT[:, t * P:(t + 1) * P], ident)
            last.then_inc(s.ssd_tr, 1)
            pe.wait_ge(s.xbc_silu, 1)
            for g in range(2):
                mm(B[6 + g][:, 0:SEQ], XBC[:, 8 + g, 0:P], XBC[:, 10 + g, :])
                mm(B[6 + g][:, SEQ:SSD_LEN], XBC[:, 8 + g, P:SEQ], XBC[:, 10 + g, P:SEQ]).then_inc(s.cb_mm, 1)
            unit2(36, H)
            pe.wait_ge(s.ssd_sb, 1)
            pe.wait_ge(s.cb_ready, 2)
            for n in range(4):
                for q in range(4):
                    t, k = n // 2, 4 * (n % 2) + q
                    last = nc.tensor.transpose(B[4 + n][:, q * P:(q + 1) * P], XBC[:, k, t * P:(t + 1) * P], ident)
                last.then_inc(s.xs_tr, 1)
            unit2(37, H)

            def spread_decay(h):
                pe.wait_ge(s.lmask_ready, h + 1)
                if h >= 2:
                    pe.wait_ge(s.seg_ready, h - 1)
                bank, lm = B[4 + h % 2], LMASK[:, h % 2, :]
                mm(bank[:, 0:SEQ], con("chunk_rows")[:, 0:P], lm)
                mm(bank[:, SEQ:SSD_LEN], con("chunk_rows")[:, P:2 * P], lm[:, P:SEQ]).then_inc(s.bc_mm, 1)

            pe.wait_ge(s.xdt_ready, 4)
            spread_decay(0)
            for h in range(SSM_H):
                if 38 + h < IN2:
                    unit2(38 + h, H)
                if h + 1 < SSM_H:
                    spread_decay(h + 1)
                pe.wait_ge(s.m_ready, h + 1)
                if h >= 4:
                    pe.wait_ge(s.ya_pair, h // 2 - 1)
                o = B[6 + h // 2 % 2][64 * (h % 2):64 * (h % 2) + 64, 0:SEQ]
                mm(o, XDT[:, 0, h * SSM_P:(h + 1) * SSM_P], SEG[:, h % 2, 0:SEQ], True, False)
                mm(o[:, P:SEQ], XDT[:, 1, h * SSM_P:(h + 1) * SSM_P], SEG[:, h % 2, SEQ:SSD_LEN],
                   False, True).then_inc(s.ssd_y, 1)
            pe.wait_ge(s.yb_ready, 1)
            for n in range(4):
                unit2(L_LRU + n, XC)
            pe.wait_ge(s.ya_sq, 1)
            for g in range(2):
                for k in range(4):
                    last = mm(B[4 + g][:, 0:SEQ], ones[:], SQ[:, 4 * g + k, :], k == 0, k == 3)
            last.then_inc(s.ya_sum, 1)
            for n in range(4, 8):
                unit2(L_LRU + n, XC)
            pe.wait_ge(s.ya_ready, 1)
            for n in range(8):
                unit2(L_SSM + n, YA)
            pe.wait_ge(s.mg_ready, 1)
            for n in range(8):
                unit2(L_OUT2 + n, PA)
            column_sums(6)
            column_sums(7)
            pe.wait_ge(s.h_ready, 2)
            tensor_loop2(pe, dense_unit, L_UP, 3, H)
            for n in range(KT):
                pu = PU2 + L_DOWN + n
                pe.wait_ge(s.dense_sb, pu - 3)
                for kg in range(3):
                    unit = L_DOWN + 3 * n + kg
                    arrived(d2_block(unit))
                    if n == 0:
                        pe.wait_ge(s.f_ready, kg + 1)
                    last = dense_unit(d2_block(unit), unit % UNITS, B[pu % 4], FV[:, KT * kg:KT * kg + KT, :],
                                      start=kg == 0, stop=kg == 2)
                    if block_ends(unit):
                        last.then_inc(s.ring_used, 1)
                    elif kg == 2:
                        last.then_inc(s.dense_mm, 1)
            column_sums(8)

        def scalar_loop2(act, fn, units_done, first, rounds):
            mids = units_done[0]
            with act.Fori(0, rounds) as r:
                n = 0
                for j in range(ROUND):
                    unit = first + j
                    if block_ends(unit):
                        act.wait_ge(s.ring_used, r * RING + (d2_block(unit) + 1))
                    else:
                        n += 1
                        act.wait_ge(s.dense_mm, r * (ROUND - RING) + (mids + n))
                    at = r * (ROUND * SEQ) + (unit - (0 if first == 0 else L_UP)) * SEQ
                    fn(U[:, bass.ds(at, SEQ)], B[(PU2 + unit) % 4][:, 0:SEQ], ACT.Copy).then_inc(s.dense_sb, 1)
            units_done[0] += rounds * (ROUND - RING)

        def scalar_block2(act, fn, link, squares, norm_scale, unit_done, units_done):
            def copy2(unit, dst):
                unit_done(d2_block(unit), block_ends(unit))
                fn(dst, B[(PU2 + unit) % 4][:, 0:SEQ], ACT.Copy).then_inc(s.dense_sb, 1)

            def soft(x, t):
                link(fn(t, x, ACT.Abs))
                link(fn(t, t, ACT.Exp, scale=-1.0))
                return fn(t, t, ACT.Ln, bias=1.0)

            act.wait_ge(s.x2_ready, 1)
            squares(flat(X))
            norm_scale(5)
            scalar_loop2(act, fn, units_done, 0, 2)
            act.wait_ge(s.dt_in, 1)
            soft(DT, ADT).then_inc(s.dt_soft, 1)
            fn(NEGA, par("a_log"), ACT.Exp).then_inc(s.a_exp, 1)
            soft(par("lru_lam"), LAMT).then_inc(s.lam_soft, 1)
            act.wait_ge(s.xbc_conv, 1)
            fn(tiles(53, 12), tiles(53, 12), ACT.Silu).then_inc(s.xbc_silu, 1)
            for unit in (32, 33):
                copy2(unit, RAW[:, unit, :])
            for k in range(KT):
                act.wait_ge(s.ri_mm, k + 1)
                bank = B[4 + k % 4]
                fn(TH[:, k, :], bank[:, 0:SEQ], ACT.Sigmoid, bias=par("lru_br", k, k + 1))
                fn(tiles(I_OF[k], 1), bank[:, SEQ:2 * SEQ], ACT.Sigmoid, bias=par("lru_bi", k, k + 1)).then_inc(s.ri_sig, 1)
            act.wait_ge(s.lam_ready, 1)
            act.wait_ge(s.ri_sig, KT)
            for k in range(KT):
                last = fn(TH[:, k, :], TH[:, k, :], ACT.Tanh, scale=LAMC[:, k:k + 1])
            last.then_inc(s.th_ready, 1)
            for unit in (34, 35, 36):
                copy2(unit, RAW[:, unit, :])
            fn(tiles(21, 8), tiles(21, 8), ACT.Gelu_apprx_tanh).then_inc(s.ly_gelu, 1)
            act.wait_ge(s.dense_sb, PU2 + 37)
            fn(tiles(29, 8), tiles(29, 8), ACT.Silu).then_inc(s.z_silu, 1)
            copy2(37, RAW[:, 37, :])
            for h in range(SSM_H):
                act.wait_ge(s.seg_ready, h + 1)
                fn(SEG[:, h % 2, :], SEG[:, h % 2, :], ACT.Exp).then_inc(s.seg_exp, 1)
                if 38 + h < IN2:
                    copy2(38 + h, RAW[:, 38 + h, :])
                if h % 2:
                    act.wait_ge(s.lru_neg, h // 2 + 1)
                    fn(XC[:, h // 2, :], XC[:, h // 2, :], ACT.Sqrt).then_inc(s.lru_root, 1)
            act.wait_ge(s.dense_sb, PU2 + IN2)
            for k in range(16):
                last = fn(GATE[:, k, :], GATE[:, k, :], ACT.Sigmoid, bias=par("gate_b", k, k + 1))
            last.then_inc(s.g_sig, 1)
            for n in range(4):
                copy2(L_LRU + n, PB[:, n, :])
            act.wait_ge(s.ya_gated, 1)
            fn(flat(SQ), tiles(53, 8), ACT.Square).then_inc(s.ya_sq, 1)
            act.wait_ge(s.ya_inv, 1)
            fn(flat(RS), flat(RS), ACT.Sqrt).then_inc(s.ya_rstd, 1)
            for n in range(4, 8):
                copy2(L_LRU + n, PB[:, n, :])
            for n in range(8):
                copy2(L_SSM + n, PA[:, n, :])
            for n in range(8):
                copy2(L_OUT2 + n, MO2[:, n, :])
            act.wait_ge(s.dense_sb, PU2 + L_UP)
            squares(tiles(13, 8))
            norm_scale(6)
            act.wait_ge(s.x2_ready, 2)
            squares(flat(X))
            norm_scale(7)
            scalar_loop2(act, fn, units_done, L_UP, 3)
            for c in range(3):
                act.wait_ge(s.conv_step, 48 * (c + 1))
                fn(tiles(48 + 8 * c, 8), tiles(48 + 8 * c, 8), ACT.Gelu_apprx_tanh).then_inc(s.ffn_gelu, 1)
            act.wait_ge(s.f_ready, 3)
            for n in range(KT):
                unit = L_DOWN + 3 * n + 2
                unit_done(d2_block(unit), block_ends(unit))
                fn(DO[:, n, :], B[(PU2 + L_DOWN + n) % 4][:, 0:SEQ], ACT.Copy).then_inc(s.dense_sb, 1)
            act.wait_ge(s.dense_sb, PU2 + L_DOWN + 8)
            squares(tiles(0, 8))
            norm_scale(8)

        def vector_block2(dve, v, link, norm_invert, norm_apply):
            norm_invert(5)
            norm_apply(H, X, par("mix_pre")).then_inc(s.h_ready, 1)

            def conv(n, out_t, src_t, w, b):
                w = par(w, 4 * n, 4 * n + 4)
                dve.wait_ge(s.dense_sb, PU2 + src_t + 1)
                return conv_taps(dve, nc, link, tiles(out_t, 1), tiles(src_t, 1), w, par(b, n, n + 1), 4)

            for n in range(12):
                last = conv(n, 53 + n, n, "ssm_conv_w", "ssm_conv_b")
            last.then_inc(s.xbc_conv, 1)
            dve.wait_ge(s.dense_sb, PU2 + 13)
            v.tensor_scalar(DT, tiles(12, 1), par("dt_bias"), None, ALU.add).then_inc(s.dt_in, 1)
            for n in range(KT):
                last = conv(n, n, 13 + n, "lru_conv_w", "lru_conv_b")
            last.then_inc(s.xc_ready, 1)
            dve.wait_ge(s.dt_soft, 1)
            dve.wait_ge(s.dt_in, 1)
            link(v.scalar_tensor_tensor(out=DT, in0=DT, scalar=0.0, in1=ADT, op0=ALU.max, op1=ALU.add))
            dve.wait_ge(s.a_exp, 1)
            link(v.tensor_scalar(ADT, DT, NEGA, -1.0, ALU.mult, ALU.mult))
            link(v.tensor_tensor_scan(LCUM, con("ssd_reset"), ADT, 0.0, ALU.mult, ALU.add))
            for c in range(4):
                r, a, b = slice(32 * c, 32 * c + 32), CHUNK * c, CHUNK * (c + 1)
                link(v.tensor_copy(TOT[r, :], LCUM[r, b - 1:b]))
                last = v.tensor_scalar(LCUM[r, a:b], LCUM[r, a:b], TOT[r, :], None, ALU.subtract)
            last.then_inc(s.cs_ready, 1)
            dve.wait_ge(s.lam_soft, 1)
            link(v.tensor_scalar(LAMC, par("lru_lam"), -1.0, 0.0, ALU.mult, ALU.max))
            link(v.tensor_tensor(LAMC, LAMC, LAMT, ALU.add))
            v.tensor_scalar(LAMC, LAMC, -4.0, None, ALU.mult).then_inc(s.lam_ready, 1)
            dve.wait_ge(s.ssd_tr, 1)
            for t in range(TT):
                for half in range(2):
                    r, at = slice(64 * half, 64 * half + 64), P * t + 64 * t + 32 * half
                    v.tensor_copy(LSH[r, t, :], B[4][r, at:at + SSM_H])
                last = v.tensor_copy(DTT[:, t, :], B[5][:, t * P:t * P + SSM_H])
            last.then_inc(s.ssd_sb, 1)
            dve.wait_ge(s.cs_ready, 1)
            for h in range(2):
                v.tensor_scalar(LMASK[:, h, :], LCUM, con("head_rows")[:, h:h + 1], None, ALU.mult).then_inc(s.lmask_ready, 1)
            for g in range(2):
                dve.wait_ge(s.cb_mm, g + 1)
                v.tensor_tensor(CBM[:, g, :], B[6 + g][:, 0:SSD_LEN], con("causal"), ALU.mult).then_inc(s.cb_ready, 1)
            dve.wait_ge(s.ssd_sb, 1)
            for n in range(4):
                t, part = n // 2, n % 2
                dve.wait_ge(s.xs_tr, n + 1)
                v.tensor_tensor(XDT[:, t, part * 512:(part + 1) * 512].rearrange("p (h c) -> p h c", h=8),
                                B[4 + n][:].rearrange("p (h c) -> p h c", h=8),
                                spread(DTT[:, t, 8 * part:8 * part + 8], 2, SSM_P), ALU.mult).then_inc(s.xdt_ready, 1)

            def segments(h):
                dve.wait_ge(s.bc_mm, h + 1)
                if h >= 2:
                    dve.wait_ge(s.ssd_y, h - 1)
                bank, seg = B[4 + h % 2], SEG[:, h % 2, :]
                v.tensor_scalar(seg[:, 0:SEQ], bank[:, 0:SEQ], LSH[:, 0, h:h + 1], 0.0, ALU.subtract, ALU.min)
                v.tensor_scalar(seg[:, SEQ:SSD_LEN], bank[:, SEQ:SSD_LEN], LSH[:, 1, h:h + 1], 0.0,
                                ALU.subtract, ALU.min).then_inc(s.seg_ready, 1)

            def lru_tile(k):
                i, th, t1 = tiles(I_OF[k], 1), TH[:, k, :], LRU_T
                if k == 0:
                    dve.wait_ge(s.th_ready, 1)
                    dve.wait_ge(s.ri_sig, KT)
                    dve.wait_ge(s.ly_gelu, 1)
                v.tensor_tensor(i, i, XC[:, k, :], ALU.mult)
                link(v.tensor_scalar(t1, th, -1.0, 1.0, ALU.mult, ALU.add))
                link(v.reciprocal(t1, t1))
                link(v.tensor_tensor(i, i, t1, ALU.mult))
                v.tensor_scalar(XC[:, k, :], th, -4.0, None, ALU.mult).then_inc(s.lru_neg, 1)
                link(v.scalar_tensor_tensor(out=th, in0=th, scalar=1.0, in1=t1, op0=ALU.add, op1=ALU.mult))
                dve.wait_ge(s.lru_root, k + 1)
                link(v.tensor_tensor(i, i, XC[:, k, :], ALU.mult))
                link(v.tensor_tensor_scan(XC[:, k, :], th, i, 0.0, ALU.mult, ALU.add))
                return v.tensor_tensor(XC[:, k, :], XC[:, k, :], LY[:, k, :], ALU.mult)

            def pair_out(n):
                dve.wait_ge(s.ssd_y, 2 * n + 2)
                v.scalar_tensor_tensor(out=YA[:, n, :], in0=YA[:, n, :], scalar=par("ssm_d", n, n + 1),
                                       in1=B[6 + n % 2][:, 0:SEQ], op0=ALU.mult, op1=ALU.add).then_inc(s.ya_pair, 1)

            segments(0)
            for h in range(SSM_H):
                if h + 1 < SSM_H:
                    segments(h + 1)
                if h + 2 < SSM_H:
                    dve.wait_ge(s.bc_mm, h + 1)
                    v.tensor_scalar(LMASK[:, h % 2, :], LCUM, con("head_rows")[:, h + 2:h + 3], None,
                                    ALU.mult).then_inc(s.lmask_ready, 1)
                dve.wait_ge(s.seg_exp, h + 1)
                v.tensor_tensor(SEG[:, h % 2, :], SEG[:, h % 2, :], CBM[:, h // 8, :], ALU.mult).then_inc(s.m_ready, 1)
                if h % 2:
                    last = lru_tile(h // 2)
                    if h >= 3:
                        pair_out(h // 2 - 1)
            last.then_inc(s.yb_ready, 1)
            pair_out(7)
            dve.wait_ge(s.ya_pair, 8)
            dve.wait_ge(s.z_silu, 1)
            v.tensor_tensor(YA, YA, Z, ALU.mult).then_inc(s.ya_gated, 1)
            dve.wait_ge(s.ya_sum, 1)
            for g in range(2):
                link(v.tensor_scalar(RS[:, g, :], B[4 + g][:, 0:SEQ], 1.0 / 512, EPS, ALU.mult, ALU.add))
            v.reciprocal(flat(RS), flat(RS)).then_inc(s.ya_inv, 1)
            dve.wait_ge(s.ya_gated, 1)
            dve.wait_ge(s.ya_rstd, 1)
            for k in range(KT):
                last = v.scalar_tensor_tensor(out=YA[:, k, :], in0=YA[:, k, :], scalar=par("ssm_norm", k, k + 1),
                                              in1=RS[:, k // 4, :], op0=ALU.mult, op1=ALU.mult)
            last.then_inc(s.ya_ready, 1)
            dve.wait_ge(s.g_sig, 1)
            dve.wait_ge(s.dense_sb, PU2 + L_SSM)
            link(v.tensor_tensor(PB, PB, GATE[:, 8:16, :], ALU.mult))
            dve.wait_ge(s.dense_sb, PU2 + L_OUT2)
            link(v.tensor_tensor(PA, PA, GATE[:, 0:8, :], ALU.mult))
            v.tensor_tensor(PA, PA, PB, ALU.add).then_inc(s.mg_ready, 1)
            norm_invert(6)
            link(norm_apply(MO2, MO2, par("mix_post")))
            v.tensor_tensor(X[:, :, :], X[:, :, :], MO2, ALU.add).then_inc(s.x2_ready, 1)
            norm_invert(7)
            norm_apply(H, X, par("ffn_pre")).then_inc(s.h_ready, 1)
            w_at, b_at = P_AT["ffn_conv_w"][0], P_AT["ffn_conv_b"][0]
            with dve.Fori(0, 3) as r:
                for j in range(8):
                    dve.wait_ge(s.dense_sb, r * ROUND + (PU2 + L_UP + 2 * j + 2))
                    gate = U[:, bass.ds(r * (ROUND * SEQ) + 2 * j * SEQ, SEQ)]
                    value = U[:, bass.ds(r * (ROUND * SEQ) + (2 * j + 1) * SEQ, SEQ)]
                    conved = U[:, bass.ds(r * (8 * SEQ) + (48 + j) * SEQ, SEQ)]
                    for n, (o, src) in enumerate(((conved, gate), (gate, value))):
                        def w(tap):
                            return params[:, bass.ds(r * 48 + (w_at + 6 * j + 3 * n + tap), 1)]

                        step = 6 * j + 3 * n
                        if n:
                            dve.wait_ge(s.conv_step, r * 48 + step)
                        v.tensor_scalar(o, src, w(2), params[:, bass.ds(r * 16 + (b_at + 2 * j + n), 1)],
                                        ALU.mult, ALU.add).then_inc(s.conv_step, 1)
                        for shift in (1, 2):
                            dve.wait_ge(s.conv_step, r * 48 + (step + shift))
                            v.scalar_tensor_tensor(out=o[:, shift:SEQ], in0=src[:, 0:SEQ - shift], scalar=w(2 - shift),
                                                   in1=o[:, shift:SEQ], op0=ALU.mult, op1=ALU.add).then_inc(s.conv_step, 1)
            values = tiles(0, 48).rearrange("p (n a t) -> p n a t", a=2, t=SEQ)[:, :, 0, :]
            for c in range(3):
                dve.wait_ge(s.ffn_gelu, c + 1)
                v.tensor_tensor(FV[:, 8 * c:8 * c + 8, :], FV[:, 8 * c:8 * c + 8, :], values[:, 8 * c:8 * c + 8, :],
                                ALU.mult).then_inc(s.f_ready, 1)
            norm_invert(8)
            link(norm_apply(DO, DO, par("ffn_post")))
            v.tensor_tensor(X[:, :, :], X[:, :, :], DO, ALU.add).then_inc(s.x2_ready, 1)

        AQ, AK, DOWNR, AG = tiles3(0, 2), tiles3(2, 2), tiles(4, 1), tiles3(5, 4)
        BQ, BK, BG = tiles3(9, 4), tiles(13, 1), tiles3(14, 4)
        AV = tiles(18, 4).rearrange("p (t c) -> p t c", t=TT)
        BV = tiles(22, 1).rearrange("p (t c) -> p t c", t=TT)
        LSG, SOFT, CUM = tiles3(23, 2), tiles3(25, 2), tiles3(27, 2)
        EXPB = tiles3(29, 2)
        QH = tiles3(31, 4)
        KE, KP = tiles3(35, 2), tiles3(37, 2)
        KPT = tiles(39, 4).rearrange("p (a t c) -> p a t c", a=2, t=TT)
        ATT = tiles(43, 4).rearrange("p (h t c) -> p h t c", h=4, t=TT)
        STATE = tiles(47, 3).rearrange("p (c n e) -> p c n e", c=3, n=2)
        GO, GR = tiles3(50, 4), tiles3(23, 4)
        LOG = tiles(56, 12).rearrange("p (h j) -> p h j", j=TPITCH)
        BIAS = tiles(68, 12).rearrange("p (h j) -> p h j", j=TPITCH)
        BQH = SQ
        EO, OO = tiles3(0, 8), tiles3(20, 8)
        CQ, CK, CG = tiles3(0, 8), tiles3(8, 2), tiles3(10, 8)
        CV = tiles(18, 2).rearrange("p (t c) -> p t c", t=TT)
        NCH = SEQ // CHUNK

        def bias_block(kind):
            toep = d["toep"]
            return [bass.AP(toep.tensor, kind * AH * P * TPITCH + first + P - 1,
                            [[TPITCH - 1, P], [P * TPITCH, AH], [1, n]]) for first, n in ((P, P), (0, 2 * P))]

        def side_block3(pool):
            pool.wait_ge(s.toep_stored, 16)
            for kind in range(2):
                if kind == 0:
                    pool.wait_ge(s.x2_ready, 3)
                else:
                    pool.wait_ge(s.lg_sb, AH)
                first, second = bias_block(kind)
                pool.dma_start(BIAS[:, :, 0:P], first).then_inc(s.bias_in, 16)
                pool.dma_start(BIAS[:, :, P:3 * P], second).then_inc(s.bias_in, 16)

        def tensor_block3(pe, mm, arrived, dense_unit, column_sums):
            def unit3(unit, act, tokens_out=False):
                tensor_dense2(pe, arrived, dense_unit, unit, act, PU3 + unit, tokens_out)

            column_sums(9)
            pe.wait_ge(s.h_ready, 3)
            for n in range(EVEN3):
                unit3(L_EVEN + n, H, n >= 18)
            pe.wait_ge(s.dense_sb, PU3 + L_EVEN + 5)
            up = par("gla_w_up")
            for n in range(2):
                last = mm(B[4][:, n * SEQ:(n + 1) * SEQ], up[0:16, n * P:(n + 1) * P], DOWNR[0:16, :])
            last.then_inc(s.gl_mm, 1)
            pe.wait_ge(s.kp_ready, 1)
            for t in range(TT):
                for n in range(2):
                    last = nc.tensor.transpose(B[5][:, t * SEQ + n * P:t * SEQ + (n + 1) * P], KP[:, n, t * P:(t + 1) * P], ident)
            last.then_inc(s.kp_tr, 1)
            for h in range(4):
                for t in range(TT):
                    last = mm(B[6 + h // 2][:, (h % 2) * SEQ + t * P:(h % 2) * SEQ + (t + 1) * P],
                              KE[:, h // 2, t * P:(t + 1) * P], QH[:, h, t * P:(t + 1) * P])
                if h % 2:
                    last.then_inc(s.att_mm, 1)
            pe.wait_ge(s.kpt_ready, 2)
            pe.wait_ge(s.dense_sb, PU3 + L_EVEN + EVEN3)
            for c in range(NCH - 1):
                for n in range(2):
                    last = mm(B[c][:, n * SEQ:(n + 1) * SEQ], KPT[:, c % 2, c // 2, n * P:(n + 1) * P],
                              AV[:, c // 2, n * SEQ:(n + 1) * SEQ])
                last.then_inc(s.kv_mm, 1)
            pe.wait_ge(s.att_ready, 2)
            pe.wait_ge(s.st_ready, 1)
            for h in range(4):
                o = B[4 + h]
                for t in range(TT):
                    mm(o[:, t * P:(t + 1) * P], AV[:, t, h * P:(h + 1) * P], ATT[:, h, t, :], t == 0, False)
                for c in range(1, NCH):
                    last = mm(o[:, c * CHUNK:(c + 1) * CHUNK], STATE[:, c - 1, h // 2, :], QH[:, h, c * CHUNK:(c + 1) * CHUNK],
                              False, c == NCH - 1)
                last.then_inc(s.o_mm, 1)
            pe.wait_ge(s.o_sq, 1)
            pe.wait_ge(s.o_sb, 4)
            for n in range(2):
                mm(B[4 + n][:], ones[:], tiles(43 + 2 * n, 2)).then_inc(s.o_sum, 1)

            def attention(kind, q_of, k_of, v_of, heads_of_tile):
                base = AH * kind
                for h in range(AH):
                    if h >= 4:
                        pe.wait_ge(s.lg_sb, base + h - 3)
                    q, k, bank = q_of(h), k_of(h), B[4 + h % 4]
                    mm(bank[:, 0:P], q[:, 0:P], k[:, 0:P])
                    mm(bank[:, P:3 * P], q[:, P:SEQ], k).then_inc(s.lg_mm, 1)
                pe.wait_ge(s.lg_ready, kind + 1)
                for h in range(AH):
                    if h >= 4:
                        pe.wait_ge(s.pt_sb, base + h - 3)
                    for j in range(3):
                        last = nc.tensor.transpose(B[4 + h % 4][:, j * P:(j + 1) * P], LOG[:, h, j * P:(j + 1) * P], ident)
                    last.then_inc(s.pt_tr, 1)
                pe.wait_ge(s.pt_sb, base + AH)
                for n, heads in enumerate(heads_of_tile):
                    if n >= 4:
                        pe.wait_ge(s.ao_ready, 4 * kind + n - 3)
                    rows = P // len(heads)
                    for i, h in enumerate(heads):
                        o = B[4 + n % 4][rows * i:rows * (i + 1), 0:SEQ]
                        mm(o[:, 0:P], v_of(h, 0), LOG[:, h, 0:P], True, False)
                        mm(o[:, P:SEQ], v_of(h, 0), LOG[:, h, P:2 * P], False, False)
                        last = mm(o[:, P:SEQ], v_of(h, 1), LOG[:, h, 2 * P:3 * P], False, True)
                    last.then_inc(s.ao_mm, 1)

            pe.wait_ge(s.oa_var, 1)
            pe.wait_ge(s.bqh_ready, 1)
            attention(0, lambda h: BQH[:, h, :], lambda h: BK,
                      lambda h, t: BV[:, t, 64 * (h // 4):64 * (h // 4) + 64], [(n, n + 4) for n in range(4)])
            pe.wait_ge(s.ao_ready, 4)
            for n in range(8):
                unit3(L_OE + n, H)
            column_sums(10)
            pe.wait_ge(s.h_ready, 4)
            for n in range(ODD3):
                unit3(L_ODD + n, H, n >= 18)
            pe.wait_ge(s.dense_sb, PU3 + L_OO)
            attention(1, lambda h: CQ[:, h, :], lambda h: CK[:, h // 4, :],
                      lambda h, t: CV[:, t, P * (h // 4):P * (h // 4) + P], [(n,) for n in range(AH)])
            pe.wait_ge(s.ao_ready, 12)
            for n in range(8):
                unit3(L_OO + n, H)
            column_sums(11)

        def scalar_block3(act, fn, link, squares, norm_scale, unit_done, units_done):
            def copy3(unit, dst, tokens_out=False):
                unit_done(d2_block(unit), block_ends(unit))
                src = B[(PU3 + unit) % 4][:, 0:SEQ]
                fn(dst, src.rearrange("p (t c) -> p t c", t=TT) if tokens_out else src, ACT.Copy).then_inc(s.dense_sb, 1)

            act.wait_ge(s.x2_ready, 3)
            squares(flat(X))
            norm_scale(9)
            for n in range(18):
                copy3(L_EVEN + n, tiles(n, 1))
            for n in range(18, 22):
                copy3(L_EVEN + n, AV[:, :, (n - 18) * P:(n - 17) * P], True)
            copy3(L_EVEN + 22, BV, True)
            act.wait_ge(s.gl_in, 1)
            flat2 = lambda a: tiles(a, 2)
            link(fn(flat2(25), flat2(23), ACT.Abs))
            link(fn(flat2(25), flat2(25), ACT.Exp, scale=-1.0))
            fn(flat2(25), flat2(25), ACT.Ln, bias=1.0).then_inc(s.gl_soft, 1)
            act.wait_ge(s.gl_b, 1)
            fn(flat2(29), flat2(27), ACT.Exp).then_inc(s.gl_exp, 1)
            fn(flat2(35), flat2(27), ACT.Exp, scale=-1.0).then_inc(s.gl_exp, 1)
            fn(DEC, CUM.rearrange("p n (c t) -> p n c t", t=CHUNK)[:, :, :, CHUNK - 1], ACT.Exp).then_inc(s.gl_exp, 1)
            act.wait_ge(s.gl_left, 1)
            fn(flat2(37), flat2(37), ACT.Exp).then_inc(s.gl_exp, 1)
            act.wait_ge(s.dense_sb, PU3 + L_EVEN + EVEN3)
            fn(tiles(5, 4), tiles(5, 4), ACT.Silu)
            fn(tiles(14, 4), tiles(14, 4), ACT.Silu).then_inc(s.eg_silu, 1)
            for h in range(4):
                act.wait_ge(s.o_mm, h + 1)
                fn(GO[:, h, :], B[4 + h][:, 0:SEQ], ACT.Copy).then_inc(s.o_sb, 1)
            act.wait_ge(s.o_sb, 4)
            fn(tiles(43, 4), tiles(50, 4), ACT.Square).then_inc(s.o_sq, 1)
            act.wait_ge(s.oa_var, 1)
            fn(tiles(23, 4), tiles(23, 4), ACT.Sqrt).then_inc(s.o_rstd, 1)

            def attention(kind):
                act.wait_ge(s.lg_shift, kind + 1)
                if kind == 0:
                    fn(ASNK, ASNK, ACT.Exp)
                fn(tiles(56, 12), tiles(56, 12), ACT.Exp).then_inc(s.lg_exp, 1)
                for h in range(AH):
                    act.wait_ge(s.pt_tr, AH * kind + h + 1)
                    fn(LOG[:, h, :], B[4 + h % 4][:, 0:3 * P], ACT.Copy).then_inc(s.pt_sb, 1)

            attention(0)
            for n in range(8):
                copy3(L_OE + n, EO[:, n, :])
            act.wait_ge(s.x2_ready, 4)
            squares(flat(X))
            norm_scale(10)
            for n in range(18):
                copy3(L_ODD + n, tiles(n, 1))
            for n in range(18, ODD3):
                copy3(L_ODD + n, CV[:, :, (n - 18) * P:(n - 17) * P], True)
            act.wait_ge(s.dense_sb, PU3 + L_OO)
            fn(tiles(10, 8), tiles(10, 8), ACT.Silu).then_inc(s.eg_silu, 1)
            attention(1)
            for n in range(8):
                copy3(L_OO + n, OO[:, n, :])
            act.wait_ge(s.x2_ready, 5)
            squares(flat(X))
            norm_scale(11)

        def vector_block3(dve, v, link, norm_invert, norm_apply):
            norm_invert(9)
            norm_apply(H, X, par("norm_gain", 0, 8)).then_inc(s.h_ready, 1)
            dve.wait_ge(s.gl_mm, 1)
            for n in range(2):
                last = v.tensor_scalar(LSG[:, n, :], B[4][:, n * SEQ:(n + 1) * SEQ], par("gla_b_up", n, n + 1), None, ALU.add)
            last.then_inc(s.gl_in, 1)
            dve.wait_ge(s.gl_soft, 1)
            dve.wait_ge(s.gl_in, 1)
            link(v.scalar_tensor_tensor(out=LSG, in0=LSG, scalar=0.0, in1=SOFT, op0=ALU.min, op1=ALU.subtract))
            link(v.tensor_scalar(LSG, LSG, 1.0 / 16.0, None, ALU.mult))
            for n in range(2):
                last = v.tensor_tensor_scan(CUM[:, n, :], con("gla_reset"), LSG[:, n, :], 0.0, ALU.mult, ALU.add)
            last.then_inc(s.gl_b, 1)
            dve.wait_ge(s.gl_b, 1)
            by_chunk = lambda ap: ap.rearrange("p n (c t) -> p (n c) t", t=CHUNK)
            cum = by_chunk(CUM)
            v.tensor_tensor(by_chunk(KP), spread(cum[:, :, CHUNK - 1], 2, CHUNK), cum, ALU.subtract).then_inc(s.gl_left, 1)
            dve.wait_ge(s.gl_exp, 2)
            dve.wait_ge(s.dense_sb, PU3 + L_EVEN + 4)
            link(v.scalar_tensor_tensor(out=EXPB, in0=AQ, scalar=float(64) ** -0.5, in1=EXPB, op0=ALU.mult, op1=ALU.mult))
            for h in range(4):
                v.tensor_scalar(QH[:, h, :], EXPB[:, h // 2, :], con("half")[:, h % 2:h % 2 + 1], None, ALU.mult)
            v.tensor_tensor(KE, KE, AK, ALU.mult)
            dve.wait_ge(s.gl_exp, 4)
            v.tensor_tensor(KP, KP, AK, ALU.mult).then_inc(s.kp_ready, 1)
            dve.wait_ge(s.kp_tr, 1)
            for a in range(2):
                v.tensor_scalar(KPT[:, a].rearrange("p t c -> p (t c)"), B[5][:], con("half")[:, a:a + 1], None,
                                ALU.mult).then_inc(s.kpt_ready, 1)
            dve.wait_ge(s.dense_sb, PU3 + L_EVEN + EVEN3)
            for h in range(AH):
                last = v.tensor_scalar(BQH[:, h, :], BQ[:, h % 4, :], con("half")[:, h // 4:h // 4 + 1], None, ALU.mult)
            last.then_inc(s.bqh_ready, 1)
            mask = spread(spread(con("gla_mask"), 1, TT), 1, 2)
            for n in range(2):
                dve.wait_ge(s.att_mm, n + 1)
                a = ATT[:, 2 * n:2 * n + 2]
                link(v.tensor_scalar(a.rearrange("p h t c -> p (h t c)"), B[6 + n][:], 3e38, -3e38, ALU.min, ALU.max))
                v.tensor_tensor(a, a, mask, ALU.mult).then_inc(s.att_ready, 1)
            for c in range(NCH - 1):
                dve.wait_ge(s.kv_mm, c + 1)
                for n in range(2):
                    for half in range(2):
                        r = slice(64 * half, 64 * half + 64)
                        own = B[c][r, n * SEQ + half * P:n * SEQ + (half + 1) * P]
                        if c == 0:
                            last = v.tensor_copy(STATE[r, 0, n, :], own)
                        else:
                            last = v.scalar_tensor_tensor(out=STATE[r, c, n, :], in0=STATE[r, c - 1, n, :],
                                                          scalar=DEC[r, n, c:c + 1], in1=own, op0=ALU.mult, op1=ALU.add)
                if c < NCH - 2:
                    link(last)
            last.then_inc(s.st_ready, 1)
            for n in range(2):
                dve.wait_ge(s.o_sum, n + 1)
                link(v.tensor_scalar(tiles(23 + 2 * n, 2), B[4 + n][:], 1.0 / P, EPS, ALU.mult, ALU.add))
            v.reciprocal(tiles(23, 4), tiles(23, 4)).then_inc(s.oa_var, 1)
            dve.wait_ge(s.o_rstd, 1)
            dve.wait_ge(s.eg_silu, 1)
            link(v.scalar_tensor_tensor(out=GO, in0=GO, scalar=par("gla_gain"), in1=GR, op0=ALU.mult, op1=ALU.mult))
            v.tensor_tensor(H[:, 0:4, :], GO, AG, ALU.mult)

            def attention(kind, scale):
                dve.wait_ge(s.bias_in, 32 * (kind + 1))
                for h in range(AH):
                    dve.wait_ge(s.lg_mm, AH * kind + h + 1)
                    v.scalar_tensor_tensor(out=LOG[:, h, :], in0=B[4 + h % 4][:, 0:3 * P], scalar=scale, in1=BIAS[:, h, :],
                                           op0=ALU.mult, op1=ALU.add).then_inc(s.lg_sb, 1)
                dve.wait_ge(s.lg_sb, AH * (kind + 1))
                parts = LOG[:, :, 0:P], LOG[:, :, P:3 * P]
                for b in range(2):
                    last = v.tensor_reduce(AMAX[:, :, b], parts[b], AXX, ALU.max)
                link(last)
                if kind == 0:
                    sinks = spread(par("sinks"), 2, 2)
                    link(v.tensor_tensor(AMAX, AMAX, sinks, ALU.max))
                    v.tensor_tensor(ASNK, sinks, AMAX, ALU.subtract)
                for b in range(2):
                    last = v.tensor_tensor(parts[b], parts[b], spread(AMAX[:, :, b], 2, (b + 1) * P), ALU.subtract)
                last.then_inc(s.lg_shift, 1)
                dve.wait_ge(s.lg_exp, kind + 1)
                for b in range(2):
                    last = v.tensor_reduce(ASUM[:, :, b], parts[b], AXX, ALU.add)
                link(last)
                if kind == 0:
                    link(v.tensor_tensor(ASUM, ASUM, ASNK, ALU.add))
                link(v.reciprocal(ASUM, ASUM))
                for b in range(2):
                    last = v.tensor_tensor(parts[b], parts[b], spread(ASUM[:, :, b], 2, (b + 1) * P), ALU.mult)
                last.then_inc(s.lg_ready, 1)

            attention(0, float(64) ** -0.5)
            for n in range(4):
                dve.wait_ge(s.ao_mm, n + 1)
                v.tensor_tensor(H[:, 4 + n, :], B[4 + n][:, 0:SEQ], BG[:, n, :], ALU.mult).then_inc(s.ao_ready, 1)
            dve.wait_ge(s.dense_sb, PU3 + L_ODD)
            v.tensor_tensor(X[:, :, :], X[:, :, :], EO, ALU.add).then_inc(s.x2_ready, 1)
            norm_invert(10)
            norm_apply(H, X, par("norm_gain", 8, 16)).then_inc(s.h_ready, 1)
            attention(1, float(P) ** -0.5)
            dve.wait_ge(s.eg_silu, 2)
            for n in range(AH):
                dve.wait_ge(s.ao_mm, 4 + n + 1)
                v.tensor_tensor(H[:, n, :], B[4 + n % 4][:, 0:SEQ], CG[:, n, :], ALU.mult).then_inc(s.ao_ready, 1)
            dve.wait_ge(s.dense_sb, PU3 + L_OO + 8)
            v.tensor_tensor(X[:, :, :], X[:, :, :], OO, ALU.add).then_inc(s.x2_ready, 1)
            norm_invert(11)
            norm_apply(X, X, par("final_gain")).then_inc(s.out_ready, 1)

        block = ctx.enter_context(nc.Block())

        @block.sync
        def _(sp):
            def load(block_no, src, wait=True):
                if wait and block_no >= RING:
                    sp.wait_ge(s.ring_used, block_no - RING + 1)
                sp.dma_start(ring[:, block_no % RING, :].rearrange("p (a n) -> p a n", a=src.shape[1]),
                             src).then_inc(ring_loaded[block_no % RING], 16)

            ada = d["w_ada"].rearrange("(k p) n -> p k n", p=P)
            for r in range(3):
                for b in range(4):
                    load(4 * r + b, ada[:, 2 * b:2 * b + 2, r * DEXP:(r + 1) * DEXP])
            for b in range(D1_BLOCKS):
                load(D1_BLOCK0 + b, d["dense1"][b].rearrange("p (a n) -> p a n", a=1))
            rows = EXPERTS * DM
            gate = d["w_gate"].rearrange("(k p) n -> p k n", p=P)
            up = d["w_up"].rearrange("(k p) n -> p k n", p=P)
            down = d["w_down"].rearrange("(e j c p) n -> e c p j n", e=EXPERTS, j=4, c=4)
            with sp.Fori(0, EXPERTS) as e:
                for b in range(EXP_BLOCKS):
                    sp.wait_ge(s.ring_used, e * EXP_BLOCKS + (EXP_BLOCK0 + b - RING + 1))
                    if b < 4:
                        src = gate[:, bass.ds(e * KT + 2 * b, 2), :]
                    elif b < 8:
                        src = up[:, bass.ds(e * KT + 2 * (b - 4), 2), :]
                    else:
                        src = down[bass.ds(e, 1), b - 8].rearrange("e p j n -> p (e j) n")
                    slot = (EXP_BLOCK0 + b) % RING
                    sp.dma_start(ring[:, slot, :].rearrange("p (a n) -> p a n", a=src.shape[1]),
                                 src).then_inc(ring_loaded[slot], 16)
            with sp.Fori(0, D2_BLOCKS // RING) as r:
                for b in range(RING):
                    sp.wait_ge(s.ring_used, r * RING + (D2_BLOCK0 + b - RING + 1))
                    slot = (D2_BLOCK0 + b) % RING
                    sp.dma_start(ring[:, slot, :], d["dense2"][bass.ds(r * RING + b, 1)]
                                 .rearrange("b p n -> p (b n)")).then_inc(ring_loaded[slot], 16)

        @block.gpsimd
        def _(pool):
            pool.wait_ge(s.toep_sb, 16)
            pool.dma_start(d["toep"].rearrange("h p j -> p h j")[:, :, 0:TOEP], TW[:, :, 0:TOEP]).then_inc(s.toep_stored, 16)
            side_block3(pool)
            pool.wait_ge(s.out_ready, 1)
            pool.dma_start(out, X[:, :, :]).then_inc(s.out_stored, 16)
            pool.wait_ge(s.lru_in, 16)
            pool.wait_ge(s.out_stored, 16)
            pool.wait_ge(s.toep_stored, 16)


        @block.tensor
        def _(pe):
            def mm(o, lhsT, rhs, start=True, stop=True):
                return nc.tensor.matmul(o, lhsT, rhs, start=start, stop=stop)

            def arrived(block_no):
                pe.wait_ge(ring_loaded[block_no % RING], uses(block_no))

            def dense_unit(block_no, sub, bank, act, tokens_out=False, start=True, stop=True):
                if not tokens_out:
                    for k in range(KT):
                        last = mm(bank[:, 0:SEQ], weights(block_no, sub, k), act[:, k, :],
                                  start and k == 0, stop and k == KT - 1)
                else:
                    for t in range(TT):
                        for k in range(KT):
                            last = mm(bank[:, t * P:(t + 1) * P], act[:, k, t * P:(t + 1) * P],
                                      weights(block_no, sub, k), k == 0, k == KT - 1)
                return last

            def column_sums(i, bank=7):
                pe.wait_ge(s.norm_squared, i + 1)
                if i:
                    pe.wait_ge(s.norm_inverted, i)
                for k in range(KT):
                    last = mm(B[bank][:, 0:SEQ], ones[:], SQ[:, k, :], k == 0, k == KT - 1)
                last.then_inc(s.norm_summed, 1)

            pe.wait_ge(s.consts_in, 16)
            pe.wait_ge(s.ones_ready, 1)
            pe.wait_ge(s.rel_ready, 1)
            for i in range(2 * AH):
                if i >= 2:
                    pe.wait_ge(s.toep_sb, i - 1)
                kind, h = i // AH, i % AH
                mm(B[4 + i % 2][:, 0:TOEP], RELB[0:REL_BUCKETS + 1, h, 0:P],
                   con("buckets")[0:REL_BUCKETS + 1, kind * TOEP:(kind + 1) * TOEP]).then_inc(s.toep_mm, 1)

            column_sums(0)
            column_sums(1)

            pe.wait_ge(s.c_ready, 1)
            for r in range(3):
                if r:
                    pe.wait_ge(s.ada_sb, r)
                for b in range(4):
                    arrived(4 * r + b)
                    for kk in range(2):
                        k = 2 * b + kk
                        for j in range(4):
                            at = kk * DEXP + j * 512
                            last = mm(B[0][32 * j:32 * j + 32, :], C2[:, k, :],
                                      ring[:, (4 * r + b) % RING, at:at + 512], k == 0, k == KT - 1)
                    last.then_inc(s.ring_used, 1)
                pe.wait_ge(s.ada_sb, r + 1)
                if r:
                    pe.wait_ge(s.mod_ready, r)
                for q in range(4):
                    last = nc.tensor.transpose(B[1][:, q * P:(q + 1) * P], ADA[:, q * P:(q + 1) * P], ident)
                last.then_inc(s.ada_tr, 1)

            pe.wait_ge(s.hc_ready, 1)
            pe.wait_ge(s.hx_ready, 1)
            pe.wait_ge(s.mod_ready, 3)
            for pu, (unit, act, tokens_out) in enumerate(DENSE1):
                if pu >= 4:
                    pe.wait_ge(s.dense_sb, pu - 3)
                blk, sub = D1_BLOCK0 + unit // UNITS, unit % UNITS
                arrived(blk)
                last = dense_unit(blk, sub, B[pu % 4], H if act == "x" else HC, tokens_out)
                last.then_inc(s.ring_used if block_ends(unit, act) else s.dense_mm, 1)
                if pu == 24:
                    pe.wait_ge(s.dense_sb, 20)
                    pe.wait_ge(s.toep_sb, 2 * AH)
                    pe.wait_ge(s.norm_inverted, 2)
                    for i in range(4):
                        mm(B[4 + i][:], con("swap"), tiles(16 + 2 * i, 2)).then_inc(s.rot_mm, 1)

            pe.wait_ge(s.kw_ready, 2)
            pe.wait_ge(s.qk_rot, 4)
            pe.wait_ge(s.dense_sb, 16)
            for a in range(2):
                for h in range(HEADS1):
                    for t in range(TT):
                        last = mm(B[4 + a][:, h * P:(h + 1) * P], KW[:, a, t, h * P:(h + 1) * P],
                                  VC[:, t, h * P:(h + 1) * P], t == 0, t == TT - 1)
                last.then_inc(s.state_mm, 1)
            for h in range(HEADS1):
                if h == 2:
                    pe.wait_ge(s.state_sb, 2)
                for m in range(TT):
                    last = mm(B[SCORE_BANK[h]][:, m * SEQ:(m + 1) * SEQ], KQR[:, h, m * P:(m + 1) * P], KQR[:, 4 + h, :])
                last.then_inc(s.score_mm, 1)
            pe.wait_ge(s.state_sb, 2)
            pe.wait_ge(s.qfb_ready, 1)
            for h in range(HEADS1):
                pe.wait_ge(s.sd_ready, h + 1)
                bank = B[SCORE_BANK[h]][:, 0:SEQ]
                for m in range(TT):
                    mm(bank, VX[:, m, h * P:(h + 1) * P], DM_[:, h, m, :], m == 0, False)
                mm(bank, SFB[:, 0, h, :], QFB[:, h, :], False, False)
                mm(bank, SFB[:, 1, h, :], QFB[:, 4 + h, :], False, True).then_inc(s.y_mm, 1)
            pe.wait_ge(s.y_sb, 4)
            for i in range(2):
                mm(B[4 + i][:], ones[:], tiles(16 + 2 * i, 2)).then_inc(s.mean_mm, 1)
            pe.wait_ge(s.ysq_ready, 1)
            for i in range(2):
                mm(B[6 + i][:], ones[:], tiles(16 + 2 * i, 2)).then_inc(s.var_mm, 1)

            pe.wait_ge(s.mix_ready, 1)
            for i in range(8):
                pu, unit = 36 + i, 28 + i
                pe.wait_ge(s.dense_sb, pu - 3)
                blk, sub = D1_BLOCK0 + unit // UNITS, unit % UNITS
                arrived(blk)
                last = dense_unit(blk, sub, B[pu % 4], MIX)
                last.then_inc(s.ring_used if block_ends(unit) else s.dense_mm, 1)
            column_sums(2)
            column_sums(3)

            pe.wait_ge(s.h2_ready, 1)
            wr = par("w_router").rearrange("p (k e) -> p k e", k=KT)
            for t in range(TT):
                for k in range(KT):
                    last = mm(B[4][:, t * EXPERTS:(t + 1) * EXPERTS], H[:, k, t * P:(t + 1) * P], wr[:, k, :], k == 0, k == KT - 1)
            last.then_inc(s.router_mm, 1)
            pe.wait_ge(s.dense_sb, 44)
            for n in range(4):
                for q in range(4):
                    t, k = n // 2, 4 * (n % 2) + q
                    last = nc.tensor.transpose(B[n][:, q * P:(q + 1) * P], H[:, k, t * P:(t + 1) * P], ident)
                last.then_inc(s.ht_tr, 1)
            pe.wait_ge(s.aff_ready, 1)
            for t in range(TT):
                last = nc.tensor.transpose(B[5][0:EXPERTS, t * P:(t + 1) * P], LOGIT[:, t, :], ident)
            last.then_inc(s.aff_tr, 1)
            pe.wait_ge(s.topk_ready, 1)
            mm(B[6][:], ones[0:EXPERTS, :], R16[0:EXPERTS, :])
            mm(B[7][:, 0:EXPERTS], IDX4[0:EXPERTS, :], ident[0:EXPERTS, 0:EXPERTS])
            mm(B[7][:, EXPERTS:2 * EXPERTS], VAL4[0:EXPERTS, :], ident[0:EXPERTS, 0:EXPERTS]).then_inc(s.slot_mm, 1)
            pe.wait_ge(s.sel_ready, 1)
            pe.wait_ge(s.ht_sb, 4)
            for k in range(KT):
                if k >= 4:
                    pe.wait_ge(s.xs_sb, k - 3)
                for t in range(TT):
                    last = mm(B[k % 4][:], HT[:, t, k * P:(k + 1) * P], SEL[:, t, :], t == 0, t == TT - 1)
                last.then_inc(s.xs_mm, 1)

            pe.wait_ge(s.xs_sb, KT)
            pe.wait_ge(s.slots_ready, 1)
            for q in range(4):
                mm(B[4 + q][:], ZERO[0:1, 0:P], ZERO[0:1, :], True, False)
            with pe.Fori(0, EXPERTS) as e:
                def expert_block(b):
                    blk = EXP_BLOCK0 + b
                    pe.wait_ge(ring_loaded[blk % RING], e * (16 * EXP_BLOCKS // RING) + uses(blk))
                    return blk % RING

                pe.wait_ge(s.xse_ready, e + 1)
                for half, bank in ((0, B[0]), (1, B[1])):
                    for b in range(4):
                        slot = expert_block(4 * half + b)
                        for kk in range(2):
                            k = 2 * b + kk
                            for j in range(4):
                                at = kk * DEXP + j * 512
                                last = mm(bank[32 * j:32 * j + 32, :], XSE[:, k, :], ring[:, slot, at:at + 512],
                                          k == 0, k == KT - 1)
                        last.then_inc(s.ring_used, 1)
                pe.wait_ge(s.hid_ready, e + 1)
                for q in range(4):
                    last = nc.tensor.transpose(B[0][:, q * P:(q + 1) * P], HID[:, q * P:(q + 1) * P], ident)
                last.then_inc(s.hid_tr, 1)
                pe.wait_ge(s.hidt_sb, e + 1)
                for c in range(4):
                    slot = expert_block(8 + c)
                    for half in range(2):
                        for j in range(4):
                            at = j * DM + half * 512
                            last = mm(B[2 + half][32 * j:32 * j + 32, :], HIDT[:, c * P + 32 * j:c * P + 32 * j + 32],
                                      ring[:, slot, at:at + 512], c == 0, c == 3)
                    last.then_inc(s.ring_used, 1)
                pe.wait_ge(s.selt_ready, e + 1)
                pe.wait_ge(s.y_low, e + 1)
                pe.wait_ge(s.y_high, e + 1)
                for k in range(KT):
                    last = nc.tensor.matmul(B[4 + k // 2][:, (k % 2) * SEQ:(k % 2 + 1) * SEQ], YE[:, k * P:(k + 1) * P],
                                            SELT[:], start=False, stop=False)
                last.then_inc(s.acc_done, 1)
            for q in range(4):
                last = mm(B[4 + q][:], ZERO[0:1, 0:P], ZERO[0:1, :], False, True)
            last.then_inc(s.acc_done, 1)
            column_sums(4, bank=3)
            tensor_block2(pe, mm, arrived, dense_unit, column_sums)
            tensor_block3(pe, mm, arrived, dense_unit, column_sums)

        @block.scalar
        def _(act):
            steps = [0]

            def link(ins):
                steps[0] += 1
                ins.then_inc(s.act_step, 1)
                act.wait_ge(s.act_step, steps[0])

            units_done = [0]

            def unit_done(block_no, ends):
                if ends:
                    act.wait_ge(s.ring_used, block_no + 1)
                else:
                    units_done[0] += 1
                    act.wait_ge(s.dense_mm, units_done[0])

            def fn(o, i, f, **kw):
                return nc.scalar.activation(o, i, f, **kw)

            def squares(src):
                return fn(flat(SQ), src, ACT.Square).then_inc(s.norm_squared, 1)

            def norm_scale(i):
                act.wait_ge(s.norm_inverted, i + 1)
                fn(RS[:, 0, :], RS[:, 0, :], ACT.Sqrt).then_inc(s.norm_scale, 1)

            act.dma_start(params[:], d["params"]).then_inc(s.params_in, 16)
            act.dma_start(consts[:], d["consts"]).then_inc(s.consts_in, 16)
            act.dma_start(CTXR, d["ctx"]).then_inc(s.ctx_in, 16)
            act.dma_start(X[:, :, :], d["x"]).then_inc(s.x_in, 16)
            act.dma_start(lru_w[:, :, :, :], d["lru_w"]).then_inc(s.lru_in, 16)

            act.wait_ge(s.params_in, 16)
            act.wait_ge(s.zeros_ready, 1)
            fn(C2[:, :, 0:2], par("cc").rearrange("p (k m) -> p k m", m=2), ACT.Silu).then_inc(s.c_ready, 1)
            link(fn(LT, par("decay"), ACT.Abs))
            link(fn(LT, LT, ACT.Exp, scale=-1.0))
            fn(LT, LT, ACT.Ln, bias=1.0).then_inc(s.decay_soft, 1)
            for i in range(2 * AH):
                act.wait_ge(s.toep_mm, i + 1)
                fn(TW[:, i, 0:TOEP], B[4 + i % 2][:, 0:TOEP], ACT.Copy).then_inc(s.toep_sb, 1)
            act.wait_ge(s.ctx_in, 16)
            squares(tiles(0, 8))
            norm_scale(0)
            act.wait_ge(s.x_in, 16)
            squares(flat(X))

            def ada_copy(r):
                act.wait_ge(s.ring_used, 4 * (r + 1))
                if r:
                    act.wait_ge(s.ada_tr, r)
                fn(ADA, B[0][:], ACT.Copy).then_inc(s.ada_sb, 1)

            ada_copy(0)
            norm_scale(1)
            act.wait_ge(s.consts_in, 16)
            act.wait_ge(s.ramp_ready, 1)
            fn(tiles(60, 8), tiles(60, 8), ACT.Exp).then_inc(s.dmat_ready, 1)
            for h in range(HEADS1):
                fn(QFB[:, h, :], con("row1"), ACT.Exp, scale=LG[:, h:h + 1])
                fn(QFB[:, 4 + h, :], con("row_rev"), ACT.Exp, scale=LG[:, 4 + h:5 + h])
                fn(WFB[:, :, h], con("tok_rev"), ACT.Exp, scale=LG[:, h:h + 1])
                last = fn(WFB[:, :, 4 + h], con("tok"), ACT.Exp, scale=LG[:, 4 + h:5 + h])
            last.then_inc(s.xi_ready, 1)
            ada_copy(1)
            ada_copy(2)

            act.wait_ge(s.toep_stored, 16)
            for pu, (unit, a, tokens_out) in enumerate(DENSE1):
                unit_done(D1_BLOCK0 + unit // UNITS, block_ends(unit, a))
                src, scale, i = B[pu % 4][:, 0:SEQ], 1.0, unit % 4
                if tokens_out:
                    src = src.rearrange("p (t c) -> p t c", t=TT)
                if unit < 4:
                    dst, scale = (KQ[:, i, :] if a == "x" else KC[:, :, i, :]), float(P) ** -0.5
                elif unit < 8:
                    dst = (VX if a == "x" else VC)[:, :, i * P:(i + 1) * P]
                else:
                    dst = (KQ[:, 4 + i, :], G_[:, i, :], B_[:, i, :], C_[:, i, :], XI_[:, i, :])[unit // 4 - 2]
                fn(dst, src, ACT.Copy, scale=scale).then_inc(s.dense_sb, 1)
            act.wait_ge(s.dense_sb, 36)
            fn(tiles(36, 4), tiles(36, 4), ACT.Silu).then_inc(s.g_silu, 1)
            for a in range(2):
                act.wait_ge(s.state_mm, a + 1)
                fn(SFB[:, a].rearrange("p h c -> p (h c)"), B[4 + a][:], ACT.Copy).then_inc(s.state_sb, 1)
            for h in range(HEADS1):
                act.wait_ge(s.y_mm, h + 1)
                fn(Y[:, h, :], B[SCORE_BANK[h]][:, 0:SEQ], ACT.Copy).then_inc(s.y_sb, 1)
            act.wait_ge(s.yc_ready, 1)
            fn(tiles(16, 4), tiles(20, 4), ACT.Square).then_inc(s.ysq_ready, 1)
            act.wait_ge(s.yvar_ready, 1)
            fn(tiles(52, 4), tiles(52, 4), ACT.Sqrt).then_inc(s.yrstd_ready, 1)
            for i in range(8):
                unit_done(D1_BLOCK0 + (28 + i) // UNITS, block_ends(28 + i))
                fn(MO[:, i, :], B[(36 + i) % 4][:, 0:SEQ], ACT.Copy).then_inc(s.dense_sb, 1)
            act.wait_ge(s.dense_sb, 44)
            squares(tiles(28, 8))
            norm_scale(2)
            act.wait_ge(s.x1_ready, 1)
            squares(flat(X))
            norm_scale(3)
            act.wait_ge(s.logit_shift, 1)
            fn(LOGIT, LOGIT, ACT.Exp).then_inc(s.aff_exp, 1)
            for n in range(4):
                act.wait_ge(s.ht_tr, n + 1)
                fn(HT[:, n // 2, (n % 2) * 512:(n % 2 + 1) * 512], B[n][:], ACT.Copy).then_inc(s.ht_sb, 1)
            for k in range(KT):
                act.wait_ge(s.xs_mm, k + 1)
                fn(XS[:, k, 0:EXPERTS * CAP], B[k % 4][:], ACT.Copy).then_inc(s.xs_sb, 1)
            with act.Fori(0, EXPERTS) as e:
                act.wait_ge(s.ring_used, e * EXP_BLOCKS + (EXP_BLOCK0 + 4))
                fn(SG, B[0][:], ACT.Silu).then_inc(s.silu_sb, 1)
                act.wait_ge(s.hid_tr, e + 1)
                fn(HIDT, B[0][:], ACT.Copy).then_inc(s.hidt_sb, 1)
                act.wait_ge(s.ring_used, e * EXP_BLOCKS + (EXP_BLOCK0 + 12))
                fn(YE[:, 0:512], B[2][:], ACT.Copy).then_inc(s.y_low, 1)
            act.wait_ge(s.acc_done, EXPERTS + 1)
            for q in range(4):
                last = fn(FO[:, 2 * q:2 * q + 2, :].rearrange("p k t -> p (k t)"), B[4 + q][:], ACT.Copy)
            last.then_inc(s.ffn_sb, 1)
            act.wait_ge(s.ffn_sb, 1)
            squares(tiles(60, 8))
            norm_scale(4)
            scalar_block2(act, fn, link, squares, norm_scale, unit_done, units_done)
            scalar_block3(act, fn, link, squares, norm_scale, unit_done, units_done)

        @block.vector
        def _(dve):
            steps = [0]
            v = nc.vector

            def link(ins):
                steps[0] += 1
                ins.then_inc(s.dve_step, 1)
                dve.wait_ge(s.dve_step, steps[0])

            def norm_invert(i, bank=7):
                dve.wait_ge(s.norm_summed, i + 1)
                link(v.tensor_scalar(RS[:, 0, :], B[bank][:, 0:SEQ], 1.0 / DM, EPS, ALU.mult, ALU.add))
                v.reciprocal(RS[:, 0, :], RS[:, 0, :]).then_inc(s.norm_inverted, 1)
                dve.wait_ge(s.norm_scale, i + 1)

            def norm_apply(dst, src, gain, shift=None):
                if shift is None:
                    for k in range(KT):
                        last = v.scalar_tensor_tensor(out=dst[:, k, :], in0=src[:, k, :], scalar=gain[:, k:k + 1],
                                                      in1=RS[:, 0, :], op0=ALU.mult, op1=ALU.mult)
                    return last
                link(v.tensor_tensor(dst, src, spread(RS[:, 0, :], 1, KT), ALU.mult))
                for k in range(KT):
                    last = v.tensor_scalar(dst[:, k, :], dst[:, k, :], gain[:, k:k + 1], shift[:, k:k + 1], ALU.mult, ALU.add)
                return last

            v.memset(ones[:], 1.0).then_inc(s.ones_ready, 1)
            v.memset(small(0, KT * 32), 0.0).then_inc(s.zeros_ready, 1)
            dve.wait_ge(s.params_in, 16)
            nb = REL_BUCKETS + 1
            v.tensor_copy(RELB[0:nb, :, :], spread(par("rel")[0:nb, :], 2, P)).then_inc(s.rel_ready, 1)
            dve.wait_ge(s.decay_soft, 1)
            v.scalar_tensor_tensor(out=LG, in0=par("decay"), scalar=0.0, in1=LT, op0=ALU.min,
                                   op1=ALU.subtract).then_inc(s.decay_ready, 1)
            dve.wait_ge(s.decay_ready, 1)
            dve.wait_ge(s.consts_in, 16)
            for h in range(HEADS1):
                ramp = DM_[:, h].rearrange("p m n -> p (m n)")
                link(v.tensor_scalar(ramp, con("ahead"), LG[:, h:h + 1], None, ALU.mult))
                last = v.scalar_tensor_tensor(out=ramp, in0=con("behind"), scalar=LG[:, 4 + h:5 + h], in1=ramp,
                                              op0=ALU.mult, op1=ALU.add)
            last.then_inc(s.ramp_ready, 1)

            def modulation(r):
                dve.wait_ge(s.ada_tr, r + 1)
                bias = par("b_ada", 16 * r, 16 * r + 16).rearrange("p (j q) -> p j q", j=4)
                v.tensor_tensor(MOD[:, 16 * r:16 * r + 16, :].rearrange("p (j q) s -> p j q s", j=4),
                                B[1][:].rearrange("p (q j m) -> p j q m", q=4, j=4)[:, :, :, 0:2],
                                spread(bias, 3, 2), ALU.add).then_inc(s.mod_ready, 1)
                dve.wait_ge(s.mod_ready, r + 1)

            def plus_one_times(o, scale, gain):
                link(v.scalar_tensor_tensor(out=o, in0=scale, scalar=1.0, in1=gain, op0=ALU.add, op1=ALU.mult))

            norm_invert(0)
            modulation(0)
            for a in range(2):
                plus_one_times(A1[:, a, :], MOD[:, 8:16, a], par("pre_mix_g"))
            norm_apply(HC, CTXR, A1[:, 1, :], MOD[:, 0:8, 1]).then_inc(s.hc_ready, 1)
            norm_invert(1)
            norm_apply(H[:, :, :], X[:, :, :], A1[:, 0, :], MOD[:, 0:8, 0]).then_inc(s.hx_ready, 1)
            modulation(1)
            modulation(2)
            plus_one_times(A2, MOD[:, 32:40, 0], par("pre_ffn_g"))
            link(v.tensor_tensor(G1P, MOD[:, 16:24, 0], par("post_mix_g"), ALU.mult))
            link(v.tensor_tensor(G2P, MOD[:, 40:48, 0], par("post_ffn_g"), ALU.mult))

            dve.wait_ge(s.toep_mm, 2 * AH)
            dve.wait_ge(s.hc_ready, 1)
            dve.wait_ge(s.dense_sb, 8)
            rot = ROT.rearrange("p (t h c) -> p t h c", t=TT, h=HEADS1)
            half = P // 2
            cos = spread(con("cos_t").rearrange("p (t c) -> p t c", t=TT), 2, HEADS1)
            sin = spread(con("sin_t").rearrange("p (t c) -> p t c", t=TT), 2, HEADS1)
            ta = tiles(0, 2).rearrange("p (t h c) -> p t h c", t=TT, h=HEADS1)
            tb = tiles(2, 2).rearrange("p (t h c) -> p t h c", t=TT, h=HEADS1)
            k1, k2 = KC[:, :, :, 0:half], KC[:, :, :, half:P]
            v.tensor_tensor(rot[:, :, :, 0:half], k1, cos, ALU.mult)
            link(v.tensor_tensor(ta, k2, sin, ALU.mult))
            v.tensor_tensor(rot[:, :, :, 0:half], rot[:, :, :, 0:half], ta, ALU.subtract)
            v.tensor_tensor(rot[:, :, :, half:P], k1, sin, ALU.mult)
            link(v.tensor_tensor(tb, k2, cos, ALU.mult))
            link(v.tensor_tensor(rot[:, :, :, half:P], rot[:, :, :, half:P], tb, ALU.add))
            dve.wait_ge(s.xi_ready, 1)
            for a in range(2):
                v.tensor_tensor(KW[:, a].rearrange("p t (h c) -> p t h c", h=HEADS1), rot,
                                spread(WFB[:, :, 4 * a:4 * a + 4], 3, P), ALU.mult).then_inc(s.kw_ready, 1)
            dve.wait_ge(s.dense_sb, 20)
            link(v.tensor_tensor(KQR, KQ, spread(con("cos_c"), 1, 8), ALU.mult))
            for i in range(4):
                dve.wait_ge(s.rot_mm, i + 1)
                t2 = tiles3(2 * i, 2)
                link(v.tensor_tensor(t2, B[4 + i][:].rearrange("p (k t) -> p k t", k=2), spread(con("sin_c"), 1, 2), ALU.mult))
                v.tensor_tensor(KQR[:, 2 * i:2 * i + 2, :], KQR[:, 2 * i:2 * i + 2, :], t2, ALU.add).then_inc(s.qk_rot, 1)
            dve.wait_ge(s.qk_rot, 4)
            v.tensor_tensor(QFB[:, 0:4, :], QFB[:, 0:4, :], KQR[:, 4:8, :], ALU.mult)
            v.tensor_tensor(QFB[:, 4:8, :], QFB[:, 4:8, :], KQR[:, 4:8, :], ALU.mult).then_inc(s.qfb_ready, 1)
            dve.wait_ge(s.dmat_ready, 1)
            for h in range(HEADS1):
                dve.wait_ge(s.score_mm, h + 1)
                dm = DM_[:, h].rearrange("p m n -> p (m n)")
                v.tensor_tensor(dm, B[SCORE_BANK[h]][:], dm, ALU.mult).then_inc(s.sd_ready, 1)
            dve.wait_ge(s.dense_sb, 36)
            link(v.tensor_tensor(C_, C_, XI_, ALU.mult))
            grid = lambda ap: ap.rearrange("p (r w) -> p r w", w=64)
            for i in range(4):
                w = par("conv_w", 3 * i, 3 * i + 3)
                o, u = grid(XI_[:, i, :]), grid(C_[:, i, :])
                link(v.tensor_scalar(XI_[:, i, :], C_[:, i, :], w[:, 1:2], par("conv_b", i, i + 1), ALU.mult, ALU.add))
                link(v.scalar_tensor_tensor(out=o[:, :, 1:64], in0=u[:, :, 0:63], scalar=w[:, 0:1], in1=o[:, :, 1:64],
                                            op0=ALU.mult, op1=ALU.add))
                link(v.scalar_tensor_tensor(out=o[:, :, 0:63], in0=u[:, :, 1:64], scalar=w[:, 2:3], in1=o[:, :, 0:63],
                                            op0=ALU.mult, op1=ALU.add))
            v.tensor_tensor(MIX[:, 0:4, :], XI_, B_, ALU.mult)
            dve.wait_ge(s.y_sb, 4)
            for i in range(2):
                dve.wait_ge(s.mean_mm, i + 1)
                last = v.scalar_tensor_tensor(out=tiles(20 + 2 * i, 2), in0=B[4 + i][:], scalar=-1.0 / P, in1=tiles(16 + 2 * i, 2),
                                              op0=ALU.mult, op1=ALU.add)
            last.then_inc(s.yc_ready, 1)
            for i in range(2):
                dve.wait_ge(s.var_mm, i + 1)
                link(v.tensor_scalar(tiles(52 + 2 * i, 2), B[6 + i][:], 1.0 / P, EPS, ALU.mult, ALU.add))
            v.reciprocal(tiles(52, 4), tiles(52, 4)).then_inc(s.yvar_ready, 1)
            dve.wait_ge(s.yrstd_ready, 1)
            link(v.tensor_tensor(YC, YC, R4, ALU.mult))
            dve.wait_ge(s.g_silu, 1)
            for h in range(HEADS1):
                last = v.scalar_tensor_tensor(out=MIX[:, 4 + h, :], in0=YC[:, h, :], scalar=par("ret_norm_g", h, h + 1),
                                              in1=G_[:, h, :], op0=ALU.mult, op1=ALU.mult)
            last.then_inc(s.mix_ready, 1)

            norm_invert(2)
            link(norm_apply(MO, MO, G1P))
            v.tensor_tensor(X[:, :, :], X[:, :, :], MO, ALU.add).then_inc(s.x1_ready, 1)
            norm_invert(3)
            norm_apply(H[:, :, :], X[:, :, :], A2, MOD[:, 24:32, 0]).then_inc(s.h2_ready, 1)
            v.memset(ZERO[0:1, :], 0.0)
            v.memset(XS[:, :, EXPERTS * CAP:], 0.0)

            dve.wait_ge(s.router_mm, 1)
            link(v.tensor_tensor(LOGIT, B[4][:, 0:32].rearrange("p (t e) -> p t e", t=TT), spread(par("b_router"), 1, TT), ALU.add))
            link(v.tensor_reduce(RMAX, LOGIT, AXX, ALU.max))
            v.tensor_tensor(LOGIT, LOGIT, spread(RMAX, 2, EXPERTS), ALU.subtract).then_inc(s.logit_shift, 1)
            dve.wait_ge(s.aff_exp, 1)
            link(v.tensor_reduce(RSUM, LOGIT, AXX, ALU.add))
            link(v.reciprocal(RSUM, RSUM))
            v.tensor_tensor(LOGIT, LOGIT, spread(RSUM, 2, EXPERTS), ALU.mult).then_inc(s.aff_ready, 1)
            dve.wait_ge(s.aff_tr, 1)
            at = AT[0:EXPERTS, :]
            link(v.tensor_copy(at, B[5][0:EXPERTS, 0:SEQ]))
            for r in range(CAP // 8):
                best = VAL[0:EXPERTS, 8 * r:8 * r + 8]
                link(v.max(best, at))
                link(v.max_index(idx_u[:, 8 * r:8 * r + 8], best, at))
                link(v.match_replace(at, best, at, -1.0))
            link(v.tensor_copy(IDXF[0:EXPERTS, :], idx_u[:]))
            e16 = EXPERTS
            v.tensor_tensor(R16[0:e16, :].rearrange("p (e c) -> p e c", e=e16), spread(IDXF[0:e16, :], 1, e16),
                            con("own_expert")[0:e16, :].rearrange("p (e c) -> p e c", e=e16), ALU.mult)
            v.tensor_copy(IDX4[0:e16, :].rearrange("p (j c) -> p j c", j=4), spread(IDXF[0:e16, :], 1, 4))
            v.tensor_copy(VAL4[0:e16, :].rearrange("p (j c) -> p j c", j=4), spread(VAL[0:e16, :], 1, 4)).then_inc(s.topk_ready, 1)
            dve.wait_ge(s.slot_mm, 1)
            for t in range(TT):
                last = v.tensor_scalar(SEL[:, t, :], B[6][:], con("tok")[:, t:t + 1], None, ALU.is_equal)
            last.then_inc(s.sel_ready, 1)
            v.tensor_copy(small(460, 32), B[7][:, 0:32]).then_inc(s.slots_ready, 1)

            dve.wait_ge(s.xs_sb, KT)
            dve.wait_ge(s.slots_ready, 1)
            v.tensor_copy(XSE, XS[:, :, 0:CAP]).then_inc(s.xse_ready, 1)
            with dve.Fori(0, EXPERTS) as e:
                dve.wait_ge(s.ring_used, e * EXP_BLOCKS + (EXP_BLOCK0 + 8))
                dve.wait_ge(s.silu_sb, e + 1)
                v.tensor_tensor(HID, SG, B[1][:], ALU.mult).then_inc(s.hid_ready, 1)
                v.tensor_copy(XSE, XS[:, :, bass.ds(e * CAP + CAP, CAP)]).then_inc(s.xse_ready, 1)
                v.tensor_scalar(SELT, con("row"), SLOT_TOK[:, bass.ds(e, 1)], SLOT_GATE[:, bass.ds(e, 1)],
                                ALU.is_equal, ALU.mult).then_inc(s.selt_ready, 1)
                dve.wait_ge(s.ring_used, e * EXP_BLOCKS + (EXP_BLOCK0 + 12))
                v.tensor_copy(YE[:, 512:1024], B[3][:]).then_inc(s.y_high, 1)
            dve.wait_ge(s.ffn_sb, 1)
            norm_invert(4, bank=3)
            link(norm_apply(FO, FO, G2P))
            v.tensor_tensor(X[:, :, :], X[:, :, :], FO, ALU.add).then_inc(s.x2_ready, 1)
            vector_block2(dve, v, link, norm_invert, norm_apply)
            vector_block3(dve, v, link, norm_invert, norm_apply)


def bucket_table():
    dist = 2 * P - 1 - np.arange(TOEP)
    n = np.maximum(dist, 0)
    ratio = np.log(np.maximum(n, 1).astype(np.float32) / np.float32(REL_EXACT)) / np.float32(math.log(REL_DIST / REL_EXACT))
    large = np.minimum(REL_EXACT + (ratio * np.float32(REL_BUCKETS - REL_EXACT)).astype(np.int32), REL_BUCKETS - 1)
    bucket = np.where(n < REL_EXACT, n, large)
    out = np.zeros((P, 2, TOEP), np.float32)
    for kind, limit in enumerate((P, SEQ)):
        row = np.where((dist >= 0) & (dist < limit), bucket, REL_BUCKETS)
        out[row, kind, np.arange(TOEP)] = 1.0
    return out.reshape(P, 2 * TOEP)


def const_table():
    f = np.float32
    p, n = np.arange(P), np.arange(SEQ)
    t = np.zeros((P, C_COLS), f)

    def put(name, a):
        at, cols = C_AT[name]
        a = np.asarray(a, f)
        t[:, at:at + cols] = np.broadcast_to(a.reshape(a.shape[0], -1) if a.ndim > 1 else a[None], (P, cols))

    put("ident", np.eye(P))
    swap = np.zeros((P, P), f)
    swap[np.arange(64) + 64, np.arange(64)] = -1.0
    swap[np.arange(64), np.arange(64) + 64] = 1.0
    put("swap", swap)
    half = P // 2
    inv = f(1.0) / np.power(f(10000.0), np.arange(half, dtype=f) / f(half))
    ang = (SEQ + n).astype(f)[None, :] * inv[p % half][:, None]
    put("cos_c", np.cos(ang)), put("sin_c", np.sin(ang))
    pos = p[:, None] + P * np.arange(TT)[None, :]
    ang = pos.astype(f)[:, :, None] * inv[None, None, :]
    put("cos_t", np.cos(ang)), put("sin_t", np.sin(ang))
    rel = n[None, None, :] - pos[:, :, None]
    put("ahead", np.maximum(rel, 0)), put("behind", np.maximum(-rel, 0))
    put("row1", n + 1), put("row_rev", SEQ - n), put("row", n)
    put("tok", pos), put("tok_rev", SEQ - 1 - pos)
    put("own_expert", (p[:, None, None] == np.arange(EXPERTS)[None, :, None]) * np.ones((1, 1, CAP)))
    c = p // 32
    starts = n % CHUNK == 0
    put("ssd_reset", ~(starts[None] & ((n // CHUNK)[None] >= c[:, None]) & ((n // CHUNK)[None] <= c[:, None] + 1)))
    chunk_of = (pos // CHUNK).T
    put("chunk_rows", c[:, None, None] == chunk_of[None])
    put("head_rows", (p % 32)[:, None] == np.arange(SSM_H)[None])
    causal = pos[:, :, None] <= n[None, None, :]
    put("causal", np.concatenate([causal[:, 0], causal[:, 1, P:]], 1))
    put("gla_reset", ~starts)
    put("gla_mask", (p[:, None] // CHUNK == p[None] // CHUNK) & (p[:, None] <= p[None]))
    put("half", np.stack([p < 64, p >= 64], 1))
    put("buckets", bucket_table())
    return t


def kernel(**inputs):
    import concourse.bacc as bacc
    from concourse.bass_utils import run_bass_kernel_spmd

    f = np.float32
    i = {k: np.asarray(v) for k, v in inputs.items()}
    cols = lambda a: np.asarray(a).reshape(-1, P).T
    taps = lambda w: w.reshape(w.shape[0], -1, P).transpose(2, 1, 0).reshape(P, -1)
    every = lambda a: np.broadcast_to(np.asarray(a).reshape(1, -1), (P, np.asarray(a).size))

    def rows(a, at=(0,)):
        o = np.zeros((P, a.shape[1]), f)
        for r in at:
            o[r:r + a.shape[0]] = a
        return o

    pairs = np.arange(2 * FT).reshape(2, FT).T.ravel()
    by_tile = lambda a: a.reshape(a.shape[0], -1, P)[:, pairs].reshape(a.shape[0], -1)
    chunks = range(0, P, 32)
    values = {
        "cc": np.stack([cols(i["c"][0]), cols(i["c_ctx"])], -1).reshape(P, -1),
        "b_ada": cols(i["b_ada"][0]), "pre_mix_g": cols(i["pre_mix_g"][0]), "post_mix_g": cols(i["post_mix_g"][0]),
        "pre_ffn_g": cols(i["pre_ffn_g"][0]), "post_ffn_g": cols(i["post_ffn_g"][0]),
        "conv_w": taps(i["conv_w"][0]), "conv_b": cols(i["conv_b"][0]), "decay": every(i["ret_decay_logit"][0]),
        "ret_norm_g": cols(i["ret_norm_g"][0]), "b_router": every(i["b_router"][0]),
        "w_router": i["w_router"][0].reshape(KT, P, EXPERTS).transpose(1, 0, 2).reshape(P, -1),
        "mix_pre": cols(i["mix_pre_norm_2"][0]), "mix_post": cols(i["mix_post_norm_2"][0]),
        "ssm_conv_w": taps(i["ssm_conv_w_2"][0]), "ssm_conv_b": cols(i["ssm_conv_b_2"][0]),
        "dt_bias": rows(i["ssm_dt_bias_2"][0][:, None], chunks), "a_log": rows(i["ssm_a_log_2"][0][:, None], chunks),
        "ssm_d": cols(np.repeat(i["ssm_d_2"][0], SSM_P)), "ssm_norm": cols(i["ssm_norm_2"][0]),
        "lru_conv_w": taps(i["lru_conv_w_2"][0]), "lru_conv_b": cols(i["lru_conv_b_2"][0]),
        "lru_br": cols(i["lru_br_2"][0].ravel()), "lru_bi": cols(i["lru_bi_2"][0].ravel()), "lru_lam": cols(i["lru_lambda_2"][0]),
        "gate_b": cols(i["gate_b_2"][0].ravel()), "ffn_pre": cols(i["ffn_pre_norm_2"][0]), "ffn_post": cols(i["ffn_post_norm_2"][0]),
        "ffn_conv_w": taps(by_tile(i["ffn_conv_w_2"][0])), "ffn_conv_b": cols(by_tile(i["ffn_conv_b_2"])[0]),
        "norm_gain": cols(i["norm_gain_3"].ravel()), "final_gain": cols(i["final_gain_3"]),
        "gla_b_up": cols(i["gla_b_up_3"][0]), "gla_gain": cols(i["gla_norm_gain_3"][0]), "sinks": every(i["swa_sinks_3"][0]),
        "rel": rows(np.concatenate([i["rel_bias_3"], np.full((1, AH), -1e30, f)])),
        "gla_w_up": rows(i["gla_w_up_3"][0]),
    }
    params = np.zeros((P, P_COLS), f)
    for name, (at, n) in P_AT.items():
        params[:, at:at + n] = values[name]

    def units(w, pick=None):
        w = w if pick is None else w[:, pick]
        return w.reshape(KT, P, -1, P).transpose(2, 1, 0, 3)

    def blocks(parts):
        u = np.concatenate(parts)
        return np.ascontiguousarray(u.reshape(-1, UNITS, P, KT * P).transpose(0, 2, 1, 3)).reshape(-1, P, BLK)

    r = lambda a, b: np.arange(a, b)
    w1 = i["w_in"][0]
    dense1 = blocks([units(w1, np.concatenate([r(2048, 3072), r(1536, 2048), r(3072, 3584), r(0, 1536)])), units(i["w_out"][0])])

    w2 = i["w_in_2"][0]
    z, xbc = r(0, 1024), r(1024, 2560)
    dt = np.zeros((DM, P), f)
    for a in chunks:
        dt[:, a:a + SSM_H] = w2[:, 2560:2576]
    w3 = i["w_in_even_3"][0]
    splits = np.cumsum([0, 256, 256, 512, 16, 512, 512, 128, 128, 512])
    aq, ak, av, ad, ag, bq, bk, bv, bg = (r(a, b) for a, b in zip(splits[:-1], splits[1:]))
    pair = (r(0, 512).reshape(2, 4, 64).transpose(1, 0, 2)).ravel()
    down_rank = np.zeros((DM, P), f)
    down_rank[:, 0:16] = w3[:, ad]
    we = i["w_out_even_3"][0][np.concatenate([r(0, 512), 512 + pair])]
    w4 = i["w_in_odd_3"][0]
    wd = i["w_ffn_down_2"][0].reshape(3, KT, P, KT, P).transpose(3, 0, 2, 1, 4).reshape(-1, P, KT, P)
    dense2 = blocks([
        units(w2, xbc), units(dt), units(w2, np.concatenate([r(3600, 4624), r(2576, 3600), z, r(4624, 6672)])),
        units(i["w_proj_lru_2"][0]), units(i["w_proj_ssm_2"][0]), units(i["w_out_2"][0]),
        units(i["w_ffn_up_2"][0].reshape(DM, -1, P)[:, pairs].reshape(DM, -1)), wd,
        units(w3, np.concatenate([aq, ak])), units(down_rank), units(w3, np.concatenate([ag, bq[pair], bk, bg[pair], av, bv])),
        units(we), units(w4, np.concatenate([r(0, 1280), r(1536, 2560), r(1280, 1536)])), units(i["w_out_odd_3"][0])])
    lru = np.zeros((2, KT, P, P), f)
    for n, name in enumerate(("lru_wr_2", "lru_wi_2")):
        w = i[name][0].reshape(KT, 2, 64, 64)
        for b in range(2):
            lru[n, :, 64 * b:64 * b + 64, 64 * b:64 * b + 64] = w[:, b]
    by_channel = lambda a: np.ascontiguousarray(a.reshape(SEQ, KT, P).transpose(2, 1, 0))
    arrays = {
        "in_x": by_channel(i["x"][0]), "in_ctx": by_channel(i["ctx"][0]), "in_params": params, "in_consts": const_table(),
        "in_lru_w": np.ascontiguousarray(lru.transpose(2, 0, 1, 3)), "in_w_ada": i["w_ada"][0],
        "in_dense1": dense1, "in_dense2": dense2, "in_w_gate": i["w_gate"][0].reshape(-1, DEXP),
        "in_w_up": i["w_up"][0].reshape(-1, DEXP), "in_w_down": i["w_down"][0].reshape(-1, DM),
    }
    nc = bacc.Bacc("TRN2", target_bir_lowering=False, num_devices=1)
    d = {n[3:]: nc.dram_tensor(n, a.shape, F32, kind="ExternalInput").ap() for n, a in arrays.items()}
    d["toep"] = nc.dram_tensor("bias_diagonals", (2 * AH, P, TPITCH), F32).ap()
    out = nc.dram_tensor("out_x", (P, KT, SEQ), F32, kind="ExternalOutput").ap()
    program(nc, d, out)
    got = run_bass_kernel_spmd(nc, [arrays], core_ids=[0]).results[0]["out_x"]
    return np.ascontiguousarray(got.transpose(2, 1, 0)).reshape(1, SEQ, DM)
```

```python
import math
from contextlib import ExitStack
from collections import namedtuple

import numpy as np

import concourse.bass as bass
from concourse import mybir
from concourse.alu_op_type import AluOpType as ALU

F32 = mybir.dt.float32
U32 = mybir.dt.uint32
ACT = mybir.ActivationFunctionType
AXX = mybir.AxisListType.X

P = 128
SEQ = 256
DM = 1024
KT = DM // P
TT = SEQ // P
EPS = 1e-6
HEADS1 = 4
EXPERTS = 16
CAP = 2 * SEQ // EXPERTS
DEXP = 2 * DM
SSM_H, SSM_P, CHUNK = 16, 64, 64
FFN = 3072
FT = FFN // P
REL_BUCKETS, REL_EXACT, REL_DIST = 32, 16, 128
AH = 8
TOEP = 383
TPITCH = 384

RING = 4
BLK = 4096
UNITS = 4
ADA_BLOCKS = 12
D1_UNITS = 28 + 8
D1_BLOCKS = D1_UNITS // UNITS
EXP_BLOCKS = 12
IN2, OUT2 = 53, 8
EVEN3, ODD3 = 23, 20
D2_LAYERS = (IN2, 8, 8, 8, 2 * FT, 8 * 3, EVEN3, 8, ODD3, 8)
D2_UNITS = sum(D2_LAYERS)
D2_BLOCKS = D2_UNITS // UNITS
FIRST = ([("ada", b) for b in range(4)]
         + [x for b in range(4) for x in (("dense", b), ("ada", 4 + 2 * b), ("ada", 5 + 2 * b))]
         + [("dense", b) for b in range(4, D1_BLOCKS)])
EXP_BLOCK0 = len(FIRST)
D2_BLOCK0 = EXP_BLOCK0 + EXPERTS * EXP_BLOCKS

PARAMS = [("cc", 16), ("b_ada", 48), ("pre_mix_g", 8), ("post_mix_g", 8), ("pre_ffn_g", 8), ("post_ffn_g", 8),
          ("conv_w", 12), ("conv_b", 4), ("decay", 8), ("ret_norm_g", 4), ("b_router", 16), ("w_router", 128),
          ("mix_pre", 8), ("mix_post", 8), ("ssm_conv_w", 48), ("ssm_conv_b", 12), ("dt_bias", 1), ("a_log", 1),
          ("ssm_d", 8), ("ssm_norm", 8), ("lru_conv_w", 32), ("lru_conv_b", 8), ("lru_br", 8), ("lru_bi", 8),
          ("lru_lam", 8), ("gate_b", 16), ("ffn_pre", 8), ("ffn_post", 8), ("ffn_conv_w", 144), ("ffn_conv_b", 48),
          ("norm_gain", 16), ("final_gain", 8), ("gla_b_up", 2), ("gla_gain", 1), ("sinks", 8), ("rel", 8),
          ("gla_w_up", 256)]
CONSTS = [("ident", 128), ("swap", 128), ("cos_c", 256), ("sin_c", 256), ("cos_t", 128), ("sin_t", 128),
          ("ahead", 512), ("behind", 512), ("row1", 256), ("row_rev", 256), ("row", 256), ("tok", 2), ("tok_rev", 2),
          ("own_expert", 512), ("ssd_reset", 256), ("chunk_rows", 256), ("head_rows", 16), ("causal", 384),
          ("gla_reset", 256), ("gla_mask", 128), ("half", 2), ("buckets", 2 * TOEP)]


def offsets(entries):
    at, out = 0, {}
    for name, n in entries:
        out[name] = (at, n)
        at += n
    return out, at


P_AT, P_COLS = offsets(PARAMS)
C_AT, C_COLS = offsets(CONSTS)

SEMS = """dense_sb ring_used dense_mm h_ready xc_ready lru_in ri_sig ri_mm cs_ready ssd_tr xbc_silu cb_mm ssd_sb cb_ready
xs_tr lmask_ready seg_ready bc_mm xdt_ready m_ready ya_pair ssd_y yb_ready ya_sq ya_sum ya_ready mg_ready f_ready
x_ready dt_in dt_soft a_exp lam_soft xbc_conv lam_ready th_ready ly_gelu z_silu seg_exp lru_neg lru_root g_sig
ya_gated ya_inv ya_rstd conv_step ffn_gelu toep_stored lg_sb bias_in lg_mm lg_ready pt_sb pt_tr ao_ready ao_mm
gl_mm kp_ready kp_tr att_mm kpt_ready att_ready bqh_ready kv_mm st_ready o_mm o_sq o_sb o_sum oa_var oa_ready
lg_shift lg_exp gl_in gl_soft gl_b gl_exp gl_left eg_silu o_rstd out_ready out_stored toep_sb norm_squared
norm_root norm_summed consts_in ones_ready rel_ready toep_mm ada_sb ada_tr c_ready mod_ready hc_ready hx_ready
rot_mm kw_ready qk_rot state_mm state_sb score_mm qfb_ready sd_ready y_mm y_sb mean_mm ysq_ready var_mm mix_ready
h2_ready router_mm ht_tr aff_ready aff_tr topk_ready slot_mm sel_ready ht_sb xs_sb xs_mm slots_ready xse_ready
hid_ready hid_tr hidt_sb selt_ready y_low y_high acc_done act_step params_in ctx_in x_in zeros_ready decay_soft
ramp_ready dmat_ready xi_ready g_silu yc_ready yvar_ready yrstd_ready logit_shift aff_exp silu_sb ffn_sb dve_step
norm_inverted decay_ready""".split()


DENSE1 = ([(u, a, a == "ctx" or u >= 4) for u in range(8) for a in ("ctx", "x")]
          + [(u, "x", False) for u in range(8, 28)])
SCORE_BANK = (6, 7, 4, 5)
ADA_BANK = (0, 4, 6)
ADA_AFTER = {7: (4, 5), 15: (6, 7), 19: (8, 9), 23: (10, 11)}


def ada_block(b):
    return FIRST.index(("ada", b))


def d1_block(unit):
    return FIRST.index(("dense", unit // UNITS))


def block_ends(unit, act="x"):
    return unit % UNITS == UNITS - 1 and act == "x"


def conv_taps(dve, nc, link, out, src, w, bias, taps):
    link(nc.vector.tensor_scalar(out, src, w[:, taps - 1:taps], bias, ALU.mult, ALU.add))
    for s in range(1, taps):
        last = nc.vector.scalar_tensor_tensor(out=out[:, s:SEQ], in0=src[:, 0:SEQ - s], scalar=w[:, taps - 1 - s:taps - s],
                                              in1=out[:, s:SEQ], op0=ALU.mult, op1=ALU.add)
        if s < taps - 1:
            link(last)
    return last


def spread(ap, axis, n):
    a = ap.unsqueeze(axis)
    shape = list(a.shape)
    shape[axis] = n
    return a.broadcast_to(shape)


def program(nc, d, out):
    ctx = ExitStack()
    with ctx:
        def sb(name, shape, dt=F32):
            return ctx.enter_context(nc.sbuf_tensor(name, shape, dt))

        s = namedtuple("Semaphores", SEMS)(*[ctx.enter_context(nc.semaphore(n)) for n in SEMS])
        ring_loaded = [ctx.enter_context(nc.semaphore(f"ring_loaded{i}")) for i in range(RING)]
        B = [ctx.enter_context(nc.psum_tensor(f"bank{i}", [P, 512], F32)) for i in range(8)]

        ring = sb("ring", [P, RING, BLK])
        params = sb("params", [P, P_COLS])
        consts = sb("consts", [P, C_COLS])
        lru_w = sb("lru_w", [P, 2, KT, P])
        X = sb("x_resid", [P, KT, SEQ])
        H = sb("h_normed", [P, KT, SEQ])
        SQ = sb("squares", [P, KT, SEQ])
        RS = sb("rstd", [P, 2, SEQ])
        U = sb("work", [P, 80 * SEQ])
        ones = sb("ones", [P, P])
        sm = sb("small", [P, 1024])
        idx_u = sb("topk_index", [EXPERTS, CAP], U32)

        def par(name, a=None, b=None):
            at, n = P_AT[name]
            return params[:, at + (0 if a is None else a):at + (n if b is None else b)]

        def con(name):
            at, n = C_AT[name]
            return consts[:, at:at + n]

        def tiles(a, n):
            return U[:, a * SEQ:(a + n) * SEQ]

        def tiles3(a, n):
            return tiles(a, n).rearrange("p (n t) -> p n t", t=SEQ)

        def small(at, n):
            return sm[:, at:at + n]

        ident = con("ident")
        flat = lambda ap: ap[:, :, :].rearrange("p k t -> p (k t)")

        def weights(block, sub, k):
            at = (sub * KT + k) * P
            return ring[:, block % RING, at:at + P]

        def uses(block):
            return 16 * (block // RING + 1)

        C2 = small(0, KT * 32).rearrange("p (k m) -> p k m", m=32)
        MOD = small(256, 96).rearrange("p (n s) -> p n s", s=2)
        A1 = small(352, 16).rearrange("p (s k) -> p s k", s=2)
        A2 = small(368, 8)
        G1P = small(376, 8)
        G2P = small(384, 8)
        LG = small(392, 8)
        LT = small(400, 8)
        WFB = small(408, 16).rearrange("p (t h) -> p t h", t=TT)
        LOGIT = small(424, 32).rearrange("p (t e) -> p t e", t=TT)
        RMAX = small(456, 2)
        RSUM = small(458, 2)
        SLOT_TOK = small(460, 16)
        SLOT_GATE = small(476, 16)
        VAL = small(492, 32)
        IDXF = small(524, 32)
        IDX4 = small(556, 128)
        VAL4 = small(684, 128)
        ROOT_WARM, EPS_COL = small(958, 12), small(957, 1)
        NEGA = small(812, 1)
        TOT = small(813, 1)
        LSH = small(814, 32).rearrange("p (t h) -> p t h", t=TT)
        LAMC = small(846, 8)
        LAMT = small(854, 8)
        DEC = small(862, 8).rearrange("p (t c) -> p t c", t=2)
        AMAX = small(870, 16).rearrange("p (h b) -> p h b", b=2)
        ASUM = small(886, 16).rearrange("p (h b) -> p h b", b=2)
        ASNK = small(902, 16).rearrange("p (h b) -> p h b", b=2)

        CTXR, HC = tiles3(0, 8), tiles3(8, 8)
        KQ = tiles3(16, 8)
        VX = tiles(24, 4).rearrange("p (t c) -> p t c", t=TT)
        KC = tiles(28, 4).rearrange("p (t h c) -> p t h c", t=TT, h=HEADS1)
        VC = tiles(32, 4).rearrange("p (t c) -> p t c", t=TT)
        G_, B_, C_, XI_ = tiles3(36, 4), tiles3(40, 4), tiles3(44, 4), tiles3(48, 4)
        KQR = tiles3(52, 8)
        DM_ = tiles(60, 8).rearrange("p (h m n) -> p h m n", h=HEADS1, m=TT)
        QFB = tiles3(68, 8)
        ROT = tiles(76, 4)
        KW = SQ[:, :, :].rearrange("p (s t x) n -> p s t (x n)", s=2, t=TT)
        SFB = tiles(76, 4).rearrange("p (s h c) -> p s h c", s=2, h=HEADS1)
        TW = tiles(28, 24).rearrange("p (h j) -> p h j", j=TPITCH)
        RELB = tiles(76, 4).rearrange("p (h j) -> p h j", h=AH)
        ADA = tiles(52, 2), tiles(4, 2), tiles(6, 2)
        Y, YC = tiles3(16, 4), tiles3(20, 4)
        MIX, MO = tiles3(8, 8), tiles3(28, 8)
        R4 = tiles3(52, 4)
        HT = tiles(0, 8).rearrange("p (t c) -> p t c", t=TT)
        XS = tiles(8, 17).rearrange("p (k j) -> p k j", k=KT)
        SEL = tiles(25, 4).rearrange("p (t j) -> p t j", t=TT)
        R16 = tiles(36, 2)
        AT = tiles(38, 1)
        XSE = tiles(39, 1).rearrange("p (k m) -> p k m", k=KT)
        SG, HID, HIDT = tiles(40, 2), tiles(42, 2), tiles(44, 2)
        YE = tiles(46, 4)
        SELT = tiles(50, 1)
        ZERO = tiles(51, 2)
        FO = tiles3(60, 8)

        RAW = tiles3(0, IN2)
        XC = tiles3(0, 8)
        TH, LY, Z, GATE = tiles3(13, 8), tiles3(21, 8), tiles3(29, 8), tiles3(37, 16)
        XBC = tiles3(53, 12)
        YA = tiles3(53, 8)
        DT, ADT, LCUM = tiles(65, 1), tiles(66, 1), tiles(67, 1)
        CBM = tiles(68, 3).rearrange("p (g l) -> p g l", g=2)
        SEG = tiles(71, 3).rearrange("p (b l) -> p b l", b=2)
        LMASK = tiles3(74, 2)
        I_OF = (8, 9, 10, 11, 76, 77, 78, 79)
        XDT = SQ[:, :, :].rearrange("p (t x) n -> p t (x n)", t=TT)
        DTT = small(924, 32).rearrange("p (t h) -> p t h", t=TT)
        LRU_T = tiles(12, 1)
        PA, PB, MO2 = tiles3(29, 8), tiles3(21, 8), tiles3(13, 8)
        UP, FV = tiles3(0, 48), tiles3(48, FT)
        DO = tiles3(0, 8)
        PU2 = 44
        MID2 = 35
        L_LRU, L_SSM, L_OUT2, L_UP, L_DOWN, L_EVEN, L_OE, L_ODD, L_OO = (
            sum(D2_LAYERS[:n]) for n in range(1, len(D2_LAYERS)))
        PU3 = PU2 + L_DOWN + 8 - L_EVEN
        ROUND = RING * UNITS
        SSD_LEN = 3 * P

        def units_through(unit):
            return MID2 + sum(not block_ends(u) and not (L_DOWN <= u < L_EVEN and (u - L_DOWN) % 3 < 2) for u in range(unit + 1))

        def d2_block(unit):
            return D2_BLOCK0 + unit // UNITS

        def tensor_dense2(pe, arrived, dense_unit, unit, act, pu, tokens_out=False, ready=None):
            pe.wait_ge(s.dense_sb, pu - 3)
            arrived(d2_block(unit))
            dense_unit(d2_block(unit), unit % UNITS, B[pu % 4], act, tokens_out, ready=ready).then_inc(
                s.ring_used if block_ends(unit) else s.dense_mm, 1)

        def tensor_loop2(pe, dense_unit, first, rounds, act, ready):
            with pe.Fori(0, rounds) as r:
                for j in range(ROUND):
                    unit = first + j
                    pe.wait_ge(s.dense_sb, r * ROUND + (PU2 + unit - 3))
                    blk = d2_block(unit)
                    pe.wait_ge(ring_loaded[blk % RING], r * 16 + uses(blk))
                    dense_unit(blk, unit % UNITS, B[(PU2 + unit) % 4], act, ready=None if j else ready).then_inc(
                        s.ring_used if block_ends(unit) else s.dense_mm, 1)

        def tensor_block2(pe, mm, arrived, dense_unit, column_sum, column_sums):
            def unit2(unit, act):
                tensor_dense2(pe, arrived, dense_unit, unit, act, PU2 + unit)

            column_sums(5)
            tensor_loop2(pe, dense_unit, 0, 2, H, (s.h_ready, 0))
            unit2(32, H), unit2(33, H)
            pe.wait_ge(s.xc_ready, 1)
            pe.wait_ge(s.lru_in, 16)
            for k in range(KT):
                if k >= 4:
                    pe.wait_ge(s.ri_sig, k - 3)
                for n in range(2):
                    last = mm(B[4 + k % 4][:, n * SEQ:(n + 1) * SEQ], lru_w[:, n, k, :], XC[:, k, :])
                last.then_inc(s.ri_mm, 1)
            unit2(34, H), unit2(35, H)
            pe.wait_ge(s.ri_sig, KT)
            pe.wait_ge(s.cs_ready, 1)
            for t in range(TT):
                nc.tensor.transpose(B[4][:, t * P:(t + 1) * P], LCUM[:, t * P:(t + 1) * P], ident)
                last = nc.tensor.transpose(B[5][:, t * P:(t + 1) * P], DT[:, t * P:(t + 1) * P], ident)
            last.then_inc(s.ssd_tr, 1)
            pe.wait_ge(s.xbc_silu, 1)
            for g in range(2):
                mm(B[6 + g][:, 0:SEQ], XBC[:, 8 + g, 0:P], XBC[:, 10 + g, :])
                mm(B[6 + g][:, SEQ:SSD_LEN], XBC[:, 8 + g, P:SEQ], XBC[:, 10 + g, P:SEQ]).then_inc(s.cb_mm, 1)
            unit2(36, H)
            pe.wait_ge(s.ssd_sb, 1)
            pe.wait_ge(s.cb_ready, 2)
            for n in range(4):
                for q in range(4):
                    t, k = n // 2, 4 * (n % 2) + q
                    last = nc.tensor.transpose(B[4 + n][:, q * P:(q + 1) * P], XBC[:, k, t * P:(t + 1) * P], ident)
                last.then_inc(s.xs_tr, 1)
            unit2(37, H)

            def spread_decay(h):
                pe.wait_ge(s.lmask_ready, h + 1)
                if h >= 2:
                    pe.wait_ge(s.seg_ready, h - 1)
                bank, lm = B[4 + h % 2], LMASK[:, h % 2, :]
                mm(bank[:, 0:SEQ], con("chunk_rows")[:, 0:P], lm)
                mm(bank[:, SEQ:SSD_LEN], con("chunk_rows")[:, P:2 * P], lm[:, P:SEQ]).then_inc(s.bc_mm, 1)

            pe.wait_ge(s.xdt_ready, 4)
            spread_decay(0)
            for h in range(SSM_H):
                if 38 + h < IN2:
                    unit2(38 + h, H)
                if h + 1 < SSM_H:
                    spread_decay(h + 1)
                pe.wait_ge(s.m_ready, h + 1)
                if h >= 4:
                    pe.wait_ge(s.ya_pair, h // 2 - 1)
                o = B[6 + h // 2 % 2][64 * (h % 2):64 * (h % 2) + 64, 0:SEQ]
                mm(o, XDT[:, 0, h * SSM_P:(h + 1) * SSM_P], SEG[:, h % 2, 0:SEQ], True, False)
                mm(o[:, P:SEQ], XDT[:, 1, h * SSM_P:(h + 1) * SSM_P], SEG[:, h % 2, SEQ:SSD_LEN],
                   False, True).then_inc(s.ssd_y, 1)
            pe.wait_ge(s.yb_ready, 1)
            for n in range(4):
                unit2(L_LRU + n, XC)
            pe.wait_ge(s.ya_sq, 1)
            for g in range(2):
                for k in range(4):
                    last = mm(B[4 + g][:, 0:SEQ], ones[:], SQ[:, 4 * g + k, :], k == 0, k == 3)
            last.then_inc(s.ya_sum, 1)
            for n in range(4, 8):
                unit2(L_LRU + n, XC)
            pe.wait_ge(s.ya_ready, 1)
            for n in range(8):
                unit2(L_SSM + n, YA)
            pe.wait_ge(s.mg_ready, 1)
            for n in range(8):
                unit2(L_OUT2 + n, PA)
                if n:
                    column_sum(6, n - 1)
            column_sum(6, KT - 1)
            column_sums(7)
            tensor_loop2(pe, dense_unit, L_UP, 3, H, (s.h_ready, KT))
            for n in range(KT):
                pu = PU2 + L_DOWN + n
                pe.wait_ge(s.dense_sb, pu - 3)
                for kg in range(3):
                    unit = L_DOWN + 3 * n + kg
                    arrived(d2_block(unit))
                    if n == 0:
                        pe.wait_ge(s.f_ready, kg + 1)
                    last = dense_unit(d2_block(unit), unit % UNITS, B[pu % 4], FV[:, KT * kg:KT * kg + KT, :],
                                      start=kg == 0, stop=kg == 2)
                    if block_ends(unit):
                        last.then_inc(s.ring_used, 1)
                    elif kg == 2:
                        last.then_inc(s.dense_mm, 1)
                if n:
                    column_sum(8, n - 1)
            column_sum(8, KT - 1)

        def scalar_loop2(act, fn, units_done, first, rounds):
            mids = units_done[0]
            with act.Fori(0, rounds) as r:
                n = 0
                for j in range(ROUND):
                    unit = first + j
                    if block_ends(unit):
                        act.wait_ge(s.ring_used, r * RING + (d2_block(unit) + 1))
                    else:
                        n += 1
                        act.wait_ge(s.dense_mm, r * (ROUND - RING) + (mids + n))
                    at = r * (ROUND * SEQ) + (unit - (0 if first == 0 else L_UP)) * SEQ
                    fn(U[:, bass.ds(at, SEQ)], B[(PU2 + unit) % 4][:, 0:SEQ], ACT.Copy).then_inc(s.dense_sb, 1)
            units_done[0] += rounds * (ROUND - RING)

        def scalar_block2(act, fn, link, square, squares_of_x, root, unit_done, units_done):
            def copy2(unit, dst, tile=None):
                unit_done(d2_block(unit), block_ends(unit))
                if tile is not None:
                    square(tile, B[(PU2 + unit) % 4][:, 0:SEQ])
                fn(dst, B[(PU2 + unit) % 4][:, 0:SEQ], ACT.Copy).then_inc(s.dense_sb, 1)

            def soft(x, t):
                link(fn(t, x, ACT.Abs))
                link(fn(t, t, ACT.Exp, scale=-1.0))
                return fn(t, t, ACT.Ln, bias=1.0)

            squares_of_x(s.x_ready, KT)
            root(5)
            scalar_loop2(act, fn, units_done, 0, 2)
            act.wait_ge(s.dt_in, 1)
            soft(DT, ADT).then_inc(s.dt_soft, 1)
            fn(NEGA, par("a_log"), ACT.Exp).then_inc(s.a_exp, 1)
            soft(par("lru_lam"), LAMT).then_inc(s.lam_soft, 1)
            act.wait_ge(s.xbc_conv, 1)
            fn(tiles(53, 12), tiles(53, 12), ACT.Silu).then_inc(s.xbc_silu, 1)
            for unit in (32, 33):
                copy2(unit, RAW[:, unit, :])
            for k in range(KT):
                act.wait_ge(s.ri_mm, k + 1)
                bank = B[4 + k % 4]
                fn(TH[:, k, :], bank[:, 0:SEQ], ACT.Sigmoid, bias=par("lru_br", k, k + 1))
                fn(tiles(I_OF[k], 1), bank[:, SEQ:2 * SEQ], ACT.Sigmoid, bias=par("lru_bi", k, k + 1)).then_inc(s.ri_sig, 1)
            act.wait_ge(s.lam_ready, 1)
            act.wait_ge(s.ri_sig, KT)
            for k in range(KT):
                last = fn(TH[:, k, :], TH[:, k, :], ACT.Tanh, scale=LAMC[:, k:k + 1])
            last.then_inc(s.th_ready, 1)
            for unit in (34, 35, 36):
                copy2(unit, RAW[:, unit, :])
            fn(tiles(21, 8), tiles(21, 8), ACT.Gelu_apprx_tanh).then_inc(s.ly_gelu, 1)
            act.wait_ge(s.dense_sb, PU2 + 37)
            fn(tiles(29, 8), tiles(29, 8), ACT.Silu).then_inc(s.z_silu, 1)
            copy2(37, RAW[:, 37, :])
            for h in range(SSM_H):
                act.wait_ge(s.seg_ready, h + 1)
                fn(SEG[:, h % 2, :], SEG[:, h % 2, :], ACT.Exp).then_inc(s.seg_exp, 1)
                if 38 + h < IN2:
                    copy2(38 + h, RAW[:, 38 + h, :])
                if h % 2:
                    act.wait_ge(s.lru_neg, h // 2 + 1)
                    fn(XC[:, h // 2, :], XC[:, h // 2, :], ACT.Sqrt).then_inc(s.lru_root, 1)
            act.wait_ge(s.dense_sb, PU2 + IN2)
            for k in range(16):
                last = fn(GATE[:, k, :], GATE[:, k, :], ACT.Sigmoid, bias=par("gate_b", k, k + 1))
            last.then_inc(s.g_sig, 1)
            for n in range(4):
                copy2(L_LRU + n, PB[:, n, :])
            act.wait_ge(s.ya_gated, 1)
            fn(flat(SQ), tiles(53, 8), ACT.Square).then_inc(s.ya_sq, 1)
            act.wait_ge(s.ya_inv, 1)
            fn(flat(RS), flat(RS), ACT.Sqrt).then_inc(s.ya_rstd, 1)
            for n in range(4, 8):
                copy2(L_LRU + n, PB[:, n, :])
            for n in range(8):
                copy2(L_SSM + n, PA[:, n, :])
            for n in range(8):
                copy2(L_OUT2 + n, MO2[:, n, :], tile=n)
            root(6)
            squares_of_x(s.x_ready, 2 * KT)
            root(7)
            scalar_loop2(act, fn, units_done, L_UP, 3)
            for c in range(3):
                act.wait_ge(s.conv_step, 48 * (c + 1))
                fn(tiles(48 + 8 * c, 8), tiles(48 + 8 * c, 8), ACT.Gelu_apprx_tanh).then_inc(s.ffn_gelu, 1)
            act.wait_ge(s.f_ready, 3)
            for n in range(KT):
                unit = L_DOWN + 3 * n + 2
                unit_done(d2_block(unit), block_ends(unit))
                square(n, B[(PU2 + L_DOWN + n) % 4][:, 0:SEQ])
                fn(DO[:, n, :], B[(PU2 + L_DOWN + n) % 4][:, 0:SEQ], ACT.Copy).then_inc(s.dense_sb, 1)
            root(8)

        def vector_block2(dve, v, link, norm_invert, norm_to, add_normed):
            norm_invert(5)
            norm_to(H, X, par("mix_pre"), s.h_ready)

            def conv(n, out_t, src_t, w, b):
                w = par(w, 4 * n, 4 * n + 4)
                dve.wait_ge(s.dense_sb, PU2 + src_t + 1)
                return conv_taps(dve, nc, link, tiles(out_t, 1), tiles(src_t, 1), w, par(b, n, n + 1), 4)

            for n in range(12):
                last = conv(n, 53 + n, n, "ssm_conv_w", "ssm_conv_b")
            last.then_inc(s.xbc_conv, 1)
            dve.wait_ge(s.dense_sb, PU2 + 13)
            v.tensor_scalar(DT, tiles(12, 1), par("dt_bias"), None, ALU.add).then_inc(s.dt_in, 1)
            for n in range(KT):
                last = conv(n, n, 13 + n, "lru_conv_w", "lru_conv_b")
            last.then_inc(s.xc_ready, 1)
            dve.wait_ge(s.dt_soft, 1)
            dve.wait_ge(s.dt_in, 1)
            link(v.scalar_tensor_tensor(out=DT, in0=DT, scalar=0.0, in1=ADT, op0=ALU.max, op1=ALU.add))
            dve.wait_ge(s.a_exp, 1)
            link(v.tensor_scalar(ADT, DT, NEGA, -1.0, ALU.mult, ALU.mult))
            link(v.tensor_tensor_scan(LCUM, con("ssd_reset"), ADT, 0.0, ALU.mult, ALU.add))
            for c in range(4):
                r, a, b = slice(32 * c, 32 * c + 32), CHUNK * c, CHUNK * (c + 1)
                link(v.tensor_copy(TOT[r, :], LCUM[r, b - 1:b]))
                last = v.tensor_scalar(LCUM[r, a:b], LCUM[r, a:b], TOT[r, :], None, ALU.subtract)
            last.then_inc(s.cs_ready, 1)
            dve.wait_ge(s.lam_soft, 1)
            link(v.tensor_scalar(LAMC, par("lru_lam"), -1.0, 0.0, ALU.mult, ALU.max))
            link(v.tensor_tensor(LAMC, LAMC, LAMT, ALU.add))
            v.tensor_scalar(LAMC, LAMC, -4.0, None, ALU.mult).then_inc(s.lam_ready, 1)
            dve.wait_ge(s.ssd_tr, 1)
            for t in range(TT):
                for half in range(2):
                    r, at = slice(64 * half, 64 * half + 64), P * t + 64 * t + 32 * half
                    v.tensor_copy(LSH[r, t, :], B[4][r, at:at + SSM_H])
                last = v.tensor_copy(DTT[:, t, :], B[5][:, t * P:t * P + SSM_H])
            last.then_inc(s.ssd_sb, 1)
            dve.wait_ge(s.cs_ready, 1)
            for h in range(2):
                v.tensor_scalar(LMASK[:, h, :], LCUM, con("head_rows")[:, h:h + 1], None, ALU.mult).then_inc(s.lmask_ready, 1)
            for g in range(2):
                dve.wait_ge(s.cb_mm, g + 1)
                v.tensor_tensor(CBM[:, g, :], B[6 + g][:, 0:SSD_LEN], con("causal"), ALU.mult).then_inc(s.cb_ready, 1)
            dve.wait_ge(s.ssd_sb, 1)
            for n in range(4):
                t, part = n // 2, n % 2
                dve.wait_ge(s.xs_tr, n + 1)
                v.tensor_tensor(XDT[:, t, part * 512:(part + 1) * 512].rearrange("p (h c) -> p h c", h=8),
                                B[4 + n][:].rearrange("p (h c) -> p h c", h=8),
                                spread(DTT[:, t, 8 * part:8 * part + 8], 2, SSM_P), ALU.mult).then_inc(s.xdt_ready, 1)

            def segments(h):
                dve.wait_ge(s.bc_mm, h + 1)
                if h >= 2:
                    dve.wait_ge(s.ssd_y, h - 1)
                bank, seg = B[4 + h % 2], SEG[:, h % 2, :]
                v.tensor_scalar(seg[:, 0:SEQ], bank[:, 0:SEQ], LSH[:, 0, h:h + 1], 0.0, ALU.subtract, ALU.min)
                v.tensor_scalar(seg[:, SEQ:SSD_LEN], bank[:, SEQ:SSD_LEN], LSH[:, 1, h:h + 1], 0.0,
                                ALU.subtract, ALU.min).then_inc(s.seg_ready, 1)

            def lru_tile(k):
                i, th, t1 = tiles(I_OF[k], 1), TH[:, k, :], LRU_T
                if k == 0:
                    dve.wait_ge(s.th_ready, 1)
                    dve.wait_ge(s.ri_sig, KT)
                    dve.wait_ge(s.ly_gelu, 1)
                v.tensor_tensor(i, i, XC[:, k, :], ALU.mult)
                link(v.tensor_scalar(t1, th, -1.0, 1.0, ALU.mult, ALU.add))
                link(v.reciprocal(t1, t1))
                link(v.tensor_tensor(i, i, t1, ALU.mult))
                v.tensor_scalar(XC[:, k, :], th, -4.0, None, ALU.mult).then_inc(s.lru_neg, 1)
                link(v.scalar_tensor_tensor(out=th, in0=th, scalar=1.0, in1=t1, op0=ALU.add, op1=ALU.mult))
                dve.wait_ge(s.lru_root, k + 1)
                link(v.tensor_tensor(i, i, XC[:, k, :], ALU.mult))
                link(v.tensor_tensor_scan(XC[:, k, :], th, i, 0.0, ALU.mult, ALU.add))
                return v.tensor_tensor(XC[:, k, :], XC[:, k, :], LY[:, k, :], ALU.mult)

            def pair_out(n):
                dve.wait_ge(s.ssd_y, 2 * n + 2)
                v.scalar_tensor_tensor(out=YA[:, n, :], in0=YA[:, n, :], scalar=par("ssm_d", n, n + 1),
                                       in1=B[6 + n % 2][:, 0:SEQ], op0=ALU.mult, op1=ALU.add).then_inc(s.ya_pair, 1)

            segments(0)
            for h in range(SSM_H):
                if h + 1 < SSM_H:
                    segments(h + 1)
                if h + 2 < SSM_H:
                    dve.wait_ge(s.bc_mm, h + 1)
                    v.tensor_scalar(LMASK[:, h % 2, :], LCUM, con("head_rows")[:, h + 2:h + 3], None,
                                    ALU.mult).then_inc(s.lmask_ready, 1)
                dve.wait_ge(s.seg_exp, h + 1)
                v.tensor_tensor(SEG[:, h % 2, :], SEG[:, h % 2, :], CBM[:, h // 8, :], ALU.mult).then_inc(s.m_ready, 1)
                if h % 2:
                    last = lru_tile(h // 2)
                    if h >= 3:
                        pair_out(h // 2 - 1)
            last.then_inc(s.yb_ready, 1)
            pair_out(7)
            dve.wait_ge(s.ya_pair, 8)
            dve.wait_ge(s.z_silu, 1)
            v.tensor_tensor(YA, YA, Z, ALU.mult).then_inc(s.ya_gated, 1)
            dve.wait_ge(s.ya_sum, 1)
            for g in range(2):
                link(v.tensor_scalar(RS[:, g, :], B[4 + g][:, 0:SEQ], 1.0 / 512, EPS, ALU.mult, ALU.add))
            v.reciprocal(flat(RS), flat(RS)).then_inc(s.ya_inv, 1)
            dve.wait_ge(s.ya_gated, 1)
            dve.wait_ge(s.ya_rstd, 1)
            for k in range(KT):
                last = v.scalar_tensor_tensor(out=YA[:, k, :], in0=YA[:, k, :], scalar=par("ssm_norm", k, k + 1),
                                              in1=RS[:, k // 4, :], op0=ALU.mult, op1=ALU.mult)
            last.then_inc(s.ya_ready, 1)
            dve.wait_ge(s.g_sig, 1)
            dve.wait_ge(s.dense_sb, PU2 + L_SSM)
            link(v.tensor_tensor(PB, PB, GATE[:, 8:16, :], ALU.mult))
            dve.wait_ge(s.dense_sb, PU2 + L_OUT2)
            link(v.tensor_tensor(PA, PA, GATE[:, 0:8, :], ALU.mult))
            v.tensor_tensor(PA, PA, PB, ALU.add).then_inc(s.mg_ready, 1)
            norm_invert(6)
            dve.wait_ge(s.dense_sb, PU2 + L_UP)
            add_normed(MO2, par("mix_post"))
            norm_invert(7)
            norm_to(H, X, par("ffn_pre"), s.h_ready)
            w_at, b_at = P_AT["ffn_conv_w"][0], P_AT["ffn_conv_b"][0]
            with dve.Fori(0, 3) as r:
                for j in range(8):
                    dve.wait_ge(s.dense_sb, r * ROUND + (PU2 + L_UP + 2 * j + 2))
                    gate = U[:, bass.ds(r * (ROUND * SEQ) + 2 * j * SEQ, SEQ)]
                    value = U[:, bass.ds(r * (ROUND * SEQ) + (2 * j + 1) * SEQ, SEQ)]
                    conved = U[:, bass.ds(r * (8 * SEQ) + (48 + j) * SEQ, SEQ)]
                    for n, (o, src) in enumerate(((conved, gate), (gate, value))):
                        def w(tap):
                            return params[:, bass.ds(r * 48 + (w_at + 6 * j + 3 * n + tap), 1)]

                        step = 6 * j + 3 * n
                        if n:
                            dve.wait_ge(s.conv_step, r * 48 + step)
                        v.tensor_scalar(o, src, w(2), params[:, bass.ds(r * 16 + (b_at + 2 * j + n), 1)],
                                        ALU.mult, ALU.add).then_inc(s.conv_step, 1)
                        for shift in (1, 2):
                            dve.wait_ge(s.conv_step, r * 48 + (step + shift))
                            v.scalar_tensor_tensor(out=o[:, shift:SEQ], in0=src[:, 0:SEQ - shift], scalar=w(2 - shift),
                                                   in1=o[:, shift:SEQ], op0=ALU.mult, op1=ALU.add).then_inc(s.conv_step, 1)
            values = tiles(0, 48).rearrange("p (n a t) -> p n a t", a=2, t=SEQ)[:, :, 0, :]
            for c in range(3):
                dve.wait_ge(s.ffn_gelu, c + 1)
                v.tensor_tensor(FV[:, 8 * c:8 * c + 8, :], FV[:, 8 * c:8 * c + 8, :], values[:, 8 * c:8 * c + 8, :],
                                ALU.mult).then_inc(s.f_ready, 1)
            norm_invert(8)
            dve.wait_ge(s.dense_sb, PU2 + L_DOWN + KT)
            add_normed(DO, par("ffn_post"))

        DOWNR, AQ, AK, BQ, BK = tiles(0, 1), tiles3(1, 2), tiles3(3, 2), tiles3(5, 4), tiles(9, 1)
        BV = tiles(10, 1).rearrange("p (t c) -> p t c", t=TT)
        AV = tiles(11, 4).rearrange("p (t c) -> p t c", t=TT)
        AG, BG = tiles3(15, 4), tiles3(19, 4)
        EIN = tiles3(15, 8)
        LSG, SOFT, CUM = tiles3(23, 2), tiles3(25, 2), tiles3(27, 2)
        EXPB = tiles3(29, 2)
        QH = tiles3(31, 4)
        KE, KP = tiles3(35, 2), tiles3(37, 2)
        KPT = tiles(39, 4).rearrange("p (a t c) -> p a t c", a=2, t=TT)
        ATT = tiles(43, 4).rearrange("p (h t c) -> p h t c", h=4, t=TT)
        STATE = tiles(47, 3).rearrange("p (c n e) -> p c n e", c=3, n=2)
        GO, GR = tiles3(50, 4), tiles3(23, 4)
        LOG = tiles(56, 12).rearrange("p (h j) -> p h j", j=TPITCH)
        BIAS = tiles(68, 12).rearrange("p (h j) -> p h j", j=TPITCH)
        BQH = SQ
        CQ, CK, CG = tiles3(0, 8), tiles3(8, 2), tiles3(12, 8)
        CV = tiles(10, 2).rearrange("p (t c) -> p t c", t=TT)
        OIN = CG
        NCH = SEQ // CHUNK

        def bias_block(kind):
            toep = d["toep"]
            return [bass.AP(toep.tensor, kind * AH * P * TPITCH + first + P - 1,
                            [[TPITCH - 1, P], [P * TPITCH, AH], [1, n]]) for first, n in ((P, P), (0, 2 * P))]

        def side_block3(pool):
            pool.wait_ge(s.toep_stored, 16)
            for kind in range(2):
                if kind == 0:
                    pool.wait_ge(s.x_ready, 4 * KT)
                else:
                    pool.wait_ge(s.lg_sb, AH)
                first, second = bias_block(kind)
                pool.dma_start(BIAS[:, :, 0:P], first).then_inc(s.bias_in, 16)
                pool.dma_start(BIAS[:, :, P:3 * P], second).then_inc(s.bias_in, 16)

        def tensor_block3(pe, mm, arrived, dense_unit, column_sum, column_sums):
            def unit3(unit, act, tokens_out=False, ready=None):
                tensor_dense2(pe, arrived, dense_unit, unit, act, PU3 + unit, tokens_out, ready)

            column_sums(9)
            def logits(kind, q_of, k_of, heads):
                for h in heads:
                    if h >= 4:
                        pe.wait_ge(s.lg_sb, AH * kind + h - 3)
                    q, k, bank = q_of(h), k_of(h), B[4 + h % 4]
                    mm(bank[:, 0:P], q[:, 0:P], k[:, 0:P])
                    mm(bank[:, P:3 * P], q[:, P:SEQ], k).then_inc(s.lg_mm, 1)

            def turn_probs(kind, heads):
                pe.wait_ge(s.lg_ready, kind + 1)
                for h in heads:
                    if h >= 4:
                        pe.wait_ge(s.pt_sb, AH * kind + h - 3)
                    for j in range(3):
                        last = nc.tensor.transpose(B[4 + h % 4][:, j * P:(j + 1) * P], LOG[:, h, j * P:(j + 1) * P], ident)
                    last.then_inc(s.pt_tr, 1)

            def times_values(kind, v_of, heads_of_tile):
                pe.wait_ge(s.pt_sb, AH * (kind + 1))
                for n, heads in enumerate(heads_of_tile):
                    if n >= 4:
                        pe.wait_ge(s.ao_ready, 4 * kind + n - 3)
                    rows = P // len(heads)
                    for i, h in enumerate(heads):
                        o = B[4 + n % 4][rows * i:rows * (i + 1), 0:SEQ]
                        mm(o[:, 0:P], v_of(h, 0), LOG[:, h, 0:P], True, False)
                        mm(o[:, P:SEQ], v_of(h, 0), LOG[:, h, P:2 * P], False, False)
                        last = mm(o[:, P:SEQ], v_of(h, 1), LOG[:, h, 2 * P:3 * P], False, True)
                    last.then_inc(s.ao_mm, 1)

            def even(*units):
                for n in units:
                    unit3(L_EVEN + n, H, 10 <= n < 15, None if n else (s.h_ready, 2 * KT))

            even(0, 1)
            pe.wait_ge(s.dense_sb, PU3 + L_EVEN + 1)
            up = par("gla_w_up")
            for n in range(2):
                last = mm(B[4][:, n * SEQ:(n + 1) * SEQ], up[0:16, n * P:(n + 1) * P], DOWNR[0:16, :])
            last.then_inc(s.gl_mm, 1)
            even(2, 3, 4, 5, 6, 7, 8, 9, 10)
            pe.wait_ge(s.kp_ready, 1)
            for t in range(TT):
                for n in range(2):
                    last = nc.tensor.transpose(B[5][:, t * SEQ + n * P:t * SEQ + (n + 1) * P], KP[:, n, t * P:(t + 1) * P], ident)
            last.then_inc(s.kp_tr, 1)
            for h in range(4):
                for t in range(TT):
                    last = mm(B[6 + h // 2][:, (h % 2) * SEQ + t * P:(h % 2) * SEQ + (t + 1) * P],
                              KE[:, h // 2, t * P:(t + 1) * P], QH[:, h, t * P:(t + 1) * P])
                if h % 2:
                    last.then_inc(s.att_mm, 1)
            even(11, 12)
            window = 0, lambda h: BQH[:, h, :], lambda h: BK
            pe.wait_ge(s.kpt_ready, 2)
            pe.wait_ge(s.att_ready, 2)
            pe.wait_ge(s.dense_sb, PU3 + L_EVEN + 10)
            pe.wait_ge(s.bqh_ready, 1)
            logits(*window, range(4))
            even(13)
            logits(*window, range(4, AH))
            even(14)
            pe.wait_ge(s.lg_sb, AH)
            pe.wait_ge(s.dense_sb, PU3 + L_EVEN + 15)
            for c in range(NCH - 1):
                for n in range(2):
                    last = mm(B[4 + c][:, n * SEQ:(n + 1) * SEQ], KPT[:, c % 2, c // 2, n * P:(n + 1) * P],
                              AV[:, c // 2, n * SEQ:(n + 1) * SEQ])
                last.then_inc(s.kv_mm, 1)
            even(15, 16)
            pe.wait_ge(s.st_ready, 1)
            for h in range(4):
                o = B[4 + h]
                for t in range(TT):
                    mm(o[:, t * P:(t + 1) * P], AV[:, t, h * P:(h + 1) * P], ATT[:, h, t, :], t == 0, False)
                for c in range(1, NCH):
                    last = mm(o[:, c * CHUNK:(c + 1) * CHUNK], STATE[:, c - 1, h // 2, :], QH[:, h, c * CHUNK:(c + 1) * CHUNK],
                              False, c == NCH - 1)
                last.then_inc(s.o_mm, 1)
            even(17, 18)
            pe.wait_ge(s.o_sq, 4)
            pe.wait_ge(s.o_sb, 4)
            for n in range(2):
                mm(B[4 + n][:], ones[:], tiles(43 + 2 * n, 2)).then_inc(s.o_sum, 1)
            even(19)
            pe.wait_ge(s.oa_var, 1)
            turn_probs(0, range(4))
            even(20)
            turn_probs(0, range(4, AH))
            even(21, 22)
            times_values(0, lambda h, t: BV[:, t, 64 * (h // 4):64 * (h // 4) + 64], [(n, n + 4) for n in range(4)])
            pe.wait_ge(s.oa_ready, 1)
            pe.wait_ge(s.ao_ready, 4)
            for n in range(8):
                unit3(L_OE + n, EIN)
                if n > 1:
                    column_sum(10, n - 2)
            column_sum(10, KT - 2)
            column_sum(10, KT - 1)

            def odd(*units):
                for n in units:
                    unit3(L_ODD + n, H, 10 <= n < 12, None if n else (s.h_ready, 3 * KT))

            causal = 1, lambda h: CQ[:, h, :], lambda h: CK[:, h // 4, :]
            odd(*range(10))
            pe.wait_ge(s.dense_sb, PU3 + L_ODD + 10)
            logits(*causal, range(4))
            odd(10)
            logits(*causal, range(4, AH))
            odd(*range(11, 17))
            turn_probs(1, range(4))
            odd(17)
            turn_probs(1, range(4, AH))
            odd(18, 19)
            times_values(1, lambda h, t: CV[:, t, P * (h // 4):P * (h // 4) + P], [(n,) for n in range(AH)])
            pe.wait_ge(s.ao_ready, 12)
            for n in range(8):
                unit3(L_OO + n, OIN)
                if n > 1:
                    column_sum(11, n - 2)
            column_sum(11, KT - 2)
            column_sum(11, KT - 1)

        def scalar_block3(act, fn, link, squares_of_x, root, unit_done, units_done):
            def copy3(unit, dst, tokens_out=False):
                unit_done(d2_block(unit), block_ends(unit))
                src = B[(PU3 + unit) % 4][:, 0:SEQ]
                fn(dst, src.rearrange("p (t c) -> p t c", t=TT) if tokens_out else src, ACT.Copy).then_inc(s.dense_sb, 1)

            squares_of_x(s.x_ready, 3 * KT)
            root(9)
            def even(*units):
                for n in units:
                    unit_to = (tiles(n, 1) if n < 10 or n >= 15 else BV if n == 10 else AV[:, :, (n - 11) * P:(n - 10) * P])
                    copy3(L_EVEN + n, unit_to, 10 <= n < 15)

            def exp_scores(kind):
                act.wait_ge(s.lg_shift, kind + 1)
                if kind == 0:
                    fn(ASNK, ASNK, ACT.Exp)
                fn(tiles(56, 12), tiles(56, 12), ACT.Exp).then_inc(s.lg_exp, 1)

            def copy_probs(kind, heads):
                for h in heads:
                    act.wait_ge(s.pt_tr, AH * kind + h + 1)
                    fn(LOG[:, h, :], B[4 + h % 4][:, 0:3 * P], ACT.Copy).then_inc(s.pt_sb, 1)

            flat2 = lambda a: tiles(a, 2)
            even(0, 1)
            act.wait_ge(s.gl_in, 1)
            link(fn(flat2(25), flat2(23), ACT.Abs))
            link(fn(flat2(25), flat2(25), ACT.Exp, scale=-1.0))
            fn(flat2(25), flat2(25), ACT.Ln, bias=1.0).then_inc(s.gl_soft, 1)
            even(2, 3)
            act.wait_ge(s.gl_b, 1)
            fn(flat2(29), flat2(27), ACT.Exp).then_inc(s.gl_exp, 1)
            fn(flat2(35), flat2(27), ACT.Exp, scale=-1.0).then_inc(s.gl_exp, 1)
            fn(DEC, CUM.rearrange("p n (c t) -> p n c t", t=CHUNK)[:, :, :, CHUNK - 1], ACT.Exp).then_inc(s.gl_exp, 1)
            act.wait_ge(s.gl_left, 1)
            fn(flat2(37), flat2(37), ACT.Exp).then_inc(s.gl_exp, 1)
            even(*range(4, 17))
            exp_scores(0)
            for h in range(4):
                act.wait_ge(s.o_mm, h + 1)
                fn(tiles(43 + h, 1), B[4 + h][:, 0:SEQ], ACT.Square).then_inc(s.o_sq, 1)
                fn(GO[:, h, :], B[4 + h][:, 0:SEQ], ACT.Copy).then_inc(s.o_sb, 1)
            even(17, 18)
            act.wait_ge(s.dense_sb, PU3 + L_EVEN + 19)
            fn(tiles(15, 4), tiles(15, 4), ACT.Silu).then_inc(s.eg_silu, 1)
            act.wait_ge(s.oa_var, 1)
            fn(tiles(23, 4), tiles(23, 4), ACT.Sqrt).then_inc(s.o_rstd, 1)
            even(19)
            copy_probs(0, range(4))
            even(20)
            copy_probs(0, range(4, AH))
            even(21, 22)
            act.wait_ge(s.dense_sb, PU3 + L_EVEN + 23)
            fn(tiles(19, 4), tiles(19, 4), ACT.Silu).then_inc(s.eg_silu, 1)
            units_done[0] = units_through(L_ODD - 1)
            squares_of_x(s.dense_sb, PU3 + L_OE)
            root(10)
            def odd(*units):
                for n in units:
                    copy3(L_ODD + n, CV[:, :, (n - 10) * P:(n - 9) * P] if 10 <= n < 12 else tiles(n, 1), 10 <= n < 12)

            def silu_odd(a):
                act.wait_ge(s.dense_sb, PU3 + L_ODD + a + 4)
                fn(tiles(a, 4), tiles(a, 4), ACT.Silu).then_inc(s.eg_silu, 1)

            odd(*range(14))
            exp_scores(1)
            odd(14, 15, 16)
            silu_odd(12)
            copy_probs(1, range(4))
            odd(17)
            copy_probs(1, range(4, AH))
            odd(18, 19)
            silu_odd(16)
            squares_of_x(s.dense_sb, PU3 + L_OO)
            root(11)

        def vector_block3(dve, v, link, norm_invert, norm_to):
            def add_unit(unit, n):
                if block_ends(unit):
                    dve.wait_ge(s.ring_used, d2_block(unit) + 1)
                else:
                    dve.wait_ge(s.dense_mm, units_through(unit))
                v.tensor_tensor(X[:, n, :], X[:, n, :], B[(PU3 + unit) % 4][:, 0:SEQ], ALU.add).then_inc(s.dense_sb, 1)

            norm_invert(9)
            norm_to(H, X, par("norm_gain", 0, 8), s.h_ready)
            dve.wait_ge(s.gl_mm, 1)
            for n in range(2):
                last = v.tensor_scalar(LSG[:, n, :], B[4][:, n * SEQ:(n + 1) * SEQ], par("gla_b_up", n, n + 1), None, ALU.add)
            last.then_inc(s.gl_in, 1)
            dve.wait_ge(s.gl_soft, 1)
            dve.wait_ge(s.gl_in, 1)
            link(v.scalar_tensor_tensor(out=LSG, in0=LSG, scalar=0.0, in1=SOFT, op0=ALU.min, op1=ALU.subtract))
            link(v.tensor_scalar(LSG, LSG, 1.0 / 16.0, None, ALU.mult))
            for n in range(2):
                last = v.tensor_tensor_scan(CUM[:, n, :], con("gla_reset"), LSG[:, n, :], 0.0, ALU.mult, ALU.add)
            last.then_inc(s.gl_b, 1)
            dve.wait_ge(s.gl_b, 1)
            by_chunk = lambda ap: ap.rearrange("p n (c t) -> p (n c) t", t=CHUNK)
            cum = by_chunk(CUM)
            v.tensor_tensor(by_chunk(KP), spread(cum[:, :, CHUNK - 1], 2, CHUNK), cum, ALU.subtract).then_inc(s.gl_left, 1)
            dve.wait_ge(s.gl_exp, 2)
            dve.wait_ge(s.dense_sb, PU3 + L_EVEN + 5)
            link(v.scalar_tensor_tensor(out=EXPB, in0=AQ, scalar=float(64) ** -0.5, in1=EXPB, op0=ALU.mult, op1=ALU.mult))
            for h in range(4):
                v.tensor_scalar(QH[:, h, :], EXPB[:, h // 2, :], con("half")[:, h % 2:h % 2 + 1], None, ALU.mult)
            v.tensor_tensor(KE, KE, AK, ALU.mult)
            dve.wait_ge(s.gl_exp, 4)
            v.tensor_tensor(KP, KP, AK, ALU.mult).then_inc(s.kp_ready, 1)
            dve.wait_ge(s.dense_sb, PU3 + L_EVEN + 9)
            for h in range(AH):
                last = v.tensor_scalar(BQH[:, h, :], BQ[:, h % 4, :], con("half")[:, h // 4:h // 4 + 1], None, ALU.mult)
            last.then_inc(s.bqh_ready, 1)
            dve.wait_ge(s.kp_tr, 1)
            for a in range(2):
                v.tensor_scalar(KPT[:, a].rearrange("p t c -> p (t c)"), B[5][:], con("half")[:, a:a + 1], None,
                                ALU.mult).then_inc(s.kpt_ready, 1)
            mask = spread(spread(con("gla_mask"), 1, TT), 1, 2)
            for n in range(2):
                dve.wait_ge(s.att_mm, n + 1)
                a = ATT[:, 2 * n:2 * n + 2]
                link(v.tensor_scalar(a.rearrange("p h t c -> p (h t c)"), B[6 + n][:], 3e38, -3e38, ALU.min, ALU.max))
                v.tensor_tensor(a, a, mask, ALU.mult).then_inc(s.att_ready, 1)
            parts = LOG[:, :, 0:P], LOG[:, :, P:3 * P]

            def shift_scores(kind, scale):
                dve.wait_ge(s.bias_in, 32 * (kind + 1))
                for h in range(AH):
                    dve.wait_ge(s.lg_mm, AH * kind + h + 1)
                    v.scalar_tensor_tensor(out=LOG[:, h, :], in0=B[4 + h % 4][:, 0:3 * P], scalar=scale, in1=BIAS[:, h, :],
                                           op0=ALU.mult, op1=ALU.add).then_inc(s.lg_sb, 1)
                dve.wait_ge(s.lg_sb, AH * (kind + 1))
                for b in range(2):
                    last = v.tensor_reduce(AMAX[:, :, b], parts[b], AXX, ALU.max)
                link(last)
                if kind == 0:
                    sinks = spread(par("sinks"), 2, 2)
                    link(v.tensor_tensor(AMAX, AMAX, sinks, ALU.max))
                    v.tensor_tensor(ASNK, sinks, AMAX, ALU.subtract)
                for b in range(2):
                    last = v.tensor_tensor(parts[b], parts[b], spread(AMAX[:, :, b], 2, (b + 1) * P), ALU.subtract)
                last.then_inc(s.lg_shift, 1)

            def normalise(kind):
                dve.wait_ge(s.lg_exp, kind + 1)
                for b in range(2):
                    last = v.tensor_reduce(ASUM[:, :, b], parts[b], AXX, ALU.add)
                link(last)
                if kind == 0:
                    link(v.tensor_tensor(ASUM, ASUM, ASNK, ALU.add))
                link(v.reciprocal(ASUM, ASUM))
                for b in range(2):
                    last = v.tensor_tensor(parts[b], parts[b], spread(ASUM[:, :, b], 2, (b + 1) * P), ALU.mult)
                last.then_inc(s.lg_ready, 1)

            shift_scores(0, float(64) ** -0.5)
            for c in range(NCH - 1):
                dve.wait_ge(s.kv_mm, c + 1)
                for n in range(2):
                    for half in range(2):
                        r = slice(64 * half, 64 * half + 64)
                        own = B[4 + c][r, n * SEQ + half * P:n * SEQ + (half + 1) * P]
                        if c == 0:
                            last = v.tensor_copy(STATE[r, 0, n, :], own)
                        else:
                            last = v.scalar_tensor_tensor(out=STATE[r, c, n, :], in0=STATE[r, c - 1, n, :],
                                                          scalar=DEC[r, n, c:c + 1], in1=own, op0=ALU.mult, op1=ALU.add)
                if c < NCH - 2:
                    link(last)
            last.then_inc(s.st_ready, 1)
            normalise(0)
            for n in range(2):
                dve.wait_ge(s.o_sum, n + 1)
                link(v.tensor_scalar(tiles(23 + 2 * n, 2), B[4 + n][:], 1.0 / P, EPS, ALU.mult, ALU.add))
            v.reciprocal(tiles(23, 4), tiles(23, 4)).then_inc(s.oa_var, 1)
            dve.wait_ge(s.o_rstd, 1)
            dve.wait_ge(s.eg_silu, 1)
            link(v.scalar_tensor_tensor(out=GO, in0=GO, scalar=par("gla_gain"), in1=GR, op0=ALU.mult, op1=ALU.mult))
            v.tensor_tensor(AG, GO, AG, ALU.mult).then_inc(s.oa_ready, 1)

            dve.wait_ge(s.eg_silu, 2)
            for n in range(4):
                dve.wait_ge(s.ao_mm, n + 1)
                v.tensor_tensor(BG[:, n, :], B[4 + n][:, 0:SEQ], BG[:, n, :], ALU.mult).then_inc(s.ao_ready, 1)
            for n in range(8):
                add_unit(L_OE + n, n)
            norm_invert(10)
            norm_to(H, X, par("norm_gain", 8, 16), s.h_ready)
            shift_scores(1, float(P) ** -0.5)
            normalise(1)
            for n in range(AH):
                dve.wait_ge(s.eg_silu, 3 + n // 4)
                dve.wait_ge(s.ao_mm, 4 + n + 1)
                v.tensor_tensor(CG[:, n, :], B[4 + n % 4][:, 0:SEQ], CG[:, n, :], ALU.mult).then_inc(s.ao_ready, 1)
            for n in range(8):
                add_unit(L_OO + n, n)
            norm_invert(11)
            norm_to(X, X, par("final_gain"), s.out_ready)

        block = ctx.enter_context(nc.Block())

        @block.sync
        def _(sp):
            def load(block_no, src, wait=True):
                if wait and block_no >= RING:
                    sp.wait_ge(s.ring_used, block_no - RING + 1)
                sp.dma_start(ring[:, block_no % RING, :].rearrange("p (a n) -> p a n", a=src.shape[1]),
                             src).then_inc(ring_loaded[block_no % RING], 16)

            ada = d["w_ada"].rearrange("(k p) n -> p k n", p=P)
            for at, (kind, b) in enumerate(FIRST):
                r, k = b // 4, 2 * (b % 4)
                load(at, ada[:, k:k + 2, r * DEXP:(r + 1) * DEXP] if kind == "ada"
                     else d["dense1"][b].rearrange("p (a n) -> p a n", a=1))
            rows = EXPERTS * DM
            gate = d["w_gate"].rearrange("(k p) n -> p k n", p=P)
            up = d["w_up"].rearrange("(k p) n -> p k n", p=P)
            down = d["w_down"].rearrange("(e j c p) n -> e c p j n", e=EXPERTS, j=4, c=4)
            with sp.Fori(0, EXPERTS) as e:
                for b in range(EXP_BLOCKS):
                    sp.wait_ge(s.ring_used, e * EXP_BLOCKS + (EXP_BLOCK0 + b - RING + 1))
                    if b < 4:
                        src = gate[:, bass.ds(e * KT + 2 * b, 2), :]
                    elif b < 8:
                        src = up[:, bass.ds(e * KT + 2 * (b - 4), 2), :]
                    else:
                        src = down[bass.ds(e, 1), b - 8].rearrange("e p j n -> p (e j) n")
                    slot = (EXP_BLOCK0 + b) % RING
                    sp.dma_start(ring[:, slot, :].rearrange("p (a n) -> p a n", a=src.shape[1]),
                                 src).then_inc(ring_loaded[slot], 16)
            with sp.Fori(0, D2_BLOCKS // RING) as r:
                for b in range(RING):
                    sp.wait_ge(s.ring_used, r * RING + (D2_BLOCK0 + b - RING + 1))
                    slot = (D2_BLOCK0 + b) % RING
                    sp.dma_start(ring[:, slot, :], d["dense2"][bass.ds(r * RING + b, 1)]
                                 .rearrange("b p n -> p (b n)")).then_inc(ring_loaded[slot], 16)
            for q in range(4):
                sp.wait_ge(s.out_ready, 2 * q + 2)
                sp.dma_start(out[:, 2 * q:2 * q + 2, :], X[:, 2 * q:2 * q + 2, :]).then_inc(s.out_stored, 16)
            sp.wait_ge(s.out_stored, 64)

        @block.gpsimd
        def _(pool):
            pool.wait_ge(s.toep_sb, 16)
            pool.dma_start(d["toep"].rearrange("h p j -> p h j")[:, :, 0:TOEP], TW[:, :, 0:TOEP]).then_inc(s.toep_stored, 16)
            side_block3(pool)
            pool.wait_ge(s.lru_in, 16)
            pool.wait_ge(s.toep_stored, 16)


        @block.tensor
        def _(pe):
            def mm(o, lhsT, rhs, start=True, stop=True):
                return nc.tensor.matmul(o, lhsT, rhs, start=start, stop=stop)

            def arrived(block_no):
                pe.wait_ge(ring_loaded[block_no % RING], uses(block_no))

            def dense_unit(block_no, sub, bank, act, tokens_out=False, start=True, stop=True, ready=None):
                if not tokens_out:
                    for k in range(KT):
                        if ready:
                            pe.wait_ge(ready[0], ready[1] + k + 1)
                        last = mm(bank[:, 0:SEQ], weights(block_no, sub, k), act[:, k, :],
                                  start and k == 0, stop and k == KT - 1)
                else:
                    for t in range(TT):
                        for k in range(KT):
                            if ready and t == 0:
                                pe.wait_ge(ready[0], ready[1] + k + 1)
                            last = mm(bank[:, t * P:(t + 1) * P], act[:, k, t * P:(t + 1) * P],
                                      weights(block_no, sub, k), k == 0, k == KT - 1)
                return last

            def column_sum(i, k, bank=7):
                pe.wait_ge(s.norm_squared, KT * i + k + 1)
                if i and k == 0:
                    pe.wait_ge(s.norm_root, i)
                last = mm(B[bank][:, 0:SEQ], ones[:], SQ[:, k, :], k == 0, k == KT - 1)
                if k == KT - 1:
                    last.then_inc(s.norm_summed, 1)

            def column_sums(i, bank=7):
                for k in range(KT):
                    column_sum(i, k, bank)

            pe.wait_ge(s.consts_in, 16)
            pe.wait_ge(s.ones_ready, 1)
            pe.wait_ge(s.rel_ready, 1)
            for i in range(2 * AH):
                if i >= 2:
                    pe.wait_ge(s.toep_sb, i - 1)
                kind, h = i // AH, i % AH
                mm(B[4 + i % 2][:, 0:TOEP], RELB[0:REL_BUCKETS + 1, h, 0:P],
                   con("buckets")[0:REL_BUCKETS + 1, kind * TOEP:(kind + 1) * TOEP]).then_inc(s.toep_mm, 1)

            column_sums(0)
            column_sums(1)

            def ada_block_product(n):
                r, b = n // 4, n % 4
                slot = ada_block(n)
                arrived(slot)
                for kk in range(2):
                    k = 2 * b + kk
                    for j in range(4):
                        at = kk * DEXP + j * 512
                        last = mm(B[ADA_BANK[r]][32 * j:32 * j + 32, :], C2[:, k, :], ring[:, slot % RING, at:at + 512],
                                  k == 0, k == KT - 1)
                last.then_inc(s.ring_used, 1)

            def ada_transpose(r):
                pe.wait_ge(s.ada_sb, r + 1)
                for q in range(4):
                    last = nc.tensor.transpose(B[ADA_BANK[r] + 1][:, q * P:(q + 1) * P], ADA[r][:, q * P:(q + 1) * P], ident)
                last.then_inc(s.ada_tr, 1)

            pe.wait_ge(s.c_ready, 1)
            for b in range(4):
                ada_block_product(b)
            ada_transpose(0)

            pe.wait_ge(s.mod_ready, 1)
            pe.wait_ge(s.toep_sb, 2 * AH)
            for pu, (unit, act, tokens_out) in enumerate(DENSE1):
                if pu >= 4:
                    pe.wait_ge(s.dense_sb, pu - 3)
                blk, sub = d1_block(unit), unit % UNITS
                arrived(blk)
                last = dense_unit(blk, sub, B[pu % 4], H if act == "x" else HC, tokens_out,
                                  ready=(s.hc_ready, 0) if pu == 0 else (s.hx_ready, 0) if pu == 1 else None)
                last.then_inc(s.ring_used if block_ends(unit, act) else s.dense_mm, 1)
                if pu in ADA_AFTER:
                    for b in ADA_AFTER[pu]:
                        ada_block_product(b)
                if pu in (16, 24):
                    ada_transpose(1 if pu == 16 else 2)
                if pu == 25:
                    pe.wait_ge(s.dense_sb, 20)
                    pe.wait_ge(s.mod_ready, 3)
                    for i in range(4):
                        mm(B[4 + i][:], con("swap"), tiles(16 + 2 * i, 2)).then_inc(s.rot_mm, 1)

            pe.wait_ge(s.kw_ready, 2)
            pe.wait_ge(s.qk_rot, 4)
            pe.wait_ge(s.dense_sb, 16)
            for a in range(2):
                for h in range(HEADS1):
                    for t in range(TT):
                        last = mm(B[4 + a][:, h * P:(h + 1) * P], KW[:, a, t, h * P:(h + 1) * P],
                                  VC[:, t, h * P:(h + 1) * P], t == 0, t == TT - 1)
                last.then_inc(s.state_mm, 1)
            for h in range(HEADS1):
                if h == 2:
                    pe.wait_ge(s.state_sb, 2)
                for m in range(TT):
                    last = mm(B[SCORE_BANK[h]][:, m * SEQ:(m + 1) * SEQ], KQR[:, h, m * P:(m + 1) * P], KQR[:, 4 + h, :])
                last.then_inc(s.score_mm, 1)
            pe.wait_ge(s.state_sb, 2)
            pe.wait_ge(s.qfb_ready, 1)
            for h in range(HEADS1):
                pe.wait_ge(s.sd_ready, h + 1)
                bank = B[SCORE_BANK[h]][:, 0:SEQ]
                for m in range(TT):
                    mm(bank, VX[:, m, h * P:(h + 1) * P], DM_[:, h, m, :], m == 0, False)
                mm(bank, SFB[:, 0, h, :], QFB[:, h, :], False, False)
                mm(bank, SFB[:, 1, h, :], QFB[:, 4 + h, :], False, True).then_inc(s.y_mm, 1)
            pe.wait_ge(s.y_sb, 4)
            for i in range(2):
                mm(B[4 + i][:], ones[:], tiles(16 + 2 * i, 2)).then_inc(s.mean_mm, 1)
            pe.wait_ge(s.ysq_ready, 1)
            for i in range(2):
                mm(B[6 + i][:], ones[:], tiles(16 + 2 * i, 2)).then_inc(s.var_mm, 1)

            pe.wait_ge(s.mix_ready, 1)
            for i in range(8):
                pu, unit = 36 + i, 28 + i
                pe.wait_ge(s.dense_sb, pu - 3)
                blk, sub = d1_block(unit), unit % UNITS
                arrived(blk)
                last = dense_unit(blk, sub, B[pu % 4], MIX)
                last.then_inc(s.ring_used if block_ends(unit) else s.dense_mm, 1)
                if i:
                    column_sum(2, i - 1)
            column_sum(2, KT - 1)
            column_sums(3)

            wr = par("w_router").rearrange("p (k e) -> p k e", k=KT)
            for t in range(TT):
                for k in range(KT):
                    if t == 0:
                        pe.wait_ge(s.h2_ready, k + 1)
                    last = mm(B[4][:, t * EXPERTS:(t + 1) * EXPERTS], H[:, k, t * P:(t + 1) * P], wr[:, k, :], k == 0, k == KT - 1)
            last.then_inc(s.router_mm, 1)
            pe.wait_ge(s.dense_sb, 44)
            for n in range(4):
                for q in range(4):
                    t, k = n // 2, 4 * (n % 2) + q
                    last = nc.tensor.transpose(B[n][:, q * P:(q + 1) * P], H[:, k, t * P:(t + 1) * P], ident)
                last.then_inc(s.ht_tr, 1)
            pe.wait_ge(s.aff_ready, 1)
            for t in range(TT):
                last = nc.tensor.transpose(B[5][0:EXPERTS, t * P:(t + 1) * P], LOGIT[:, t, :], ident)
            last.then_inc(s.aff_tr, 1)
            pe.wait_ge(s.topk_ready, 1)
            mm(B[6][:], ones[0:EXPERTS, :], R16[0:EXPERTS, :])
            mm(B[7][:, 0:EXPERTS], IDX4[0:EXPERTS, :], ident[0:EXPERTS, 0:EXPERTS])
            mm(B[7][:, EXPERTS:2 * EXPERTS], VAL4[0:EXPERTS, :], ident[0:EXPERTS, 0:EXPERTS]).then_inc(s.slot_mm, 1)
            pe.wait_ge(s.sel_ready, 1)
            pe.wait_ge(s.ht_sb, 4)
            for k in range(KT):
                if k >= 4:
                    pe.wait_ge(s.xs_sb, k - 3)
                for t in range(TT):
                    last = mm(B[k % 4][:], HT[:, t, k * P:(k + 1) * P], SEL[:, t, :], t == 0, t == TT - 1)
                last.then_inc(s.xs_mm, 1)

            pe.wait_ge(s.xs_sb, KT)
            pe.wait_ge(s.slots_ready, 1)
            for q in range(4):
                mm(B[4 + q][:], ZERO[0:1, 0:P], ZERO[0:1, :], True, False)
            with pe.Fori(0, EXPERTS) as e:
                def expert_block(b):
                    blk = EXP_BLOCK0 + b
                    pe.wait_ge(ring_loaded[blk % RING], e * (16 * EXP_BLOCKS // RING) + uses(blk))
                    return blk % RING

                pe.wait_ge(s.xse_ready, e + 1)
                for half, bank in ((0, B[0]), (1, B[1])):
                    for b in range(4):
                        slot = expert_block(4 * half + b)
                        for kk in range(2):
                            k = 2 * b + kk
                            for j in range(4):
                                at = kk * DEXP + j * 512
                                last = mm(bank[32 * j:32 * j + 32, :], XSE[:, k, :], ring[:, slot, at:at + 512],
                                          k == 0, k == KT - 1)
                        last.then_inc(s.ring_used, 1)
                pe.wait_ge(s.hid_ready, e + 1)
                for q in range(4):
                    last = nc.tensor.transpose(B[0][:, q * P:(q + 1) * P], HID[:, q * P:(q + 1) * P], ident)
                last.then_inc(s.hid_tr, 1)
                pe.wait_ge(s.hidt_sb, e + 1)
                for c in range(4):
                    slot = expert_block(8 + c)
                    for half in range(2):
                        for j in range(4):
                            at = j * DM + half * 512
                            last = mm(B[2 + half][32 * j:32 * j + 32, :], HIDT[:, c * P + 32 * j:c * P + 32 * j + 32],
                                      ring[:, slot, at:at + 512], c == 0, c == 3)
                    last.then_inc(s.ring_used, 1)
                pe.wait_ge(s.selt_ready, e + 1)
                pe.wait_ge(s.y_low, e + 1)
                pe.wait_ge(s.y_high, e + 1)
                for k in range(KT):
                    last = nc.tensor.matmul(B[4 + k // 2][:, (k % 2) * SEQ:(k % 2 + 1) * SEQ], YE[:, k * P:(k + 1) * P],
                                            SELT[:], start=False, stop=False)
                last.then_inc(s.acc_done, 1)
            for q in range(4):
                last = mm(B[4 + q][:], ZERO[0:1, 0:P], ZERO[0:1, :], False, True)
            last.then_inc(s.acc_done, 1)
            column_sums(4, bank=3)
            tensor_block2(pe, mm, arrived, dense_unit, column_sum, column_sums)
            tensor_block3(pe, mm, arrived, dense_unit, column_sum, column_sums)

        @block.scalar
        def _(act):
            steps = [0]

            def link(ins):
                steps[0] += 1
                ins.then_inc(s.act_step, 1)
                act.wait_ge(s.act_step, steps[0])

            units_done = [0]

            def unit_done(block_no, ends):
                if ends:
                    act.wait_ge(s.ring_used, block_no + 1)
                else:
                    units_done[0] += 1
                    act.wait_ge(s.dense_mm, units_done[0])

            def fn(o, i, f, **kw):
                return nc.scalar.activation(o, i, f, **kw)

            def square(k, src):
                fn(SQ[:, k, :], src, ACT.Square).then_inc(s.norm_squared, 1)

            def squares_of_x(ready, count):
                for k in range(KT):
                    act.wait_ge(ready, count + k + 1)
                    square(k, X[:, k, :])

            def root(i, bank=7):
                fn(ROOT_WARM[:, i:i + 1], ones[:, 0:1], ACT.Sqrt)
                act.wait_ge(s.norm_summed, i + 1)
                fn(RS[:, i % 2, :], B[bank][:, 0:SEQ], ACT.Sqrt, scale=1.0 / DM, bias=EPS_COL).then_inc(s.norm_root, 1)

            act.dma_start(params[:], d["params"]).then_inc(s.params_in, 16)
            act.dma_start(consts[:], d["consts"]).then_inc(s.consts_in, 16)
            act.dma_start(CTXR, d["ctx"]).then_inc(s.ctx_in, 16)
            act.dma_start(X[:, :, :], d["x"]).then_inc(s.x_in, 16)

            act.wait_ge(s.params_in, 16)
            act.wait_ge(s.zeros_ready, 1)
            fn(C2[:, :, 0:2], par("cc").rearrange("p (k m) -> p k m", m=2), ACT.Silu).then_inc(s.c_ready, 1)
            link(fn(LT, par("decay"), ACT.Abs))
            link(fn(LT, LT, ACT.Exp, scale=-1.0))
            fn(LT, LT, ACT.Ln, bias=1.0).then_inc(s.decay_soft, 1)
            for i in range(2 * AH):
                act.wait_ge(s.toep_mm, i + 1)
                fn(TW[:, i, 0:TOEP], B[4 + i % 2][:, 0:TOEP], ACT.Copy).then_inc(s.toep_sb, 1)
            act.wait_ge(s.ctx_in, 16)
            for k in range(KT):
                square(k, CTXR[:, k, :])
            act.wait_ge(s.ones_ready, 2)
            root(0)
            act.wait_ge(s.x_in, 16)
            for k in range(KT):
                square(k, X[:, k, :])
            root(1)

            def ada_copy(r):
                act.wait_ge(s.ring_used, ada_block(4 * r + 3) + 1)
                fn(ADA[r], B[ADA_BANK[r]][:], ACT.Copy).then_inc(s.ada_sb, 1)

            ada_copy(0)
            act.dma_start(lru_w[:, :, :, :], d["lru_w"]).then_inc(s.lru_in, 16)
            act.wait_ge(s.consts_in, 16)
            act.wait_ge(s.ramp_ready, 1)
            fn(tiles(60, 8), tiles(60, 8), ACT.Exp).then_inc(s.dmat_ready, 1)
            for h in range(HEADS1):
                fn(QFB[:, h, :], con("row1"), ACT.Exp, scale=LG[:, h:h + 1])
                fn(QFB[:, 4 + h, :], con("row_rev"), ACT.Exp, scale=LG[:, 4 + h:5 + h])
                fn(WFB[:, :, h], con("tok_rev"), ACT.Exp, scale=LG[:, h:h + 1])
                last = fn(WFB[:, :, 4 + h], con("tok"), ACT.Exp, scale=LG[:, 4 + h:5 + h])
            last.then_inc(s.xi_ready, 1)

            act.wait_ge(s.toep_stored, 16)
            for pu, (unit, a, tokens_out) in enumerate(DENSE1):
                unit_done(d1_block(unit), block_ends(unit, a))
                src, scale, i = B[pu % 4][:, 0:SEQ], 1.0, unit % 4
                if tokens_out:
                    src = src.rearrange("p (t c) -> p t c", t=TT)
                if unit < 4:
                    dst, scale = (KQ[:, i, :] if a == "x" else KC[:, :, i, :]), float(P) ** -0.5
                elif unit < 8:
                    dst = (VX if a == "x" else VC)[:, :, i * P:(i + 1) * P]
                else:
                    dst = (KQ[:, 4 + i, :], G_[:, i, :], B_[:, i, :], C_[:, i, :], XI_[:, i, :])[unit // 4 - 2]
                fn(dst, src, ACT.Copy, scale=scale).then_inc(s.dense_sb, 1)
                if pu in (15, 23):
                    ada_copy(1 if pu == 15 else 2)
            act.wait_ge(s.dense_sb, 36)
            fn(tiles(36, 4), tiles(36, 4), ACT.Silu).then_inc(s.g_silu, 1)
            for a in range(2):
                act.wait_ge(s.state_mm, a + 1)
                fn(SFB[:, a].rearrange("p h c -> p (h c)"), B[4 + a][:], ACT.Copy).then_inc(s.state_sb, 1)
            for h in range(HEADS1):
                act.wait_ge(s.y_mm, h + 1)
                fn(Y[:, h, :], B[SCORE_BANK[h]][:, 0:SEQ], ACT.Copy).then_inc(s.y_sb, 1)
            act.wait_ge(s.yc_ready, 1)
            fn(tiles(16, 4), tiles(20, 4), ACT.Square).then_inc(s.ysq_ready, 1)
            act.wait_ge(s.yvar_ready, 1)
            fn(tiles(52, 4), tiles(52, 4), ACT.Sqrt).then_inc(s.yrstd_ready, 1)
            for i in range(8):
                unit_done(d1_block(28 + i), block_ends(28 + i))
                square(i, B[(36 + i) % 4][:, 0:SEQ])
                fn(MO[:, i, :], B[(36 + i) % 4][:, 0:SEQ], ACT.Copy).then_inc(s.dense_sb, 1)
            root(2)
            squares_of_x(s.x_ready, 0)
            root(3)
            act.wait_ge(s.logit_shift, 1)
            fn(LOGIT, LOGIT, ACT.Exp).then_inc(s.aff_exp, 1)
            for n in range(4):
                act.wait_ge(s.ht_tr, n + 1)
                fn(HT[:, n // 2, (n % 2) * 512:(n % 2 + 1) * 512], B[n][:], ACT.Copy).then_inc(s.ht_sb, 1)
            for k in range(KT):
                act.wait_ge(s.xs_mm, k + 1)
                fn(XS[:, k, 0:EXPERTS * CAP], B[k % 4][:], ACT.Copy).then_inc(s.xs_sb, 1)
            with act.Fori(0, EXPERTS) as e:
                act.wait_ge(s.ring_used, e * EXP_BLOCKS + (EXP_BLOCK0 + 4))
                fn(SG, B[0][:], ACT.Silu).then_inc(s.silu_sb, 1)
                act.wait_ge(s.hid_tr, e + 1)
                fn(HIDT, B[0][:], ACT.Copy).then_inc(s.hidt_sb, 1)
                act.wait_ge(s.ring_used, e * EXP_BLOCKS + (EXP_BLOCK0 + 12))
                fn(YE[:, 0:512], B[2][:], ACT.Copy).then_inc(s.y_low, 1)
            act.wait_ge(s.acc_done, EXPERTS + 1)
            for q in range(4):
                fn(SQ[:, 2 * q:2 * q + 2, :].rearrange("p k t -> p (k t)"), B[4 + q][:], ACT.Square).then_inc(s.norm_squared, 2)
            for q in range(4):
                last = fn(FO[:, 2 * q:2 * q + 2, :].rearrange("p k t -> p (k t)"), B[4 + q][:], ACT.Copy)
            last.then_inc(s.ffn_sb, 1)
            root(4, bank=3)
            scalar_block2(act, fn, link, square, squares_of_x, root, unit_done, units_done)
            scalar_block3(act, fn, link, squares_of_x, root, unit_done, units_done)

        @block.vector
        def _(dve):
            steps, rstd = [0], [None]
            v = nc.vector

            def link(ins):
                steps[0] += 1
                ins.then_inc(s.dve_step, 1)
                dve.wait_ge(s.dve_step, steps[0])

            def mark(ins):
                steps[0] += 1
                ins.then_inc(s.dve_step, 1)
                return steps[0]

            def norm_invert(i):
                rstd[0] = RS[:, i % 2, :]
                dve.wait_ge(s.norm_root, i + 1)
                v.reciprocal(rstd[0], rstd[0]).then_inc(s.norm_inverted, 1)
                dve.wait_ge(s.norm_inverted, i + 1)

            def times_rstd(dst, src, gain, k):
                return v.scalar_tensor_tensor(out=dst[:, k, :], in0=src[:, k, :], scalar=gain[:, k:k + 1],
                                              in1=rstd[0], op0=ALU.mult, op1=ALU.mult)

            def norm_to(dst, src, gain, ready):
                for k in range(KT):
                    times_rstd(dst, src, gain, k).then_inc(ready, 1)

            def norm_shift(dst, src, gain, shift, ready):
                scaled = mark(times_rstd(dst, src, gain, 0))
                for k in range(KT):
                    done = scaled
                    if k + 1 < KT:
                        scaled = mark(times_rstd(dst, src, gain, k + 1))
                    dve.wait_ge(s.dve_step, done)
                    v.tensor_scalar(dst[:, k, :], dst[:, k, :], shift[:, k:k + 1], None, ALU.add).then_inc(ready, 1)

            def add_normed(src, gain):
                scaled = mark(times_rstd(src, src, gain, 0))
                for k in range(KT):
                    done = scaled
                    if k + 1 < KT:
                        scaled = mark(times_rstd(src, src, gain, k + 1))
                    dve.wait_ge(s.dve_step, done)
                    v.tensor_tensor(X[:, k, :], X[:, k, :], src[:, k, :], ALU.add).then_inc(s.x_ready, 1)

            v.memset(ones[:], 1.0).then_inc(s.ones_ready, 1)
            v.memset(EPS_COL, EPS).then_inc(s.ones_ready, 1)
            v.memset(small(0, KT * 32), 0.0).then_inc(s.zeros_ready, 1)
            dve.wait_ge(s.params_in, 16)
            nb = REL_BUCKETS + 1
            v.tensor_copy(RELB[0:nb, :, :], spread(par("rel")[0:nb, :], 2, P)).then_inc(s.rel_ready, 1)
            dve.wait_ge(s.decay_soft, 1)
            v.scalar_tensor_tensor(out=LG, in0=par("decay"), scalar=0.0, in1=LT, op0=ALU.min,
                                   op1=ALU.subtract).then_inc(s.decay_ready, 1)
            dve.wait_ge(s.decay_ready, 1)
            dve.wait_ge(s.consts_in, 16)
            for h in range(HEADS1):
                ramp = DM_[:, h].rearrange("p m n -> p (m n)")
                link(v.tensor_scalar(ramp, con("ahead"), LG[:, h:h + 1], None, ALU.mult))
                last = v.scalar_tensor_tensor(out=ramp, in0=con("behind"), scalar=LG[:, 4 + h:5 + h], in1=ramp,
                                              op0=ALU.mult, op1=ALU.add)
            last.then_inc(s.ramp_ready, 1)

            def modulation(r):
                dve.wait_ge(s.ada_tr, r + 1)
                bias = par("b_ada", 16 * r, 16 * r + 16).rearrange("p (j q) -> p j q", j=4)
                v.tensor_tensor(MOD[:, 16 * r:16 * r + 16, :].rearrange("p (j q) s -> p j q s", j=4),
                                B[ADA_BANK[r] + 1][:].rearrange("p (q j m) -> p j q m", q=4, j=4)[:, :, :, 0:2],
                                spread(bias, 3, 2), ALU.add).then_inc(s.mod_ready, 1)
                dve.wait_ge(s.mod_ready, r + 1)

            def plus_one_times(o, scale, gain):
                link(v.scalar_tensor_tensor(out=o, in0=scale, scalar=1.0, in1=gain, op0=ALU.add, op1=ALU.mult))

            norm_invert(0)
            modulation(0)
            for a in range(2):
                plus_one_times(A1[:, a, :], MOD[:, 8:16, a], par("pre_mix_g"))
            norm_shift(HC, CTXR, A1[:, 1, :], MOD[:, 0:8, 1], s.hc_ready)
            norm_invert(1)
            norm_shift(H, X, A1[:, 0, :], MOD[:, 0:8, 0], s.hx_ready)
            dve.wait_ge(s.toep_mm, 2 * AH)
            dve.wait_ge(s.dense_sb, 8)
            rot = ROT.rearrange("p (t h c) -> p t h c", t=TT, h=HEADS1)
            half = P // 2
            cos = spread(con("cos_t").rearrange("p (t c) -> p t c", t=TT), 2, HEADS1)
            sin = spread(con("sin_t").rearrange("p (t c) -> p t c", t=TT), 2, HEADS1)
            ta = tiles(0, 2).rearrange("p (t h c) -> p t h c", t=TT, h=HEADS1)
            tb = tiles(2, 2).rearrange("p (t h c) -> p t h c", t=TT, h=HEADS1)
            k1, k2 = KC[:, :, :, 0:half], KC[:, :, :, half:P]
            v.tensor_tensor(rot[:, :, :, 0:half], k1, cos, ALU.mult)
            link(v.tensor_tensor(ta, k2, sin, ALU.mult))
            v.tensor_tensor(rot[:, :, :, 0:half], rot[:, :, :, 0:half], ta, ALU.subtract)
            v.tensor_tensor(rot[:, :, :, half:P], k1, sin, ALU.mult)
            link(v.tensor_tensor(tb, k2, cos, ALU.mult))
            link(v.tensor_tensor(rot[:, :, :, half:P], rot[:, :, :, half:P], tb, ALU.add))
            dve.wait_ge(s.xi_ready, 1)
            for a in range(2):
                v.tensor_tensor(KW[:, a].rearrange("p t (h c) -> p t h c", h=HEADS1), rot,
                                spread(WFB[:, :, 4 * a:4 * a + 4], 3, P), ALU.mult).then_inc(s.kw_ready, 1)
            modulation(1)
            modulation(2)
            plus_one_times(A2, MOD[:, 32:40, 0], par("pre_ffn_g"))
            link(v.tensor_tensor(G1P, MOD[:, 16:24, 0], par("post_mix_g"), ALU.mult))
            link(v.tensor_tensor(G2P, MOD[:, 40:48, 0], par("post_ffn_g"), ALU.mult))
            dve.wait_ge(s.dense_sb, 20)
            link(v.tensor_tensor(KQR, KQ, spread(con("cos_c"), 1, 8), ALU.mult))
            for i in range(4):
                dve.wait_ge(s.rot_mm, i + 1)
                t2 = tiles3(2 * i, 2)
                link(v.tensor_tensor(t2, B[4 + i][:].rearrange("p (k t) -> p k t", k=2), spread(con("sin_c"), 1, 2), ALU.mult))
                v.tensor_tensor(KQR[:, 2 * i:2 * i + 2, :], KQR[:, 2 * i:2 * i + 2, :], t2, ALU.add).then_inc(s.qk_rot, 1)
            dve.wait_ge(s.qk_rot, 4)
            v.tensor_tensor(QFB[:, 0:4, :], QFB[:, 0:4, :], KQR[:, 4:8, :], ALU.mult)
            v.tensor_tensor(QFB[:, 4:8, :], QFB[:, 4:8, :], KQR[:, 4:8, :], ALU.mult).then_inc(s.qfb_ready, 1)
            dve.wait_ge(s.dmat_ready, 1)
            for h in range(HEADS1):
                dve.wait_ge(s.score_mm, h + 1)
                dm = DM_[:, h].rearrange("p m n -> p (m n)")
                v.tensor_tensor(dm, B[SCORE_BANK[h]][:], dm, ALU.mult).then_inc(s.sd_ready, 1)
            dve.wait_ge(s.dense_sb, 36)
            link(v.tensor_tensor(C_, C_, XI_, ALU.mult))
            grid = lambda ap: ap.rearrange("p (r w) -> p r w", w=64)
            for i in range(4):
                w = par("conv_w", 3 * i, 3 * i + 3)
                o, u = grid(XI_[:, i, :]), grid(C_[:, i, :])
                link(v.tensor_scalar(XI_[:, i, :], C_[:, i, :], w[:, 1:2], par("conv_b", i, i + 1), ALU.mult, ALU.add))
                link(v.scalar_tensor_tensor(out=o[:, :, 1:64], in0=u[:, :, 0:63], scalar=w[:, 0:1], in1=o[:, :, 1:64],
                                            op0=ALU.mult, op1=ALU.add))
                link(v.scalar_tensor_tensor(out=o[:, :, 0:63], in0=u[:, :, 1:64], scalar=w[:, 2:3], in1=o[:, :, 0:63],
                                            op0=ALU.mult, op1=ALU.add))
            v.tensor_tensor(MIX[:, 0:4, :], XI_, B_, ALU.mult)
            dve.wait_ge(s.y_sb, 4)
            for i in range(2):
                dve.wait_ge(s.mean_mm, i + 1)
                last = v.scalar_tensor_tensor(out=tiles(20 + 2 * i, 2), in0=B[4 + i][:], scalar=-1.0 / P, in1=tiles(16 + 2 * i, 2),
                                              op0=ALU.mult, op1=ALU.add)
            last.then_inc(s.yc_ready, 1)
            for i in range(2):
                dve.wait_ge(s.var_mm, i + 1)
                link(v.tensor_scalar(tiles(52 + 2 * i, 2), B[6 + i][:], 1.0 / P, EPS, ALU.mult, ALU.add))
            v.reciprocal(tiles(52, 4), tiles(52, 4)).then_inc(s.yvar_ready, 1)
            dve.wait_ge(s.yrstd_ready, 1)
            link(v.tensor_tensor(YC, YC, R4, ALU.mult))
            dve.wait_ge(s.g_silu, 1)
            for h in range(HEADS1):
                last = v.scalar_tensor_tensor(out=MIX[:, 4 + h, :], in0=YC[:, h, :], scalar=par("ret_norm_g", h, h + 1),
                                              in1=G_[:, h, :], op0=ALU.mult, op1=ALU.mult)
            last.then_inc(s.mix_ready, 1)

            norm_invert(2)
            dve.wait_ge(s.dense_sb, 44)
            add_normed(MO, G1P)
            norm_invert(3)
            norm_shift(H, X, A2, MOD[:, 24:32, 0], s.h2_ready)
            v.memset(ZERO[0:1, :], 0.0)
            v.memset(XS[:, :, EXPERTS * CAP:], 0.0)

            dve.wait_ge(s.router_mm, 1)
            link(v.tensor_tensor(LOGIT, B[4][:, 0:32].rearrange("p (t e) -> p t e", t=TT), spread(par("b_router"), 1, TT), ALU.add))
            link(v.tensor_reduce(RMAX, LOGIT, AXX, ALU.max))
            v.tensor_tensor(LOGIT, LOGIT, spread(RMAX, 2, EXPERTS), ALU.subtract).then_inc(s.logit_shift, 1)
            dve.wait_ge(s.aff_exp, 1)
            link(v.tensor_reduce(RSUM, LOGIT, AXX, ALU.add))
            link(v.reciprocal(RSUM, RSUM))
            v.tensor_tensor(LOGIT, LOGIT, spread(RSUM, 2, EXPERTS), ALU.mult).then_inc(s.aff_ready, 1)
            dve.wait_ge(s.aff_tr, 1)
            at = AT[0:EXPERTS, :]
            link(v.tensor_copy(at, B[5][0:EXPERTS, 0:SEQ]))
            for r in range(CAP // 8):
                best = VAL[0:EXPERTS, 8 * r:8 * r + 8]
                link(v.max(best, at))
                link(v.max_index(idx_u[:, 8 * r:8 * r + 8], best, at))
                link(v.match_replace(at, best, at, -1.0))
            link(v.tensor_copy(IDXF[0:EXPERTS, :], idx_u[:]))
            e16 = EXPERTS
            v.tensor_tensor(R16[0:e16, :].rearrange("p (e c) -> p e c", e=e16), spread(IDXF[0:e16, :], 1, e16),
                            con("own_expert")[0:e16, :].rearrange("p (e c) -> p e c", e=e16), ALU.mult)
            v.tensor_copy(IDX4[0:e16, :].rearrange("p (j c) -> p j c", j=4), spread(IDXF[0:e16, :], 1, 4))
            v.tensor_copy(VAL4[0:e16, :].rearrange("p (j c) -> p j c", j=4), spread(VAL[0:e16, :], 1, 4)).then_inc(s.topk_ready, 1)
            dve.wait_ge(s.slot_mm, 1)
            for t in range(TT):
                last = v.tensor_scalar(SEL[:, t, :], B[6][:], con("tok")[:, t:t + 1], None, ALU.is_equal)
            last.then_inc(s.sel_ready, 1)
            v.tensor_copy(small(460, 32), B[7][:, 0:32]).then_inc(s.slots_ready, 1)

            dve.wait_ge(s.xs_sb, KT)
            dve.wait_ge(s.slots_ready, 1)
            v.tensor_copy(XSE, XS[:, :, 0:CAP]).then_inc(s.xse_ready, 1)
            with dve.Fori(0, EXPERTS) as e:
                dve.wait_ge(s.ring_used, e * EXP_BLOCKS + (EXP_BLOCK0 + 8))
                dve.wait_ge(s.silu_sb, e + 1)
                v.tensor_tensor(HID, SG, B[1][:], ALU.mult).then_inc(s.hid_ready, 1)
                v.tensor_copy(XSE, XS[:, :, bass.ds(e * CAP + CAP, CAP)]).then_inc(s.xse_ready, 1)
                v.tensor_scalar(SELT, con("row"), SLOT_TOK[:, bass.ds(e, 1)], SLOT_GATE[:, bass.ds(e, 1)],
                                ALU.is_equal, ALU.mult).then_inc(s.selt_ready, 1)
                dve.wait_ge(s.ring_used, e * EXP_BLOCKS + (EXP_BLOCK0 + 12))
                v.tensor_copy(YE[:, 512:1024], B[3][:]).then_inc(s.y_high, 1)
            dve.wait_ge(s.ffn_sb, 1)
            norm_invert(4)
            add_normed(FO, G2P)
            vector_block2(dve, v, link, norm_invert, norm_to, add_normed)
            vector_block3(dve, v, link, norm_invert, norm_to)


def bucket_table():
    dist = 2 * P - 1 - np.arange(TOEP)
    n = np.maximum(dist, 0)
    ratio = np.log(np.maximum(n, 1).astype(np.float32) / np.float32(REL_EXACT)) / np.float32(math.log(REL_DIST / REL_EXACT))
    large = np.minimum(REL_EXACT + (ratio * np.float32(REL_BUCKETS - REL_EXACT)).astype(np.int32), REL_BUCKETS - 1)
    bucket = np.where(n < REL_EXACT, n, large)
    out = np.zeros((P, 2, TOEP), np.float32)
    for kind, limit in enumerate((P, SEQ)):
        row = np.where((dist >= 0) & (dist < limit), bucket, REL_BUCKETS)
        out[row, kind, np.arange(TOEP)] = 1.0
    return out.reshape(P, 2 * TOEP)


def const_table():
    f = np.float32
    p, n = np.arange(P), np.arange(SEQ)
    t = np.zeros((P, C_COLS), f)

    def put(name, a):
        at, cols = C_AT[name]
        a = np.asarray(a, f)
        t[:, at:at + cols] = np.broadcast_to(a.reshape(a.shape[0], -1) if a.ndim > 1 else a[None], (P, cols))

    put("ident", np.eye(P))
    swap = np.zeros((P, P), f)
    swap[np.arange(64) + 64, np.arange(64)] = -1.0
    swap[np.arange(64), np.arange(64) + 64] = 1.0
    put("swap", swap)
    half = P // 2
    inv = f(1.0) / np.power(f(10000.0), np.arange(half, dtype=f) / f(half))
    ang = (SEQ + n).astype(f)[None, :] * inv[p % half][:, None]
    put("cos_c", np.cos(ang)), put("sin_c", np.sin(ang))
    pos = p[:, None] + P * np.arange(TT)[None, :]
    ang = pos.astype(f)[:, :, None] * inv[None, None, :]
    put("cos_t", np.cos(ang)), put("sin_t", np.sin(ang))
    rel = n[None, None, :] - pos[:, :, None]
    put("ahead", np.maximum(rel, 0)), put("behind", np.maximum(-rel, 0))
    put("row1", n + 1), put("row_rev", SEQ - n), put("row", n)
    put("tok", pos), put("tok_rev", SEQ - 1 - pos)
    put("own_expert", (p[:, None, None] == np.arange(EXPERTS)[None, :, None]) * np.ones((1, 1, CAP)))
    c = p // 32
    starts = n % CHUNK == 0
    put("ssd_reset", ~(starts[None] & ((n // CHUNK)[None] >= c[:, None]) & ((n // CHUNK)[None] <= c[:, None] + 1)))
    chunk_of = (pos // CHUNK).T
    put("chunk_rows", c[:, None, None] == chunk_of[None])
    put("head_rows", (p % 32)[:, None] == np.arange(SSM_H)[None])
    causal = pos[:, :, None] <= n[None, None, :]
    put("causal", np.concatenate([causal[:, 0], causal[:, 1, P:]], 1))
    put("gla_reset", ~starts)
    put("gla_mask", (p[:, None] // CHUNK == p[None] // CHUNK) & (p[:, None] <= p[None]))
    put("half", np.stack([p < 64, p >= 64], 1))
    put("buckets", bucket_table())
    return t


def kernel(**inputs):
    import concourse.bacc as bacc
    from concourse.bass_utils import run_bass_kernel_spmd

    f = np.float32
    i = {k: np.asarray(v) for k, v in inputs.items()}
    cols = lambda a: np.asarray(a).reshape(-1, P).T
    taps = lambda w: w.reshape(w.shape[0], -1, P).transpose(2, 1, 0).reshape(P, -1)
    every = lambda a: np.broadcast_to(np.asarray(a).reshape(1, -1), (P, np.asarray(a).size))

    def rows(a, at=(0,)):
        o = np.zeros((P, a.shape[1]), f)
        for r in at:
            o[r:r + a.shape[0]] = a
        return o

    pairs = np.arange(2 * FT).reshape(2, FT).T.ravel()
    by_tile = lambda a: a.reshape(a.shape[0], -1, P)[:, pairs].reshape(a.shape[0], -1)
    chunks = range(0, P, 32)
    values = {
        "cc": np.stack([cols(i["c"][0]), cols(i["c_ctx"])], -1).reshape(P, -1),
        "b_ada": cols(i["b_ada"][0]), "pre_mix_g": cols(i["pre_mix_g"][0]), "post_mix_g": cols(i["post_mix_g"][0]),
        "pre_ffn_g": cols(i["pre_ffn_g"][0]), "post_ffn_g": cols(i["post_ffn_g"][0]),
        "conv_w": taps(i["conv_w"][0]), "conv_b": cols(i["conv_b"][0]), "decay": every(i["ret_decay_logit"][0]),
        "ret_norm_g": cols(i["ret_norm_g"][0]), "b_router": every(i["b_router"][0]),
        "w_router": i["w_router"][0].reshape(KT, P, EXPERTS).transpose(1, 0, 2).reshape(P, -1),
        "mix_pre": cols(i["mix_pre_norm_2"][0]), "mix_post": cols(i["mix_post_norm_2"][0]),
        "ssm_conv_w": taps(i["ssm_conv_w_2"][0]), "ssm_conv_b": cols(i["ssm_conv_b_2"][0]),
        "dt_bias": rows(i["ssm_dt_bias_2"][0][:, None], chunks), "a_log": rows(i["ssm_a_log_2"][0][:, None], chunks),
        "ssm_d": cols(np.repeat(i["ssm_d_2"][0], SSM_P)), "ssm_norm": cols(i["ssm_norm_2"][0]),
        "lru_conv_w": taps(i["lru_conv_w_2"][0]), "lru_conv_b": cols(i["lru_conv_b_2"][0]),
        "lru_br": cols(i["lru_br_2"][0].ravel()), "lru_bi": cols(i["lru_bi_2"][0].ravel()), "lru_lam": cols(i["lru_lambda_2"][0]),
        "gate_b": cols(i["gate_b_2"][0].ravel()), "ffn_pre": cols(i["ffn_pre_norm_2"][0]), "ffn_post": cols(i["ffn_post_norm_2"][0]),
        "ffn_conv_w": taps(by_tile(i["ffn_conv_w_2"][0])), "ffn_conv_b": cols(by_tile(i["ffn_conv_b_2"])[0]),
        "norm_gain": cols(i["norm_gain_3"].ravel()), "final_gain": cols(i["final_gain_3"]),
        "gla_b_up": cols(i["gla_b_up_3"][0]), "gla_gain": cols(i["gla_norm_gain_3"][0]), "sinks": every(i["swa_sinks_3"][0]),
        "rel": rows(np.concatenate([i["rel_bias_3"], np.full((1, AH), -1e30, f)])),
        "gla_w_up": rows(i["gla_w_up_3"][0]),
    }
    params = np.zeros((P, P_COLS), f)
    for name, (at, n) in P_AT.items():
        params[:, at:at + n] = values[name]

    def units(w, pick=None):
        w = w if pick is None else w[:, pick]
        return w.reshape(KT, P, -1, P).transpose(2, 1, 0, 3)

    def blocks(parts):
        u = np.concatenate(parts)
        return np.ascontiguousarray(u.reshape(-1, UNITS, P, KT * P).transpose(0, 2, 1, 3)).reshape(-1, P, BLK)

    r = lambda a, b: np.arange(a, b)
    w1 = i["w_in"][0]
    dense1 = blocks([units(w1, np.concatenate([r(2048, 3072), r(1536, 2048), r(3072, 3584), r(0, 1536)])), units(i["w_out"][0])])

    w2 = i["w_in_2"][0]
    z, xbc = r(0, 1024), r(1024, 2560)
    dt = np.zeros((DM, P), f)
    for a in chunks:
        dt[:, a:a + SSM_H] = w2[:, 2560:2576]
    w3 = i["w_in_even_3"][0]
    splits = np.cumsum([0, 256, 256, 512, 16, 512, 512, 128, 128, 512])
    aq, ak, av, ad, ag, bq, bk, bv, bg = (r(a, b) for a, b in zip(splits[:-1], splits[1:]))
    pair = (r(0, 512).reshape(2, 4, 64).transpose(1, 0, 2)).ravel()
    down_rank = np.zeros((DM, P), f)
    down_rank[:, 0:16] = w3[:, ad]
    we = i["w_out_even_3"][0][np.concatenate([r(0, 512), 512 + pair])]
    w4 = i["w_in_odd_3"][0]
    wd = i["w_ffn_down_2"][0].reshape(3, KT, P, KT, P).transpose(3, 0, 2, 1, 4).reshape(-1, P, KT, P)
    dense2 = blocks([
        units(w2, xbc), units(dt), units(w2, np.concatenate([r(3600, 4624), r(2576, 3600), z, r(4624, 6672)])),
        units(i["w_proj_lru_2"][0]), units(i["w_proj_ssm_2"][0]), units(i["w_out_2"][0]),
        units(i["w_ffn_up_2"][0].reshape(DM, -1, P)[:, pairs].reshape(DM, -1)), wd,
        units(down_rank), units(w3, np.concatenate([aq, ak, bq[pair], bk, bv, av, ag, bg[pair]])),
        units(we), units(w4), units(i["w_out_odd_3"][0])])
    lru = np.zeros((2, KT, P, P), f)
    for n, name in enumerate(("lru_wr_2", "lru_wi_2")):
        w = i[name][0].reshape(KT, 2, 64, 64)
        for b in range(2):
            lru[n, :, 64 * b:64 * b + 64, 64 * b:64 * b + 64] = w[:, b]
    by_channel = lambda a: np.ascontiguousarray(a.reshape(SEQ, KT, P).transpose(2, 1, 0))
    arrays = {
        "in_x": by_channel(i["x"][0]), "in_ctx": by_channel(i["ctx"][0]), "in_params": params, "in_consts": const_table(),
        "in_lru_w": np.ascontiguousarray(lru.transpose(2, 0, 1, 3)), "in_w_ada": i["w_ada"][0],
        "in_dense1": dense1, "in_dense2": dense2, "in_w_gate": i["w_gate"][0].reshape(-1, DEXP),
        "in_w_up": i["w_up"][0].reshape(-1, DEXP), "in_w_down": i["w_down"][0].reshape(-1, DM),
    }
    nc = bacc.Bacc("TRN2", target_bir_lowering=False, num_devices=1)
    d = {n[3:]: nc.dram_tensor(n, a.shape, F32, kind="ExternalInput").ap() for n, a in arrays.items()}
    d["toep"] = nc.dram_tensor("bias_diagonals", (2 * AH, P, TPITCH), F32).ap()
    out = nc.dram_tensor("out_x", (P, KT, SEQ), F32, kind="ExternalOutput").ap()
    program(nc, d, out)
    got = run_bass_kernel_spmd(nc, [arrays], core_ids=[0]).results[0]["out_x"]
    return np.ascontiguousarray(got.transpose(2, 1, 0)).reshape(1, SEQ, DM)
```

```python
import math
from contextlib import ExitStack
from collections import namedtuple

import numpy as np

import concourse.bass as bass
from concourse import mybir
from concourse.alu_op_type import AluOpType as ALU

F32 = mybir.dt.float32
F32R = mybir.dt.float32r
U32 = mybir.dt.uint32
ACT = mybir.ActivationFunctionType
AXX = mybir.AxisListType.X

P = 128
SEQ = 256
DM = 1024
KT = DM // P
TT = SEQ // P
EPS = 1e-6
HEADS1 = 4
EXPERTS = 16
CAP = 2 * SEQ // EXPERTS
DEXP = 2 * DM
SSM_H, SSM_P, CHUNK = 16, 64, 64
FFN = 3072
FT = FFN // P
REL_BUCKETS, REL_EXACT, REL_DIST = 32, 16, 128
AH = 8
TOEP = 383
TPITCH = 384

RING = 4
BLK = 4096
UNITS = 4
ADA_BLOCKS = 12
D1_UNITS = 28 + 8
D1_BLOCKS = D1_UNITS // UNITS
EXP_BLOCKS = 12
IN2, OUT2 = 53, 8
EVEN3, ODD3 = 23, 20
D2_LAYERS = (IN2, 8, 8, 8, 2 * FT, 8 * 3, EVEN3, 8, ODD3, 8)
D2_UNITS = sum(D2_LAYERS)
D2_BLOCKS = D2_UNITS // UNITS
FIRST = ([("ada", b) for b in range(4)] + [("dense", 0), ("ada", 4), ("ada", 5)]
         + [(kind, b + (5 if kind == "ada" else 0)) for b in range(1, 7) for kind in ("dense", "ada")]
         + [("dense", b) for b in range(7, D1_BLOCKS)])
EXP_BLOCK0 = len(FIRST)
EXTRA = (2, 4, 5, 6)
EXP_BASE = EXP_BLOCK0 - len(EXTRA)
D2_BLOCK0 = EXP_BASE + EXPERTS * EXP_BLOCKS

PARAMS = [("cc", 16), ("b_ada", 48), ("pre_mix_g", 8), ("post_mix_g", 8), ("pre_ffn_g", 8), ("post_ffn_g", 8),
          ("conv_w", 12), ("conv_b", 4), ("decay", 8), ("ret_norm_g", 4), ("b_router", 16), ("w_router", 128),
          ("mix_pre", 8), ("mix_post", 8), ("ssm_conv_w", 48), ("ssm_conv_b", 12), ("dt_bias", 1), ("a_log", 1),
          ("ssm_d", 8), ("ssm_norm", 8), ("lru_conv_w", 32), ("lru_conv_b", 8), ("lru_br", 8), ("lru_bi", 8),
          ("lru_lam", 8), ("gate_b", 16), ("ffn_pre", 8), ("ffn_post", 8), ("ffn_conv_w", 144), ("ffn_conv_b", 48),
          ("norm_gain", 16), ("final_gain", 8), ("gla_b_up", 2), ("gla_gain", 1), ("sinks", 8), ("rel", 8),
          ("gla_w_up", 256)]
SHARED = [("ident", 128), ("tok", 2), ("tok_rev", 2), ("half", 2)]
EARLY = [("swap", 128), ("cos_c", 256), ("sin_c", 256), ("cos_t", 128), ("sin_t", 128), ("row_rev", 256), ("row", 256)]
LATE = [("ssd_reset", 256), ("chunk_rows", 256), ("head_rows", 16), ("causal", 384), ("gla_reset", 256), ("gla_mask", 128)]
START = [("buckets", 2 * TOEP), ("ahead", 512), ("behind", 512)]


def offsets(entries):
    at, out = 0, {}
    for name, n in entries:
        out[name] = (at, n)
        at += n
    return out, at


P_AT, P_COLS = offsets(PARAMS)
C_AT, SHARED_COLS = offsets(SHARED)
EARLY_AT, EARLY_COLS = offsets(EARLY)
LATE_AT, LATE_COLS = offsets(LATE)
START_AT, START_COLS = offsets(START)
for entries in (EARLY_AT, LATE_AT):
    C_AT.update({name: (SHARED_COLS + at, n) for name, (at, n) in entries.items()})
C_COLS = SHARED_COLS + max(EARLY_COLS, LATE_COLS)

HIGHS = 4
AHEAD1, AHEAD2 = 2, 4

SEMS = """dense_sb ring_used dense_mm xc_ready lru_in ri_sig ri_mm cs_ready ssd_tr xbc_silu cb_mm ssd_sb cb_ready xs_tr
lmask_ready seg_ready bc_mm xdt_ready m_ready ya_pair ssd_y ya_sq ya_sum w_high x_ready dt_in dt_soft xbc_conv
lam_ready th_ready ly_gelu lru_neg lru_root seg_exp z_silu g_sig ya_gated ya_inv ya_rstd conv_step ffn_gelu
act_full act_high a_exp late_in lam_soft act_low bias_in lg_sb lg_mm lg_ready pt_sb pt_tr ao_mm gl_mm kp_ready
kp_tr att_mm bv_tr kpt_ready att_ready bv_sb bqh_ready kv_mm st_ready o_mm o_sq o_sb o_sum o_mean lg_shift lg_exp
gl_in gl_soft gl_b gl_exp gl_left eg_silu oa_var o_rstd first_units norm_summed ht_tr extra_in out_ready
out_stored w_low ht_sb ht_low norm_squared norm_root ada_sb ada_tr c_ready ones_ready consts_in kw_ready qk_rot
state_mm score_mm sd_ready y_mm mod_ready start_in toep_mm toep_sb rot_mm state_sb qfb_ready y_sb mean_mm
ysq_ready var_mm h2_ready router_mm aff_ready aff_tr topk_ready slot_mm sel_ready xs_sb xs_mm slots_ready
xse_ready hid_ready hid_tr hidt_sb selt_ready y_low y_high acc_done act_step params_in ctx_in x_in zeros_ready
decay_soft toep_stored ramp_ready dmat_ready xi_ready g_silu yc_ready yvar_ready yrstd_ready h2_scaled
logit_shift aff_exp silu_sb ffn_sb dve_step norm_inverted decay_ready""".split()


DENSE1 = ([(0, "ctx", t) for t in range(TT)] + [(u, "x", None) for u in range(4)]
          + [(4, a, t) for a in ("ctx", "x") for t in range(TT)] + [(u, "x", None) for u in range(8, 28)])
JOBS1 = len(DENSE1)
SCORE_BANK = (6, 7, 6, 7)
ADA_BANK = (0, 4, 4)
STATES_AFTER = JOBS1 - 12
ADA_AFTER = {5: (4, 5), 9: (6,), 13: (7,), 17: (8,), 21: (9,), 25: (10,), 29: (11,)}


INPUTS = [("ctx", 8), ("x", 8), ("mix", 8), ("in2", 8), ("lru", 8), ("ssm", 8), ("merged", 8), ("up", 8), ("ffn", FT),
          ("even", 8), ("even_out", 8), ("odd", 8), ("odd_out", 8)]
IN_AT, _ = offsets(INPUTS)


def tile_count(name, k):
    return IN_AT[name][0] + k + 1


def ada_block(b):
    return FIRST.index(("ada", b))


def d1_block(unit):
    return FIRST.index(("dense", unit // UNITS))


def job_ends(unit, act, t):
    return act == "x" and (unit % UNITS == UNITS - 1 if t is None else t == TT - 1)


def block_ends(unit):
    return unit % UNITS == UNITS - 1


def first_expert_block(b):
    return EXP_BLOCK0 + b - sum(extra < b for extra in EXTRA)


def conv_taps(dve, nc, link, out, src, w, bias, taps):
    link(nc.vector.tensor_scalar(out, src, w[:, taps - 1:taps], bias, ALU.mult, ALU.add))
    for s in range(1, taps):
        last = nc.vector.scalar_tensor_tensor(out=out[:, s:SEQ], in0=src[:, 0:SEQ - s], scalar=w[:, taps - 1 - s:taps - s],
                                              in1=out[:, s:SEQ], op0=ALU.mult, op1=ALU.add)
        if s < taps - 1:
            link(last)
    return last


def spread(ap, axis, n):
    a = ap.unsqueeze(axis)
    shape = list(a.shape)
    shape[axis] = n
    return a.broadcast_to(shape)


def program(nc, d, out):
    ctx = ExitStack()
    with ctx:
        def sb(name, shape, dt=F32):
            return ctx.enter_context(nc.sbuf_tensor(name, shape, dt))

        rounded = {}

        def sb_split(name, shape):
            buffer = sb(name, shape)
            size = 4 * math.prod(shape[1:])
            rounded[name] = nc.alloc_sbuf_tensor_at(name + "_rounded", shape, F32R, offset=nc.sbuf_base - size)
            return buffer

        s = namedtuple("Semaphores", SEMS)(*[ctx.enter_context(nc.semaphore(n)) for n in SEMS])
        ring_loaded = [ctx.enter_context(nc.semaphore(f"ring_loaded{i}")) for i in range(RING)]
        B = [ctx.enter_context(nc.psum_tensor(f"bank{i}", [P, 512], F32)) for i in range(8)]

        ring = sb_split("ring", [P, RING, BLK])
        params = sb("params", [P, P_COLS])
        consts = sb("consts", [P, C_COLS])
        X = sb("x_resid", [P, KT, SEQ])
        H = sb_split("h_normed", [P, KT, SEQ])
        SQ = sb_split("squares", [P, KT, SEQ])
        RS = sb("rstd", [P, 2, SEQ])
        U = sb_split("work", [P, 80 * SEQ])
        ones = sb("ones", [P, P])
        sm = sb("small", [P, 844])
        w_high_plain = sb_split("weights_high", [P, HIGHS, KT * P])
        w_high = rounded["weights_high"]
        HH_plain = sb_split("h_high", [P, KT, SEQ])
        HH = rounded["h_high"]
        idx_u = sb("topk_index", [EXPERTS, CAP], U32)

        def par(name, a=None, b=None):
            at, n = P_AT[name]
            return params[:, at + (0 if a is None else a):at + (n if b is None else b)]

        def con(name):
            at, n = C_AT[name]
            return consts[:, at:at + n]

        def tiles(a, n):
            return U[:, a * SEQ:(a + n) * SEQ]

        def tiles3(a, n):
            return tiles(a, n).rearrange("p (n t) -> p n t", t=SEQ)

        def small(at, n):
            return sm[:, at:at + n]

        def start_con(name):
            at, n = START_AT[name]
            return STARTERS[:, at:at + n]

        ident = con("ident")
        flat = lambda ap: ap[:, :, :].rearrange("p k t -> p (k t)")

        def weights(block, sub, k):
            at = (sub * KT + k) * P
            return ring[:, block % RING, at:at + P]

        def unit_weights(block, sub):
            return ring[:, block % RING, sub * KT * P:(sub + 1) * KT * P]

        def by_tile(ap):
            return [ap[:, k, :] for k in range(ap.shape[1])]

        def unit_place(n):
            return (d1_block(n), n % UNITS) if n < D1_UNITS else (d2_block(n - D1_UNITS), n % UNITS)

        def as_r(ap):
            return bass.AP(rounded[ap.tensor.name], ap.offset, ap.ap)

        def uses(block):
            return 16 * (block // RING + 1)

        C2 = small(0, KT * 32).rearrange("p (k m) -> p k m", m=32)
        MOD = small(256, 96).rearrange("p (n s) -> p n s", s=2)
        A1 = small(352, 16).rearrange("p (s k) -> p s k", s=2)
        A2 = small(368, 8)
        G1P = small(376, 8)
        G2P = small(384, 8)
        LG = small(392, 8)
        LT = small(400, 8)
        WFB = small(408, 16).rearrange("p (t h) -> p t h", t=TT)
        LOGIT = small(424, 32).rearrange("p (t e) -> p t e", t=TT)
        RMAX = small(456, 2)
        RSUM = small(458, 2)
        SLOT_TOK = small(460, 16)
        SLOT_GATE = small(476, 16)
        VAL = small(492, 32)
        IDXF = small(524, 32)
        IDX4 = small(556, 128)
        VAL4 = small(684, 128)
        ROOT_WARM, EPS_COL = small(812, 12), small(824, 1)
        NEGA, LAMC, LAMT = small(826, 1), small(828, 8), small(836, 8)
        TOT = small(1, 1)
        LSH = small(2, 32).rearrange("p (t h) -> p t h", t=TT)
        DEC = small(50, 8).rearrange("p (t c) -> p t c", t=2)
        AMAX = small(58, 16).rearrange("p (h b) -> p h b", b=2)
        ASUM = small(74, 16).rearrange("p (h b) -> p h b", b=2)
        ASNK = small(90, 16).rearrange("p (h b) -> p h b", b=2)

        CTXR, HC = tiles3(0, 8), tiles3(8, 8)
        MIX_HIGH = tiles3(0, 8)
        STARTERS = tiles(16, 7)[:, 0:START_COLS]
        KQ = tiles3(16, 8)
        VX = tiles(24, 4).rearrange("p (t c) -> p t c", t=TT)
        KC = tiles(28, 4).rearrange("p (t h c) -> p t h c", t=TT, h=HEADS1)
        VC = tiles(32, 4).rearrange("p (t c) -> p t c", t=TT)
        G_, B_, C_, XI_ = tiles3(36, 4), tiles3(40, 4), tiles3(44, 4), tiles3(48, 4)
        KQR = tiles3(52, 8)
        DM_ = tiles(60, 8).rearrange("p (h m n) -> p h m n", h=HEADS1, m=TT)
        QFB = tiles3(68, 8)
        ROT = tiles(76, 4)
        KW = SQ[:, :, :].rearrange("p (s t x) n -> p s t (x n)", s=2, t=TT)
        SFB = tiles(76, 4).rearrange("p (s h c) -> p s h c", s=2, h=HEADS1)
        TW = tiles(36, 3).rearrange("p (h j) -> p h j", j=TPITCH)
        ADA = tiles(52, 2), tiles(48, 2), tiles(60, 2)
        Y, YC = tiles3(16, 4), tiles3(20, 4)
        MIX, MO = tiles3(8, 8), tiles3(28, 8)
        R4 = tiles3(52, 4)
        HT, HT_HIGH = (tiles(i, 8).rearrange("p (t c) -> p t c", t=TT) for i in (0, 56))
        XS = tiles(8, 17).rearrange("p (k j) -> p k j", k=KT)
        SEL = tiles(25, 4).rearrange("p (t j) -> p t j", t=TT)
        R16, ONES_R = tiles(54, 2), tiles(53, 1)[:, 0:P]
        AT = tiles(38, 1)
        XSE = tiles(39, 1).rearrange("p (k m) -> p k m", k=KT)
        SG, HID, HIDT = tiles(40, 2), tiles(42, 2), tiles(44, 2)
        YE = tiles(46, 4)
        SELT = tiles(50, 1)
        ZERO = tiles(51, 2)
        FO = tiles3(60, 8)
        w_room = w_high_plain[:, :, :].rearrange("p n c -> p (n c)")
        h_high, squares, h_normed = (a[:, :, :].rearrange("p k t -> p (k t)") for a in (HH_plain, SQ, H))
        AHEAD = ((w_room[:, 0:DEXP], w_room[:, DEXP:2 * DEXP]), (tiles(64, 8), tiles(72, 8)),
                 (h_high, tiles(29, 8)), (squares, h_normed))

        RAW = tiles3(0, IN2)
        XC = tiles3(0, 8)
        TH, LY, Z, GATE = tiles3(13, 8), tiles3(21, 8), tiles3(29, 8), tiles3(37, 16)
        XBC = tiles3(53, 12)
        YA = tiles3(53, 8)
        DT, ADT, LCUM = tiles(65, 1), tiles(66, 1), tiles(67, 1)
        CBM = tiles(68, 3).rearrange("p (g l) -> p g l", g=2)
        SEG = [tiles(71, 3)[:, 0:3 * P], tiles(71, 3)[:, 3 * P:6 * P], tiles(61, 2)[:, 0:3 * P]]
        LMASK = tiles3(74, 2)
        I_OF = (8, 9, 10, 11, 76, 77, 78, 79)
        XDT = SQ[:, :, :].rearrange("p (t x) n -> p t (x n)", t=TT)
        DTT = small(112, 32).rearrange("p (t h) -> p t h", t=TT)
        LRU_T = tiles(12, 1)
        PA, PB, MO2 = tiles3(29, 8), tiles3(21, 8), tiles3(13, 8)
        UP, FV = tiles3(0, 48), tiles3(48, FT)
        DO = tiles3(72, 8)
        LRU_W = SQ[:, :, :].rearrange("p (n a) (b c) -> p n (a b) c", n=2, b=2)
        PU2 = JOBS1 + 8
        MID2 = PU2 - D1_BLOCKS
        L_LRU, L_SSM, L_OUT2, L_UP, L_DOWN, L_EVEN, L_OE, L_ODD, L_OO = (
            sum(D2_LAYERS[:n]) for n in range(1, len(D2_LAYERS)))
        PU3 = PU2 + L_DOWN + 8 - L_EVEN
        ROUND = RING * UNITS
        SSD_LEN = 3 * P

        def units_through(unit):
            return MID2 + sum(not block_ends(u) for u in range(unit + 1)) - (2 if unit >= L_EVEN + 15 else 0)

        def pu3(unit):
            return PU3 + unit - (2 if unit >= L_EVEN + 15 else 0)

        def d2_block(unit):
            return D2_BLOCK0 + unit // UNITS

        def tensor_dense2(pe, dense_unit, unit, act, pu, base=None, first=True, last=True):
            if first:
                pe.wait_ge(s.dense_sb, pu - 3)
            dense_unit(d2_block(unit), unit % UNITS, B[pu % 4], *act, D1_UNITS + unit + 1, base, first,
                       last).then_inc(s.ring_used if block_ends(unit) else s.dense_mm, 1)

        def tensor_loop2(pe, dense_unit, start, rounds, act, base):
            with pe.Fori(0, rounds) as r:
                for j in range(ROUND):
                    unit = start + j
                    pe.wait_ge(s.dense_sb, r * ROUND + (PU2 + unit - 3))
                    dense_unit(d2_block(unit), unit % UNITS, B[(PU2 + unit) % 4], *act, D1_UNITS + unit + 1,
                               base=None if j else base, turn=r * ROUND).then_inc(
                        s.ring_used if block_ends(unit) else s.dense_mm, 1)

        def tensor_block2(pe, mm, dense_unit, column_sum, column_sums):
            def unit2(unit, act, name=None):
                tensor_dense2(pe, dense_unit, unit, act, PU2 + unit, base=IN_AT[name][0] if name else None)

            normed = by_tile(HH), by_tile(as_r(H[:, :, :]))

            column_sums(5)
            tensor_loop2(pe, dense_unit, 0, 2, normed, IN_AT["in2"][0])
            unit2(32, normed), unit2(33, normed), unit2(34, normed)
            pe.wait_ge(s.xc_ready, 1)
            pe.wait_ge(s.lru_in, 16)
            for k in range(KT):
                if k >= 4:
                    pe.wait_ge(s.ri_sig, k - 3)
                for n in range(2):
                    last = mm(B[4 + k % 4][:, n * SEQ:(n + 1) * SEQ], LRU_W[:, n, k, :], XC[:, k, :])
                last.then_inc(s.ri_mm, 1)
                if k == 3:
                    unit2(35, normed)
            unit2(36, normed)
            pe.wait_ge(s.ri_sig, KT)
            pe.wait_ge(s.cs_ready, 1)
            for t in range(TT):
                nc.tensor.transpose(B[4][:, t * P:(t + 1) * P], LCUM[:, t * P:(t + 1) * P], ident)
                last = nc.tensor.transpose(B[5][:, t * P:(t + 1) * P], DT[:, t * P:(t + 1) * P], ident)
            last.then_inc(s.ssd_tr, 1)
            pe.wait_ge(s.xbc_silu, 1)
            for g in range(2):
                mm(B[6 + g][:, 0:SEQ], XBC[:, 8 + g, 0:P], XBC[:, 10 + g, :])
                mm(B[6 + g][:, SEQ:SSD_LEN], XBC[:, 8 + g, P:SEQ], XBC[:, 10 + g, P:SEQ]).then_inc(s.cb_mm, 1)
            pe.wait_ge(s.ssd_sb, 1)
            pe.wait_ge(s.cb_ready, 2)
            for n in range(4):
                for q in range(4):
                    t, k = n // 2, 4 * (n % 2) + q
                    last = nc.tensor.transpose(B[4 + n][:, q * P:(q + 1) * P], XBC[:, k, t * P:(t + 1) * P], ident)
                last.then_inc(s.xs_tr, 1)
            unit2(37, normed)

            def spread_decay(h):
                pe.wait_ge(s.lmask_ready, h + 1)
                if h >= 2:
                    pe.wait_ge(s.seg_ready, h - 1)
                bank, lm = B[4 + h % 2], LMASK[:, h % 2, :]
                mm(bank[:, 0:SEQ], con("chunk_rows")[:, 0:P], lm)
                mm(bank[:, SEQ:SSD_LEN], con("chunk_rows")[:, P:2 * P], lm[:, P:SEQ]).then_inc(s.bc_mm, 1)

            pe.wait_ge(s.xdt_ready, 4)
            spread_decay(0), spread_decay(1)
            for h in range(SSM_H):
                if 38 + h < IN2:
                    unit2(38 + h, normed)
                if h + 2 < SSM_H:
                    spread_decay(h + 2)
                pe.wait_ge(s.m_ready, h + 1)
                if h >= 4:
                    pe.wait_ge(s.ya_pair, h // 2 - 1)
                o = B[6 + h // 2 % 2][64 * (h % 2):64 * (h % 2) + 64, 0:SEQ]
                mm(o, XDT[:, 0, h * SSM_P:(h + 1) * SSM_P], SEG[h % 3][:, 0:SEQ], True, False)
                mm(o[:, P:SEQ], XDT[:, 1, h * SSM_P:(h + 1) * SSM_P], SEG[h % 3][:, SEQ:SSD_LEN],
                   False, True).then_inc(s.ssd_y, 1)
            lru = by_tile(as_r(TH)), by_tile(as_r(XC))
            for n in range(4):
                unit2(L_LRU + n, lru, None if n else "lru")
            pe.wait_ge(s.ya_sq, 1)
            for g in range(2):
                for k in range(4):
                    last = mm(B[4 + g][:, 0:SEQ], ones[:], SQ[:, 4 * g + k, :], k == 0, k == 3)
            last.then_inc(s.ya_sum, 1)
            for n in range(4, 8):
                unit2(L_LRU + n, lru)
            ssm = by_tile(as_r(SQ[:, :, :])), by_tile(as_r(YA))
            for n in range(8):
                unit2(L_SSM + n, ssm, None if n else "ssm")
            merged = by_tile(as_r(PB)), by_tile(as_r(PA))
            for n in range(8):
                unit2(L_OUT2 + n, merged, None if n else "merged")
                if n:
                    column_sum(6, n - 1)
            column_sum(6, KT - 1)
            column_sums(7)
            tensor_loop2(pe, dense_unit, L_UP, 3, normed, IN_AT["up"][0])
            high, low = by_tile(as_r(UP[:, 0:2 * FT:2, :])), by_tile(as_r(FV))
            for n in range(KT):
                for kg in range(3):
                    part = slice(KT * kg, KT * kg + KT)
                    tensor_dense2(pe, dense_unit, L_DOWN + 3 * n + kg, (high[part], low[part]), PU2 + L_DOWN + n,
                                  base=None if n else IN_AT["ffn"][0] + KT * kg, first=kg == 0, last=kg == 2)
                if n:
                    column_sum(8, n - 1)
            column_sum(8, KT - 1)

        def scalar_loop2(act, fn, units_done, first, rounds, between=None):
            mids = units_done[0]
            with act.Fori(0, rounds) as r:
                n = 0
                for j in range(ROUND):
                    unit = first + j
                    if block_ends(unit):
                        act.wait_ge(s.ring_used, r * RING + (d2_block(unit) + 1))
                    else:
                        n += 1
                        act.wait_ge(s.dense_mm, r * (ROUND - RING) + (mids + n))
                    at = r * (ROUND * SEQ) + (unit - (0 if first == 0 else L_UP)) * SEQ
                    fn(U[:, bass.ds(at, SEQ)], B[(PU2 + unit) % 4][:, 0:SEQ], ACT.Copy).then_inc(s.dense_sb, 1)
                    blk, sub = d2_block(unit + AHEAD2), unit % UNITS
                    act.wait_ge(ring_loaded[blk % RING], r * 16 + uses(blk))
                    fn(w_high[:, (D1_UNITS + unit) % HIGHS, :], unit_weights(blk, sub), ACT.Copy).then_inc(s.w_high, 1)
                    if between:
                        between(r, j)
            units_done[0] += rounds * (ROUND - RING)

        def scalar_block2(act, fn, link, square, squares_of_x, root_table, root, unit_done, units_done, weight_high, split_high, splits_passed):
            def copy2(unit, dst, tile=None):
                unit_done(d2_block(unit), block_ends(unit))
                if tile is not None:
                    square(tile, B[(PU2 + unit) % 4][:, 0:SEQ])
                fn(dst, B[(PU2 + unit) % 4][:, 0:SEQ], ACT.Copy).then_inc(s.dense_sb, 1)
                if tile != KT - 1:
                    weight_high(D1_UNITS + unit + AHEAD2)

            def soft(x, t):
                link(fn(t, x, ACT.Abs))
                link(fn(t, t, ACT.Exp, scale=-1.0))
                return fn(t, t, ACT.Ln, bias=1.0)

            squares_of_x(s.x_ready, KT)
            root(5)
            act.dma_start(flat(SQ), d["lru_w"]).then_inc(s.lru_in, 16)
            for k in range(KT):
                split_high(HH[:, k, :], H[:, k, :])
            scalar_loop2(act, fn, units_done, 0, 2)
            act.wait_ge(s.dt_in, 1)
            soft(DT, ADT).then_inc(s.dt_soft, 1)
            copy2(32, RAW[:, 32, :])
            act.wait_ge(s.xbc_conv, 1)
            fn(tiles(53, 12), tiles(53, 12), ACT.Silu).then_inc(s.xbc_silu, 1)
            for unit in (33, 34):
                copy2(unit, RAW[:, unit, :])
            for k in range(KT):
                if k == 4:
                    copy2(35, RAW[:, 35, :])
                act.wait_ge(s.ri_mm, k + 1)
                bank = B[4 + k % 4]
                fn(TH[:, k, :], bank[:, 0:SEQ], ACT.Sigmoid, bias=par("lru_br", k, k + 1))
                fn(tiles(I_OF[k], 1), bank[:, SEQ:2 * SEQ], ACT.Sigmoid, bias=par("lru_bi", k, k + 1)).then_inc(s.ri_sig, 1)
            act.wait_ge(s.lam_ready, 1)
            act.wait_ge(s.ri_sig, KT)
            for k in range(KT):
                last = fn(TH[:, k, :], TH[:, k, :], ACT.Tanh, scale=LAMC[:, k:k + 1])
            last.then_inc(s.th_ready, 1)
            copy2(36, RAW[:, 36, :])
            fn(tiles(21, 8), tiles(21, 8), ACT.Gelu_apprx_tanh).then_inc(s.ly_gelu, 1)
            copy2(37, RAW[:, 37, :])
            act.wait_ge(s.lru_neg, 1)
            fn(tiles(0, 8), tiles(0, 8), ACT.Sqrt).then_inc(s.lru_root, 1)

            def decay(h):
                act.wait_ge(s.seg_ready, h + 1)
                fn(SEG[h % 3], SEG[h % 3], ACT.Exp).then_inc(s.seg_exp, 1)

            decay(0), decay(1)
            for h in range(SSM_H):
                if 38 + h < IN2:
                    copy2(38 + h, RAW[:, 38 + h, :])
                if h + 2 < SSM_H:
                    decay(h + 2)
                if h % 2 and h >= 3:
                    split_high(TH[:, h // 2 - 1, :], XC[:, h // 2 - 1, :])
            split_high(TH[:, KT - 1, :], XC[:, KT - 1, :])
            fn(tiles(29, 8), tiles(29, 8), ACT.Silu).then_inc(s.z_silu, 1)
            act.wait_ge(s.dense_sb, PU2 + IN2)

            def gates(first):
                for k in (first, first + 1):
                    fn(GATE[:, k, :], GATE[:, k, :], ACT.Sigmoid, bias=par("gate_b", k, k + 1)).then_inc(s.g_sig, 1)

            for n in range(4):
                copy2(L_LRU + n, PB[:, n, :])
                if n == 2:
                    act.wait_ge(s.ya_gated, 1)
                    fn(flat(SQ), tiles(53, 8), ACT.Square).then_inc(s.ya_sq, 1)
                if n < 3:
                    gates(8 + 2 * n)
            gates(14)
            act.wait_ge(s.ya_inv, 1)
            fn(flat(RS), flat(RS), ACT.Sqrt).then_inc(s.ya_rstd, 1)
            copy2(L_LRU + 4, PB[:, 4, :])
            for k in range(KT):
                split_high(SQ[:, k, :], YA[:, k, :])
            for n in range(5, 8):
                copy2(L_LRU + n, PB[:, n, :])
                gates(2 * (n - 5))
            gates(6)
            for n in range(8):
                copy2(L_SSM + n, PA[:, n, :])
                if n >= 2:
                    split_high(PB[:, n - 2, :], PA[:, n - 2, :])
            for n in range(6, 8):
                split_high(PB[:, n, :], PA[:, n, :])
            for n in range(8):
                copy2(L_OUT2 + n, MO2[:, n, :], tile=n)
                if n == KT - 2:
                    root_table(6)
            root(6)
            weight_high(D1_UNITS + L_UP - 1 + AHEAD2)
            squares_of_x(s.x_ready, 2 * KT)
            root(7)
            for k in range(KT):
                split_high(HH[:, k, :], H[:, k, :])

            def activate(r, j):
                if 4 <= j < 12:
                    act.wait_ge(s.conv_step, r * 48 + 48)
                    tile = U[:, bass.ds(r * (8 * SEQ) + (44 + j) * SEQ, SEQ)]
                    fn(tile, tile, ACT.Gelu_apprx_tanh).then_inc(s.ffn_gelu, 1)
                if 7 <= j < 15:
                    act.wait_ge(s.act_full, r * 8 + tile_count("ffn", j - 7))
                    fn(rounded["work"][:, bass.ds(r * (ROUND * SEQ) + 2 * (j - 7) * SEQ, SEQ)],
                       U[:, bass.ds(r * (8 * SEQ) + (41 + j) * SEQ, SEQ)], ACT.Copy).then_inc(s.act_high, 1)

            scalar_loop2(act, fn, units_done, L_UP, 1)
            scalar_loop2(act, fn, units_done, L_UP + ROUND, 2, activate)
            splits_passed(16)
            for k in range(16, FT + 2):
                if k < FT:
                    act.wait_ge(s.conv_step, 6 * (k + 1))
                    fn(FV[:, k, :], FV[:, k, :], ACT.Gelu_apprx_tanh).then_inc(s.ffn_gelu, 1)
                if k >= 18:
                    split_high(UP[:, 2 * (k - 2), :], FV[:, k - 2, :])
            for n in range(KT):
                for unit in range(L_DOWN + 3 * n, L_DOWN + 3 * n + 3):
                    unit_done(d2_block(unit), block_ends(unit))
                    if unit < L_DOWN + 3 * n + 2:
                        weight_high(D1_UNITS + unit + AHEAD2)
                square(n, B[(PU2 + L_DOWN + n) % 4][:, 0:SEQ])
                fn(DO[:, n, :], B[(PU2 + L_DOWN + n) % 4][:, 0:SEQ], ACT.Copy).then_inc(s.dense_sb, 1)
                if n == KT - 2:
                    root_table(8)
                if n < KT - 1:
                    weight_high(D1_UNITS + unit + AHEAD2)
            root(8)
            weight_high(D1_UNITS + L_EVEN - 1 + AHEAD2)

        def vector_block2(dve, v, link, norm_invert, norm_to, add_normed, split_low, splits_passed):
            norm_invert(5)
            norm_to(5, H, X, par("mix_pre"), HH)

            def conv(n, out_t, src_t, w, b):
                w = par(w, 4 * n, 4 * n + 4)
                dve.wait_ge(s.dense_sb, PU2 + src_t + 1)
                return conv_taps(dve, nc, link, tiles(out_t, 1), tiles(src_t, 1), w, par(b, n, n + 1), 4)

            for n in range(12):
                last = conv(n, 53 + n, n, "ssm_conv_w", "ssm_conv_b")
            last.then_inc(s.xbc_conv, 1)
            dve.wait_ge(s.dense_sb, PU2 + 13)
            v.tensor_scalar(DT, tiles(12, 1), par("dt_bias"), None, ALU.add).then_inc(s.dt_in, 1)
            for n in range(KT):
                last = conv(n, n, 13 + n, "lru_conv_w", "lru_conv_b")
            last.then_inc(s.xc_ready, 1)
            dve.wait_ge(s.dt_soft, 1)
            dve.wait_ge(s.dt_in, 1)
            link(v.scalar_tensor_tensor(out=DT, in0=DT, scalar=0.0, in1=ADT, op0=ALU.max, op1=ALU.add))
            dve.wait_ge(s.a_exp, 1)
            link(v.tensor_scalar(ADT, DT, NEGA, -1.0, ALU.mult, ALU.mult))
            dve.wait_ge(s.late_in, 16)
            link(v.tensor_tensor_scan(LCUM, con("ssd_reset"), ADT, 0.0, ALU.mult, ALU.add))
            for c in range(4):
                r, a, b = slice(32 * c, 32 * c + 32), CHUNK * c, CHUNK * (c + 1)
                link(v.tensor_copy(TOT[r, :], LCUM[r, b - 1:b]))
                last = v.tensor_scalar(LCUM[r, a:b], LCUM[r, a:b], TOT[r, :], None, ALU.subtract)
            last.then_inc(s.cs_ready, 1)
            dve.wait_ge(s.lam_soft, 1)
            link(v.tensor_scalar(LAMC, par("lru_lam"), -1.0, 0.0, ALU.mult, ALU.max))
            link(v.tensor_tensor(LAMC, LAMC, LAMT, ALU.add))
            v.tensor_scalar(LAMC, LAMC, -4.0, None, ALU.mult).then_inc(s.lam_ready, 1)
            dve.wait_ge(s.ssd_tr, 1)
            for t in range(TT):
                for half in range(2):
                    r, at = slice(64 * half, 64 * half + 64), P * t + 64 * t + 32 * half
                    v.tensor_copy(LSH[r, t, :], B[4][r, at:at + SSM_H])
                last = v.tensor_copy(DTT[:, t, :], B[5][:, t * P:t * P + SSM_H])
            last.then_inc(s.ssd_sb, 1)
            dve.wait_ge(s.cs_ready, 1)
            for h in range(2):
                v.tensor_scalar(LMASK[:, h, :], LCUM, con("head_rows")[:, h:h + 1], None, ALU.mult).then_inc(s.lmask_ready, 1)
            for g in range(2):
                dve.wait_ge(s.cb_mm, g + 1)
                v.tensor_tensor(CBM[:, g, :], B[6 + g][:, 0:SSD_LEN], con("causal"), ALU.mult).then_inc(s.cb_ready, 1)
            dve.wait_ge(s.ssd_sb, 1)
            for n in range(4):
                t, part = n // 2, n % 2
                dve.wait_ge(s.xs_tr, n + 1)
                v.tensor_tensor(XDT[:, t, part * 512:(part + 1) * 512].rearrange("p (h c) -> p h c", h=8),
                                B[4 + n][:].rearrange("p (h c) -> p h c", h=8),
                                spread(DTT[:, t, 8 * part:8 * part + 8], 2, SSM_P), ALU.mult).then_inc(s.xdt_ready, 1)

            def segments(h):
                dve.wait_ge(s.bc_mm, h + 1)
                if h >= 3:
                    dve.wait_ge(s.ssd_y, h - 2)
                bank, seg = B[4 + h % 2], SEG[h % 3]
                v.tensor_scalar(seg[:, 0:SEQ], bank[:, 0:SEQ], LSH[:, 0, h:h + 1], 0.0, ALU.subtract, ALU.min)
                v.tensor_scalar(seg[:, SEQ:SSD_LEN], bank[:, SEQ:SSD_LEN], LSH[:, 1, h:h + 1], 0.0,
                                ALU.subtract, ALU.min).then_inc(s.seg_ready, 1)

            def lru_input(k):
                i, th = tiles(I_OF[k], 1), TH[:, k, :]
                link(v.tensor_scalar(LRU_T, th, -1.0, 1.0, ALU.mult, ALU.add))
                link(v.reciprocal(LRU_T, LRU_T))
                v.tensor_tensor(i, i, LRU_T, ALU.mult)

            def lru_scan(k):
                i, th = tiles(I_OF[k], 1), TH[:, k, :]
                if k == 0:
                    dve.wait_ge(s.lru_root, 1)
                    dve.wait_ge(s.ly_gelu, 1)
                link(v.scalar_tensor_tensor(out=th, in0=th, scalar=1.0, in1=LRU_T, op0=ALU.add, op1=ALU.mult))
                link(v.tensor_tensor(i, i, XC[:, k, :], ALU.mult))
                link(v.tensor_tensor_scan(XC[:, k, :], th, i, 0.0, ALU.mult, ALU.add))
                return v.tensor_tensor(XC[:, k, :], XC[:, k, :], LY[:, k, :], ALU.mult)

            def pair_out(n):
                dve.wait_ge(s.ssd_y, 2 * n + 2)
                v.scalar_tensor_tensor(out=YA[:, n, :], in0=YA[:, n, :], scalar=par("ssm_d", n, n + 1),
                                       in1=B[6 + n % 2][:, 0:SEQ], op0=ALU.mult, op1=ALU.add).then_inc(s.ya_pair, 1)

            def mask_decay(h):
                dve.wait_ge(s.bc_mm, h - 1)
                v.tensor_scalar(LMASK[:, h % 2, :], LCUM, con("head_rows")[:, h:h + 1], None, ALU.mult).then_inc(s.lmask_ready, 1)

            dve.wait_ge(s.th_ready, 1)
            dve.wait_ge(s.ri_sig, KT)
            for k in range(KT):
                i = tiles(I_OF[k], 1)
                last = v.tensor_tensor(i, i, XC[:, k, :], ALU.mult)
            link(last)
            v.tensor_scalar(tiles(0, 8), tiles(13, 8), -4.0, None, ALU.mult).then_inc(s.lru_neg, 1)
            segments(0)
            mask_decay(2)
            segments(1)
            for h in range(SSM_H):
                dve.wait_ge(s.seg_exp, h + 1)
                v.tensor_tensor(SEG[h % 3], SEG[h % 3], CBM[:, h // 8, :], ALU.mult).then_inc(s.m_ready, 1)
                if h + 2 < SSM_H:
                    segments(h + 2)
                if h + 3 < SSM_H:
                    mask_decay(h + 3)
                if h % 2 == 0:
                    lru_input(h // 2)
                else:
                    lru_scan(h // 2).then_inc(s.act_full, 1)
                    if h >= 3:
                        split_low(XC[:, h // 2 - 1, :], TH[:, h // 2 - 1, :])
                        pair_out(h // 2 - 1)
            split_low(XC[:, KT - 1, :], TH[:, KT - 1, :])
            pair_out(7)
            dve.wait_ge(s.ya_pair, 8)
            dve.wait_ge(s.z_silu, 1)
            v.tensor_tensor(YA, YA, Z, ALU.mult).then_inc(s.ya_gated, 1)
            dve.wait_ge(s.ya_sum, 1)
            for g in range(2):
                link(v.tensor_scalar(RS[:, g, :], B[4 + g][:, 0:SEQ], 1.0 / 512, EPS, ALU.mult, ALU.add))
            v.reciprocal(flat(RS), flat(RS)).then_inc(s.ya_inv, 1)
            dve.wait_ge(s.ya_gated, 1)
            dve.wait_ge(s.ya_rstd, 1)
            for k in range(KT):
                v.scalar_tensor_tensor(out=YA[:, k, :], in0=YA[:, k, :], scalar=par("ssm_norm", k, k + 1),
                                       in1=RS[:, k // 4, :], op0=ALU.mult, op1=ALU.mult).then_inc(s.act_full, 1)
            for k in range(KT):
                split_low(YA[:, k, :], SQ[:, k, :])
            dve.wait_ge(s.g_sig, 8)
            dve.wait_ge(s.dense_sb, PU2 + L_SSM)
            link(v.tensor_tensor(PB, PB, GATE[:, 8:16, :], ALU.mult))
            for n in range(KT):
                dve.wait_ge(s.g_sig, 8 + n + 1)
                dve.wait_ge(s.dense_sb, PU2 + L_SSM + n + 1)
                link(v.tensor_tensor(PA[:, n, :], PA[:, n, :], GATE[:, n, :], ALU.mult))
                v.tensor_tensor(PA[:, n, :], PA[:, n, :], PB[:, n, :], ALU.add).then_inc(s.act_full, 1)
                if n >= 2:
                    split_low(PA[:, n - 2, :], PB[:, n - 2, :])
            for n in range(KT - 2, KT):
                split_low(PA[:, n, :], PB[:, n, :])
            norm_invert(6)
            dve.wait_ge(s.dense_sb, PU2 + L_UP)
            add_normed(6, MO2, par("mix_post"))
            norm_invert(7)
            norm_to(7, H, X, par("ffn_pre"), HH)
            w_at, b_at = P_AT["ffn_conv_w"][0], P_AT["ffn_conv_b"][0]

            def conv_pair(r, turn, j):
                dve.wait_ge(s.dense_sb, r * ROUND + (PU2 + L_UP + turn * ROUND + 2 * j + 2))
                gate = U[:, bass.ds(r * (ROUND * SEQ) + (turn * ROUND + 2 * j) * SEQ, SEQ)]
                value = U[:, bass.ds(r * (ROUND * SEQ) + (turn * ROUND + 2 * j + 1) * SEQ, SEQ)]
                conved = U[:, bass.ds(r * (8 * SEQ) + (48 + 8 * turn + j) * SEQ, SEQ)]
                for n, (o, src) in enumerate(((conved, gate), (gate, value))):
                    def w(tap):
                        return params[:, bass.ds(r * 48 + (w_at + 48 * turn + 6 * j + 3 * n + tap), 1)]

                    step = 48 * turn + 6 * j + 3 * n
                    if n:
                        dve.wait_ge(s.conv_step, r * 48 + step)
                    v.tensor_scalar(o, src, w(2), params[:, bass.ds(r * 16 + (b_at + 16 * turn + 2 * j + n), 1)],
                                    ALU.mult, ALU.add).then_inc(s.conv_step, 1)
                    for shift in (1, 2):
                        dve.wait_ge(s.conv_step, r * 48 + (step + shift))
                        v.scalar_tensor_tensor(out=o[:, shift:SEQ], in0=src[:, 0:SEQ - shift], scalar=w(2 - shift),
                                               in1=o[:, shift:SEQ], op0=ALU.mult, op1=ALU.add).then_inc(s.conv_step, 1)

            with dve.Fori(0, 1) as r:
                for j in range(8):
                    conv_pair(r, 0, j)
            with dve.Fori(0, 2) as r:
                for j in range(8):
                    conv_pair(r, 1, j)
                    for k in (2 * j - 4, 2 * j - 3):
                        if 0 <= k < 8:
                            dve.wait_ge(s.ffn_gelu, r * 8 + (k + 1))
                            tile = U[:, bass.ds(r * (8 * SEQ) + (48 + k) * SEQ, SEQ)]
                            v.tensor_tensor(tile, tile, U[:, bass.ds(r * (ROUND * SEQ) + 2 * k * SEQ, SEQ)],
                                            ALU.mult).then_inc(s.act_full, 1)
                    for k in (2 * j - 8, 2 * j - 7):
                        if 0 <= k < 8:
                            dve.wait_ge(s.act_high, r * 8 + tile_count("ffn", k))
                            low, high = r * (8 * SEQ) + (48 + k) * SEQ, r * (ROUND * SEQ) + 2 * k * SEQ
                            v.tensor_tensor(rounded["work"][:, bass.ds(low, SEQ)], U[:, bass.ds(low, SEQ)],
                                            rounded["work"][:, bass.ds(high, SEQ)], ALU.subtract).then_inc(s.act_low, 1)
            splits_passed(16)
            for k in range(16, FT + 2):
                if k < FT:
                    dve.wait_ge(s.ffn_gelu, k + 1)
                    v.tensor_tensor(FV[:, k, :], FV[:, k, :], UP[:, 2 * k, :], ALU.mult).then_inc(s.act_full, 1)
                if k >= 18:
                    split_low(FV[:, k - 2, :], UP[:, 2 * (k - 2), :])
            norm_invert(8)
            dve.wait_ge(s.dense_sb, PU2 + L_DOWN + KT)
            add_normed(8, DO, par("ffn_post"))

        DOWNR, AQ, AK, BQ, BK = tiles(0, 1), tiles3(1, 2), tiles3(3, 2), tiles3(5, 4), tiles(9, 1)
        BV_RAW = tiles(10, 1)
        BV = tiles(54, 1).rearrange("p (t c) -> p t c", t=TT)
        AV = tiles(11, 4).rearrange("p (t c) -> p t c", t=TT)
        AG, BG = tiles3(15, 4), tiles3(19, 4)
        EIN = [as_r(tiles(n, 1)) for n in (50, 51, 52, 53, 5, 6, 7, 8)], by_tile(as_r(tiles3(15, 8)))
        LSG, SOFT, CUM = tiles3(23, 2), tiles3(25, 2), tiles3(27, 2)
        EXPB = tiles3(29, 2)
        QH = tiles3(31, 4)
        KE, KP = tiles3(35, 2), tiles3(37, 2)
        KPT = tiles(39, 4).rearrange("p (a t c) -> p a t c", a=2, t=TT)
        ATT = tiles(43, 4).rearrange("p (h t c) -> p h t c", h=4, t=TT)
        STATE = tiles(47, 3).rearrange("p (c n e) -> p c n e", c=3, n=2)
        GO, GR = tiles3(50, 4), tiles3(23, 4)
        LOG = tiles(56, 12).rearrange("p (h j) -> p h j", j=TPITCH)
        BIAS = tiles(68, 12).rearrange("p (h j) -> p h j", j=TPITCH)
        BQH = SQ
        CQ, CK, CG = tiles3(0, 8), tiles3(8, 2), tiles3(12, 8)
        CV = tiles(10, 2).rearrange("p (t c) -> p t c", t=TT)
        CG_HIGH = tiles3(20, 8)
        OIN = by_tile(as_r(CG_HIGH)), by_tile(as_r(CG))
        NCH = SEQ // CHUNK

        def bias_block(kind):
            toep = d["toep"]
            return [bass.AP(toep.tensor, kind * AH * P * TPITCH + first + P - 1,
                            [[TPITCH - 1, P], [P * TPITCH, AH], [1, n]]) for first, n in ((P, P), (0, 2 * P))]

        def load_biases(act, kind):
            first, second = bias_block(kind)
            act.dma_start(BIAS[:, :, 0:P], first).then_inc(s.bias_in, 16)
            act.dma_start(BIAS[:, :, P:3 * P], second).then_inc(s.bias_in, 16)

        def tensor_block3(pe, mm, dense_unit, dense_tokens, column_sum, column_sums):
            normed = by_tile(HH), by_tile(as_r(H[:, :, :]))

            def unit3(unit, act, name=None):
                tensor_dense2(pe, dense_unit, unit, act, pu3(unit), IN_AT[name][0] if name else None)

            def values3(unit, units):
                for t in range(TT):
                    pu = pu3(unit) + t
                    pe.wait_ge(s.dense_sb, pu - 3)
                    dense_tokens(d2_block(unit), unit % UNITS, units, t, B[pu % 4], *normed, D1_UNITS + unit + 1).then_inc(
                        s.ring_used if t == TT - 1 else s.dense_mm, 1)

            column_sums(9)
            def logits(kind, q_of, k_of, heads):
                for h in heads:
                    if h >= 4:
                        pe.wait_ge(s.lg_sb, AH * kind + h - 3)
                    q, k, bank = q_of(h), k_of(h), B[4 + h % 4]
                    mm(bank[:, 0:P], q[:, 0:P], k[:, 0:P])
                    mm(bank[:, P:3 * P], q[:, P:SEQ], k).then_inc(s.lg_mm, 1)

            def turn_probs(kind, heads):
                pe.wait_ge(s.lg_ready, kind + 1)
                for h in heads:
                    if h >= 4:
                        pe.wait_ge(s.pt_sb, AH * kind + h - 3)
                    for j in range(3):
                        last = nc.tensor.transpose(B[4 + h % 4][:, j * P:(j + 1) * P], LOG[:, h, j * P:(j + 1) * P], ident)
                    last.then_inc(s.pt_tr, 1)

            def times_values(kind, v_of, heads_of_tile):
                pe.wait_ge(s.pt_sb, AH * (kind + 1))
                for n, heads in enumerate(heads_of_tile):
                    if n >= 4:
                        pe.wait_ge(s.act_full, tile_count("odd_out", n - 4))
                    rows = P // len(heads)
                    for i, h in enumerate(heads):
                        o = B[4 + n % 4][rows * i:rows * (i + 1), 0:SEQ]
                        mm(o[:, 0:P], v_of(h, 0), LOG[:, h, 0:P], True, False)
                        mm(o[:, P:SEQ], v_of(h, 0), LOG[:, h, P:2 * P], False, False)
                        last = mm(o[:, P:SEQ], v_of(h, 1), LOG[:, h, 2 * P:3 * P], False, True)
                    last.then_inc(s.ao_mm, 1)

            def even(*units):
                for n in units:
                    unit3(L_EVEN + n, normed, None if n else "even")

            even(0, 1)
            pe.wait_ge(s.dense_sb, pu3(L_EVEN) + 1)
            up = par("gla_w_up")
            for n in range(2):
                last = mm(B[4][:, n * SEQ:(n + 1) * SEQ], up[0:16, n * P:(n + 1) * P], DOWNR[0:16, :])
            last.then_inc(s.gl_mm, 1)
            even(2, 3, 4, 5, 6, 7, 8, 9, 10)
            pe.wait_ge(s.kp_ready, 1)
            for t in range(TT):
                for n in range(2):
                    last = nc.tensor.transpose(B[5][:, t * SEQ + n * P:t * SEQ + (n + 1) * P], KP[:, n, t * P:(t + 1) * P], ident)
            last.then_inc(s.kp_tr, 1)
            for h in range(4):
                for t in range(TT):
                    last = mm(B[6 + h // 2][:, (h % 2) * SEQ + t * P:(h % 2) * SEQ + (t + 1) * P],
                              KE[:, h // 2, t * P:(t + 1) * P], QH[:, h, t * P:(t + 1) * P])
                if h % 2:
                    last.then_inc(s.att_mm, 1)
            pe.wait_ge(s.dense_sb, pu3(L_EVEN + 10) + 1)
            for t in range(TT):
                last = nc.tensor.transpose(B[4][:, t * P:(t + 1) * P], BV_RAW[:, t * P:(t + 1) * P], ident)
            last.then_inc(s.bv_tr, 1)
            values3(L_EVEN + 11, 4)
            window = 0, lambda h: BQH[:, h, :], lambda h: BK
            pe.wait_ge(s.kpt_ready, 2)
            pe.wait_ge(s.att_ready, 2)
            pe.wait_ge(s.bv_sb, 1)
            pe.wait_ge(s.bqh_ready, 1)
            logits(*window, range(4))
            even(15)
            logits(*window, range(4, AH))
            even(16)
            pe.wait_ge(s.lg_sb, AH)
            pe.wait_ge(s.dense_sb, pu3(L_EVEN + 15))
            for c in range(NCH - 1):
                for n in range(2):
                    last = mm(B[4 + c][:, n * SEQ:(n + 1) * SEQ], KPT[:, c % 2, c // 2, n * P:(n + 1) * P],
                              AV[:, c // 2, n * SEQ:(n + 1) * SEQ])
                last.then_inc(s.kv_mm, 1)
            even(17, 18)
            pe.wait_ge(s.st_ready, 1)
            for h in range(4):
                o = B[4 + h]
                for t in range(TT):
                    mm(o[:, t * P:(t + 1) * P], AV[:, t, h * P:(h + 1) * P], ATT[:, h, t, :], t == 0, False)
                for c in range(1, NCH):
                    last = mm(o[:, c * CHUNK:(c + 1) * CHUNK], STATE[:, c - 1, h // 2, :], QH[:, h, c * CHUNK:(c + 1) * CHUNK],
                              False, c == NCH - 1)
                last.then_inc(s.o_mm, 1)
            even(19)
            pe.wait_ge(s.o_sq, 4)
            pe.wait_ge(s.o_sb, 4)
            for n in range(2):
                mm(B[4 + n][:], ones[:], tiles(43 + 2 * n, 2)).then_inc(s.o_sum, 1)
            even(20)
            pe.wait_ge(s.o_mean, 2)
            turn_probs(0, range(4))
            even(21)
            turn_probs(0, range(4, AH))
            even(22)
            times_values(0, lambda h, t: BV[:, t, 64 * (h // 4):64 * (h // 4) + 64], [(n, n + 4) for n in range(4)])
            for n in range(8):
                unit3(L_OE + n, EIN, name=None if n else "even_out")
                if n > 1:
                    column_sum(10, n - 2)
            column_sum(10, KT - 2)
            column_sum(10, KT - 1)

            def odd(*units):
                for n in units:
                    unit3(L_ODD + n, normed, None if n else "odd")

            causal = 1, lambda h: CQ[:, h, :], lambda h: CK[:, h // 4, :]
            odd(*range(10))
            pe.wait_ge(s.dense_sb, pu3(L_ODD + 9) + 1)
            logits(*causal, range(4))
            values3(L_ODD + 10, 2)
            logits(*causal, range(4, AH))
            odd(*range(12, 19))
            turn_probs(1, range(4))
            odd(19)
            turn_probs(1, range(4, AH))
            times_values(1, lambda h, t: CV[:, t, P * (h // 4):P * (h // 4) + P], [(n,) for n in range(AH)])
            for n in range(8):
                unit3(L_OO + n, OIN, name=None if n else "odd_out")
                if n > 1:
                    column_sum(11, n - 2)
            column_sum(11, KT - 2)
            column_sum(11, KT - 1)

        def scalar_block3(act, fn, link, squares_of_x, root_table, root, unit_done, weight_high, split_high):
            def copy3(unit, dst):
                unit_done(d2_block(unit), block_ends(unit))
                fn(dst, B[pu3(unit) % 4][:, 0:SEQ], ACT.Copy).then_inc(s.dense_sb, 1)
                weight_high(D1_UNITS + unit + AHEAD2)

            def copy_values3(unit, units, dst):
                for t in range(TT):
                    unit_done(d2_block(unit), t == TT - 1)
                    fn(dst[:, t, :], B[(pu3(unit) + t) % 4][:, 0:units * P], ACT.Copy).then_inc(s.dense_sb, 1)
                for n in range(units):
                    weight_high(D1_UNITS + unit + n + AHEAD2)

            squares_of_x(s.x_ready, 3 * KT)
            load_biases(act, 0)
            root(9)
            for k in range(KT):
                split_high(HH[:, k, :], H[:, k, :])
            def even(*units):
                for n in units:
                    copy3(L_EVEN + n, tiles(n, 1))

            def exp_scores(kind):
                act.wait_ge(s.lg_shift, kind + 1)
                if kind == 0:
                    fn(ASNK, ASNK, ACT.Exp)
                fn(tiles(56, 12), tiles(56, 12), ACT.Exp).then_inc(s.lg_exp, 1)

            def copy_probs(kind, heads):
                for h in heads:
                    act.wait_ge(s.pt_tr, AH * kind + h + 1)
                    fn(LOG[:, h, :], B[4 + h % 4][:, 0:3 * P], ACT.Copy).then_inc(s.pt_sb, 1)

            flat2 = lambda a: tiles(a, 2)
            even(0, 1)
            act.wait_ge(s.gl_in, 1)
            link(fn(flat2(25), flat2(23), ACT.Abs))
            link(fn(flat2(25), flat2(25), ACT.Exp, scale=-1.0))
            fn(flat2(25), flat2(25), ACT.Ln, bias=1.0).then_inc(s.gl_soft, 1)
            even(2, 3)
            act.wait_ge(s.gl_b, 1)
            fn(flat2(29), flat2(27), ACT.Exp).then_inc(s.gl_exp, 1)
            fn(flat2(35), flat2(27), ACT.Exp, scale=-1.0).then_inc(s.gl_exp, 1)
            fn(DEC, CUM.rearrange("p n (c t) -> p n c t", t=CHUNK)[:, :, :, CHUNK - 1], ACT.Exp).then_inc(s.gl_exp, 1)
            act.wait_ge(s.gl_left, 1)
            fn(flat2(37), flat2(37), ACT.Exp).then_inc(s.gl_exp, 1)
            even(*range(4, 11))
            act.wait_ge(s.bv_tr, 1)
            fn(BV.rearrange("p t c -> p (t c)"), B[4][:, 0:SEQ], ACT.Copy).then_inc(s.bv_sb, 1)
            copy_values3(L_EVEN + 11, 4, AV)
            even(15, 16, 17, 18)
            exp_scores(0)
            load_biases(act, 1)
            for h in range(4):
                act.wait_ge(s.o_mm, h + 1)
                fn(tiles(43 + h, 1), B[4 + h][:, 0:SEQ], ACT.Square).then_inc(s.o_sq, 1)
                fn(GO[:, h, :], B[4 + h][:, 0:SEQ], ACT.Copy).then_inc(s.o_sb, 1)
            even(19)
            act.wait_ge(s.dense_sb, pu3(L_EVEN + 18) + 1)
            fn(tiles(15, 4), tiles(15, 4), ACT.Silu).then_inc(s.eg_silu, 1)
            even(20)
            copy_probs(0, range(4))
            even(21)
            copy_probs(0, range(4, AH))
            act.wait_ge(s.oa_var, 1)
            fn(tiles(23, 4), tiles(23, 4), ACT.Sqrt).then_inc(s.o_rstd, 1)
            even(22)
            act.wait_ge(s.dense_sb, pu3(L_EVEN + 22) + 1)
            fn(tiles(19, 4), tiles(19, 4), ACT.Silu).then_inc(s.eg_silu, 1)
            for n in range(4):
                split_high(GO[:, n, :], AG[:, n, :])
            for n in range(4):
                split_high(tiles(5 + n, 1), BG[:, n, :])

            def added(norm, first, n):
                unit_done(d2_block(first + n), block_ends(first + n))
                weight_high(D1_UNITS + first + n + AHEAD2)
                if n == KT - 2:
                    root_table(norm)

            squares_of_x(s.dense_sb, pu3(L_OE), lambda n: added(10, L_OE, n))
            root(10)
            for k in range(KT):
                split_high(HH[:, k, :], H[:, k, :])
            def odd(*units):
                for n in units:
                    copy3(L_ODD + n, tiles(n, 1))

            def silu_odd(a):
                act.wait_ge(s.dense_sb, pu3(L_ODD + a + 3) + 1)
                fn(tiles(a, 4), tiles(a, 4), ACT.Silu).then_inc(s.eg_silu, 1)

            odd(*range(10))
            copy_values3(L_ODD + 10, 2, CV)
            odd(12, 13)
            exp_scores(1)
            odd(14, 15, 16, 17)
            silu_odd(12)
            odd(18)
            copy_probs(1, range(4))
            odd(19)
            copy_probs(1, range(4, AH))
            silu_odd(16)
            for n in range(AH):
                split_high(CG_HIGH[:, n, :], CG[:, n, :])
            squares_of_x(s.dense_sb, pu3(L_OO), lambda n: added(11, L_OO, n))
            root(11)

        def vector_block3(dve, v, link, norm_invert, norm_to, final_norm, split_low):
            def add_unit(unit, n):
                if block_ends(unit):
                    dve.wait_ge(s.ring_used, d2_block(unit) + 1)
                else:
                    dve.wait_ge(s.dense_mm, units_through(unit))
                v.tensor_tensor(X[:, n, :], X[:, n, :], B[pu3(unit) % 4][:, 0:SEQ], ALU.add).then_inc(s.dense_sb, 1)

            norm_invert(9)
            norm_to(9, H, X, par("norm_gain", 0, 8), HH)
            dve.wait_ge(s.gl_mm, 1)
            for n in range(2):
                last = v.tensor_scalar(LSG[:, n, :], B[4][:, n * SEQ:(n + 1) * SEQ], par("gla_b_up", n, n + 1), None, ALU.add)
            last.then_inc(s.gl_in, 1)
            dve.wait_ge(s.gl_soft, 1)
            dve.wait_ge(s.gl_in, 1)
            link(v.scalar_tensor_tensor(out=LSG, in0=LSG, scalar=0.0, in1=SOFT, op0=ALU.min, op1=ALU.subtract))
            link(v.tensor_scalar(LSG, LSG, 1.0 / 16.0, None, ALU.mult))
            for n in range(2):
                last = v.tensor_tensor_scan(CUM[:, n, :], con("gla_reset"), LSG[:, n, :], 0.0, ALU.mult, ALU.add)
            last.then_inc(s.gl_b, 1)
            dve.wait_ge(s.gl_b, 1)
            by_chunk = lambda ap: ap.rearrange("p n (c t) -> p (n c) t", t=CHUNK)
            cum = by_chunk(CUM)
            v.tensor_tensor(by_chunk(KP), spread(cum[:, :, CHUNK - 1], 2, CHUNK), cum, ALU.subtract).then_inc(s.gl_left, 1)
            dve.wait_ge(s.gl_exp, 2)
            dve.wait_ge(s.dense_sb, pu3(L_EVEN + 4) + 1)
            link(v.scalar_tensor_tensor(out=EXPB, in0=AQ, scalar=float(64) ** -0.5, in1=EXPB, op0=ALU.mult, op1=ALU.mult))
            for h in range(4):
                v.tensor_scalar(QH[:, h, :], EXPB[:, h // 2, :], con("half")[:, h % 2:h % 2 + 1], None, ALU.mult)
            v.tensor_tensor(KE, KE, AK, ALU.mult)
            dve.wait_ge(s.gl_exp, 4)
            v.tensor_tensor(KP, KP, AK, ALU.mult).then_inc(s.kp_ready, 1)
            dve.wait_ge(s.dense_sb, pu3(L_EVEN + 8) + 1)
            for h in range(AH):
                last = v.tensor_scalar(BQH[:, h, :], BQ[:, h % 4, :], con("half")[:, h // 4:h // 4 + 1], None, ALU.mult)
            last.then_inc(s.bqh_ready, 1)
            dve.wait_ge(s.kp_tr, 1)
            for a in range(2):
                v.tensor_scalar(KPT[:, a].rearrange("p t c -> p (t c)"), B[5][:], con("half")[:, a:a + 1], None,
                                ALU.mult).then_inc(s.kpt_ready, 1)
            mask = spread(spread(con("gla_mask"), 1, TT), 1, 2)
            for n in range(2):
                dve.wait_ge(s.att_mm, n + 1)
                a = ATT[:, 2 * n:2 * n + 2]
                link(v.tensor_scalar(a.rearrange("p h t c -> p (h t c)"), B[6 + n][:], 3e38, -3e38, ALU.min, ALU.max))
                v.tensor_tensor(a, a, mask, ALU.mult).then_inc(s.att_ready, 1)
            parts = LOG[:, :, 0:P], LOG[:, :, P:3 * P]

            def shift_scores(kind, scale):
                dve.wait_ge(s.bias_in, 32 * (kind + 1))
                for h in range(AH):
                    dve.wait_ge(s.lg_mm, AH * kind + h + 1)
                    v.scalar_tensor_tensor(out=LOG[:, h, :], in0=B[4 + h % 4][:, 0:3 * P], scalar=scale, in1=BIAS[:, h, :],
                                           op0=ALU.mult, op1=ALU.add).then_inc(s.lg_sb, 1)
                dve.wait_ge(s.lg_sb, AH * (kind + 1))
                for b in range(2):
                    last = v.tensor_reduce(AMAX[:, :, b], parts[b], AXX, ALU.max)
                link(last)
                if kind == 0:
                    sinks = spread(par("sinks"), 2, 2)
                    link(v.tensor_tensor(AMAX, AMAX, sinks, ALU.max))
                    v.tensor_tensor(ASNK, sinks, AMAX, ALU.subtract)
                for b in range(2):
                    last = v.tensor_tensor(parts[b], parts[b], spread(AMAX[:, :, b], 2, (b + 1) * P), ALU.subtract)
                last.then_inc(s.lg_shift, 1)

            def normalise(kind):
                dve.wait_ge(s.lg_exp, kind + 1)
                for b in range(2):
                    last = v.tensor_reduce(ASUM[:, :, b], parts[b], AXX, ALU.add)
                link(last)
                if kind == 0:
                    link(v.tensor_tensor(ASUM, ASUM, ASNK, ALU.add))
                link(v.reciprocal(ASUM, ASUM))
                for b in range(2):
                    last = v.tensor_tensor(parts[b], parts[b], spread(ASUM[:, :, b], 2, (b + 1) * P), ALU.mult)
                last.then_inc(s.lg_ready, 1)

            shift_scores(0, float(64) ** -0.5)
            for c in range(NCH - 1):
                dve.wait_ge(s.kv_mm, c + 1)
                for n in range(2):
                    for half in range(2):
                        r = slice(64 * half, 64 * half + 64)
                        own = B[4 + c][r, n * SEQ + half * P:n * SEQ + (half + 1) * P]
                        if c == 0:
                            last = v.tensor_copy(STATE[r, 0, n, :], own)
                        else:
                            last = v.scalar_tensor_tensor(out=STATE[r, c, n, :], in0=STATE[r, c - 1, n, :],
                                                          scalar=DEC[r, n, c:c + 1], in1=own, op0=ALU.mult, op1=ALU.add)
                if c < NCH - 2:
                    link(last)
            last.then_inc(s.st_ready, 1)
            normalise(0)
            for n in range(2):
                dve.wait_ge(s.o_sum, n + 1)
                v.tensor_scalar(tiles(23 + 2 * n, 2), B[4 + n][:], 1.0 / P, EPS, ALU.mult, ALU.add).then_inc(s.o_mean, 1)
            dve.wait_ge(s.o_mean, 2)
            v.reciprocal(tiles(23, 4), tiles(23, 4)).then_inc(s.oa_var, 1)
            dve.wait_ge(s.o_rstd, 1)
            dve.wait_ge(s.eg_silu, 1)
            link(v.scalar_tensor_tensor(out=GO, in0=GO, scalar=par("gla_gain"), in1=GR, op0=ALU.mult, op1=ALU.mult))
            for n in range(4):
                v.tensor_tensor(AG[:, n, :], GO[:, n, :], AG[:, n, :], ALU.mult).then_inc(s.act_full, 1)
            for n in range(4):
                split_low(AG[:, n, :], GO[:, n, :])

            dve.wait_ge(s.eg_silu, 2)
            for n in range(4):
                dve.wait_ge(s.ao_mm, n + 1)
                v.tensor_tensor(BG[:, n, :], B[4 + n][:, 0:SEQ], BG[:, n, :], ALU.mult).then_inc(s.act_full, 1)
            for n in range(4):
                split_low(BG[:, n, :], tiles(5 + n, 1))
            for n in range(8):
                add_unit(L_OE + n, n)
            norm_invert(10)
            norm_to(10, H, X, par("norm_gain", 8, 16), HH)
            shift_scores(1, float(P) ** -0.5)
            normalise(1)
            for n in range(AH):
                dve.wait_ge(s.eg_silu, 3 + n // 4)
                dve.wait_ge(s.ao_mm, 4 + n + 1)
                v.tensor_tensor(CG[:, n, :], B[4 + n % 4][:, 0:SEQ], CG[:, n, :], ALU.mult).then_inc(s.act_full, 1)
                if n:
                    split_low(CG[:, n - 1, :], CG_HIGH[:, n - 1, :])
            split_low(CG[:, AH - 1, :], CG_HIGH[:, AH - 1, :])
            for n in range(8):
                add_unit(L_OO + n, n)
            norm_invert(11)
            final_norm(11, par("final_gain"))

        block = ctx.enter_context(nc.Block())

        @block.sync
        def _(sp):
            def load(block_no, src, wait=True):
                if wait and block_no >= RING:
                    sp.wait_ge(s.ring_used, block_no - RING + 1)
                sp.dma_start(ring[:, block_no % RING, :].rearrange("p (a n) -> p a n", a=src.shape[1]),
                             src).then_inc(ring_loaded[block_no % RING], 16)

            ada = d["w_ada"].rearrange("(k p) n -> p k n", p=P)
            for at, (kind, b) in enumerate(FIRST):
                r, k = b // 4, 2 * (b % 4)
                if (kind, b) == ("dense", 0):
                    sp.wait_ge(s.ring_used, at - RING + 1)
                    for half in range(2):
                        cols = slice(half * BLK // 2, (half + 1) * BLK // 2)
                        sp.dma_start(ring[:, at % RING, cols], d["dense1"][b][:, cols]).then_inc(
                            ring_loaded[at % RING] if half else s.first_units, 16)
                    continue
                load(at, ada[:, k:k + 2, r * DEXP:(r + 1) * DEXP] if kind == "ada"
                     else d["dense1"][b].rearrange("p (a n) -> p a n", a=1))
            rows = EXPERTS * DM
            gate = d["w_gate"].rearrange("(k p) n -> p k n", p=P)
            up = d["w_up"].rearrange("(k p) n -> p k n", p=P)
            down = d["w_down"].rearrange("(e j c p) n -> e c p j n", e=EXPERTS, j=4, c=4)
            def expert_source(e, b):
                if b < 4:
                    return gate[:, bass.ds(e * KT + 2 * b, 2), :]
                if b < 8:
                    return up[:, bass.ds(e * KT + 2 * (b - 4), 2), :]
                return down[bass.ds(e, 1), b - 8].rearrange("e p j n -> p (e j) n")

            in_ring = [b for b in range(EXP_BLOCKS) if b not in EXTRA]
            for b in in_ring[:RING]:
                load(first_expert_block(b), expert_source(0, b))
            sp.wait_ge(s.ring_used, EXP_BLOCK0)
            for b, halves in zip(EXTRA, AHEAD):
                for kk in range(2):
                    if halves[kk] is AHEAD[2][1]:
                        sp.wait_ge(s.x_ready, KT)
                    if halves[kk] is squares:
                        sp.wait_ge(s.norm_summed, 4)
                    if halves[kk] is h_normed:
                        sp.wait_ge(s.ht_tr, 4)
                    sp.dma_start(halves[kk], expert_source(0, b)[:, kk, :]).then_inc(s.extra_in, 16)
            for b in in_ring[RING:]:
                load(first_expert_block(b), expert_source(0, b))
            with sp.Fori(1, EXPERTS) as e:
                for b in range(EXP_BLOCKS):
                    sp.wait_ge(s.ring_used, e * EXP_BLOCKS + (EXP_BASE + b - RING + 1))
                    src = expert_source(e, b)
                    slot = (EXP_BASE + b) % RING
                    sp.dma_start(ring[:, slot, :].rearrange("p (a n) -> p a n", a=src.shape[1]),
                                 src).then_inc(ring_loaded[slot], 16)
            with sp.Fori(0, D2_BLOCKS // RING) as r:
                for b in range(RING):
                    sp.wait_ge(s.ring_used, r * RING + (D2_BLOCK0 + b - RING + 1))
                    slot = (D2_BLOCK0 + b) % RING
                    sp.dma_start(ring[:, slot, :], d["dense2"][bass.ds(r * RING + b, 1)]
                                 .rearrange("b p n -> p (b n)")).then_inc(ring_loaded[slot], 16)
            for q in range(4):
                sp.wait_ge(s.out_ready, 2 * q + 2)
                sp.dma_start(out[:, 2 * q:2 * q + 2, :], X[:, 2 * q:2 * q + 2, :]).then_inc(s.out_stored, 16)
            sp.wait_ge(s.out_stored, 64)

        @block.gpsimd
        def _(pool):
            def low(block_no, sub, buffer):
                w = unit_weights(block_no, sub)
                nc.gpsimd.tensor_tensor(as_r(w), w, w_high[:, buffer, :], ALU.subtract).then_inc(s.w_low, 1)

            for unit in range(D1_UNITS):
                pool.wait_ge(s.w_high, unit + 1)
                low(d1_block(unit), unit % UNITS, unit % HIGHS)
            for n in range(4):
                pool.wait_ge(s.ht_sb, n + 1)
                ht, high = (part[:, n // 2, (n % 2) * 512:(n % 2 + 1) * 512] for part in (HT, HT_HIGH))
                nc.gpsimd.tensor_tensor(as_r(ht), ht, as_r(high), ALU.subtract).then_inc(s.ht_low, 1)
            with pool.Fori(0, D2_BLOCKS // RING) as r:
                for j in range(RING * UNITS):
                    pool.wait_ge(s.w_high, r * (RING * UNITS) + (D1_UNITS + j + 1))
                    low(D2_BLOCK0 + j // UNITS, j % UNITS, (D1_UNITS + j) % HIGHS)

        @block.tensor
        def _(pe):
            def mm(o, lhsT, rhs, start=True, stop=True):
                return nc.tensor.matmul(o, lhsT, rhs, start=start, stop=stop)

            def arrived(block_no):
                pe.wait_ge(ring_loaded[block_no % RING], uses(block_no))

            def dense_unit(block_no, sub, bank, high, low, counts, base=None, first=True, last=True, turn=None):
                buffer = w_high[:, (counts - 1) % HIGHS, :]
                if turn is not None:
                    counts = turn + counts
                parts = [("hh", buffer, high), ("lh", None, high), ("hl", buffer, low)]
                if base is None:
                    parts[1:] = parts[:0:-1]
                pe.wait_ge(s.w_high, counts)
                for n, (part, w, act) in enumerate(parts):
                    if part == "lh":
                        pe.wait_ge(s.w_low, counts)
                    for k in range(KT):
                        if base is not None and part != "lh":
                            pe.wait_ge(s.act_high if part == "hh" else s.act_low, base + k + 1)
                        wk = as_r(weights(block_no, sub, k)) if w is None else w[:, k * P:(k + 1) * P]
                        ins = mm(bank[:, 0:SEQ], wk, act[k], first and n == 0 and k == 0, last and n == 2 and k == KT - 1)
                return ins

            def dense_tokens(block_no, sub, units, t, bank, high, low, counts, base=None):
                spot = slice(t * P, (t + 1) * P)
                buffer = (counts - 1) % HIGHS
                by_unit = lambda ap: ap.rearrange("p (u k c) -> p u k c", u=units, k=KT)
                w_hi = by_unit(w_high[:, buffer:buffer + units, :].rearrange("p u n -> p (u n)"))
                w_lo = as_r(by_unit(ring[:, block_no % RING, sub * KT * P:(sub + units) * KT * P]))
                out = bank[:, 0:units * P].rearrange("p (u c) -> p u c", u=units)
                for n, (w, act) in enumerate(((w_hi, high), (w_hi, low), (w_lo, high))):
                    pe.wait_ge(s.w_low if n == 2 else s.w_high, counts + units - 1)
                    for k in range(KT):
                        if base is not None and n < 2:
                            pe.wait_ge(s.act_low if n else s.act_high, base + k + 1)
                        ins = mm(out, act[k][:, spot], w[:, :, k, :], n == 0 and k == 0, n == 2 and k == KT - 1)
                return ins

            def column_sum(i, k, bank=7):
                pe.wait_ge(s.norm_squared, KT * i + k + 1)
                if i and k == 0:
                    pe.wait_ge(s.norm_root, i)
                last = mm(B[bank][:, 0:SEQ], ones[:], SQ[:, k, :], k == 0, k == KT - 1)
                if k == KT - 1:
                    last.then_inc(s.norm_summed, 1)

            def column_sums(i, bank=7):
                for k in range(KT):
                    column_sum(i, k, bank)

            def ada_block_product(n):
                r, b = n // 4, n % 4
                slot = ada_block(n)
                arrived(slot)
                for kk in range(2):
                    k = 2 * b + kk
                    for j in range(4):
                        at = kk * DEXP + j * 512
                        last = mm(B[ADA_BANK[r]][32 * j:32 * j + 32, :], C2[:, k, :], ring[:, slot % RING, at:at + 512],
                                  k == 0, k == KT - 1)
                last.then_inc(s.ring_used, 1)

            def ada_transpose(r):
                pe.wait_ge(s.ada_sb, r + 1)
                for q in range(4):
                    last = nc.tensor.transpose(B[ADA_BANK[r] + 1][:, q * P:(q + 1) * P], ADA[r][:, q * P:(q + 1) * P], ident)
                last.then_inc(s.ada_tr, 1)

            pe.wait_ge(s.c_ready, 1)
            pe.wait_ge(s.ones_ready, 1)
            ada_block_product(0)
            ada_block_product(1)
            column_sums(0)
            ada_block_product(2)
            column_sums(1)
            ada_block_product(3)
            pe.wait_ge(s.consts_in, 16)
            ada_transpose(0)

            def context_states():
                pe.wait_ge(s.kw_ready, 2)
                pe.wait_ge(s.qk_rot, 4)
                for a in range(2):
                    for h in range(HEADS1):
                        for t in range(TT):
                            last = mm(B[6 + a][:, h * P:(h + 1) * P], KW[:, a, t, h * P:(h + 1) * P],
                                      VC[:, t, h * P:(h + 1) * P], t == 0, t == TT - 1)
                    last.then_inc(s.state_mm, 1)

            def scores(h):
                for m in range(TT):
                    last = mm(B[SCORE_BANK[h]][:, m * SEQ:(m + 1) * SEQ], KQR[:, h, m * P:(m + 1) * P], KQR[:, 4 + h, :])
                last.then_inc(s.score_mm, 1)

            def retention(h):
                pe.wait_ge(s.sd_ready, h + 1)
                bank = B[SCORE_BANK[h]][:, 0:SEQ]
                for m in range(TT):
                    mm(bank, VX[:, m, h * P:(h + 1) * P], DM_[:, h, m, :], m == 0, False)
                mm(bank, SFB[:, 0, h, :], QFB[:, h, :], False, False)
                mm(bank, SFB[:, 1, h, :], QFB[:, 4 + h, :], False, True).then_inc(s.y_mm, 1)

            pe.wait_ge(s.mod_ready, 1)
            for pu, (unit, act, t) in enumerate(DENSE1):
                if pu >= 4:
                    pe.wait_ge(s.dense_sb, pu - 3)
                blk, sub = d1_block(unit), unit % UNITS
                high, low = (HH, H[:, :, :]) if act == "x" else (as_r(CTXR), HC)
                high, low = by_tile(high), by_tile(as_r(low))
                base = IN_AT[act][0] if pu in (0, TT) else None
                if t is None:
                    last = dense_unit(blk, sub, B[pu % 4], high, low, unit + 1, base)
                else:
                    last = dense_tokens(blk, sub, UNITS, t, B[pu % 4], high, low, unit + 1, base)
                last.then_inc(s.ring_used if job_ends(unit, act, t) else s.dense_mm, 1)
                if pu == 1:
                    pe.wait_ge(s.start_in, 16)
                    for kind in range(2):
                        mm(B[4 + kind][0:AH, 0:TOEP], par("rel")[0:REL_BUCKETS + 1, :],
                           start_con("buckets")[0:REL_BUCKETS + 1, kind * TOEP:(kind + 1) * TOEP]).then_inc(s.toep_mm, 1)
                if pu in ADA_AFTER:
                    for b in ADA_AFTER[pu]:
                        if b == 4:
                            pe.wait_ge(s.toep_sb, 2)
                        if b == 8:
                            pe.wait_ge(s.ada_sb, 2)
                        ada_block_product(b)
                if pu == 14:
                    ada_transpose(1)
                if pu in (15, 16, 17):
                    pe.wait_ge(s.dense_sb, 14)
                    for i in {15: (0, 1), 16: (2,), 17: (3,)}[pu]:
                        if i >= 2:
                            pe.wait_ge(s.qk_rot, i - 1)
                        mm(B[6 + i % 2][:], con("swap"), tiles(16 + 2 * i, 2)).then_inc(s.rot_mm, 1)
                if pu == STATES_AFTER:
                    context_states()
                if pu == STATES_AFTER + 1:
                    pe.wait_ge(s.state_sb, 2)
                    scores(0)
                    scores(1)
                if pu == STATES_AFTER + 2:
                    pe.wait_ge(s.qfb_ready, 1)
                    retention(0)
                    retention(1)
                if pu == STATES_AFTER + 3:
                    pe.wait_ge(s.y_sb, 2)
                    scores(2)
                    scores(3)
                if pu == STATES_AFTER + 4:
                    retention(2)
                    retention(3)
                if pu == STATES_AFTER + 5:
                    pe.wait_ge(s.y_sb, 4)
                    for i in range(2):
                        mm(B[6 + i][:], ones[:], tiles(16 + 2 * i, 2)).then_inc(s.mean_mm, 1)
                if pu == STATES_AFTER + 6:
                    pe.wait_ge(s.ysq_ready, 1)
                    for i in range(2):
                        mm(B[6 + i][:], ones[:], tiles(16 + 2 * i, 2)).then_inc(s.var_mm, 1)

            for i in range(8):
                pu, unit = JOBS1 + i, 28 + i
                pe.wait_ge(s.dense_sb, pu - 3)
                blk, sub = d1_block(unit), unit % UNITS
                last = dense_unit(blk, sub, B[pu % 4], by_tile(as_r(MIX_HIGH)), by_tile(as_r(MIX)), unit + 1,
                                  base=None if i else IN_AT["mix"][0])
                last.then_inc(s.ring_used if block_ends(unit) else s.dense_mm, 1)
                if i:
                    column_sum(2, i - 1)
                if i == 1:
                    ada_transpose(2)
            column_sum(2, KT - 1)
            column_sums(3)

            wr = par("w_router").rearrange("p (k e) -> p k e", k=KT)
            for k in range(KT):
                pe.wait_ge(s.h2_ready, k + 1)
                for t in range(TT):
                    last = mm(B[4 + t][:, 0:EXPERTS], H[:, k, t * P:(t + 1) * P], wr[:, k, :], k == 0, k == KT - 1)
            last.then_inc(s.router_mm, 1)
            pe.wait_ge(s.dense_sb, JOBS1 + 8)
            for n in range(4):
                for q in range(4):
                    t, k = n // 2, 4 * (n % 2) + q
                    last = nc.tensor.transpose(B[n][:, q * P:(q + 1) * P], H[:, k, t * P:(t + 1) * P], ident)
                last.then_inc(s.ht_tr, 1)
            pe.wait_ge(s.aff_ready, 1)
            for t in range(TT):
                last = nc.tensor.transpose(B[7][0:EXPERTS, t * P:(t + 1) * P], LOGIT[:, t, :], ident)
            last.then_inc(s.aff_tr, 1)
            def clear(q):
                mm(B[4 + q][:], ZERO[0:1, 0:P], ZERO[0:1, :], True, False)

            clear(0)
            clear(1)
            pe.wait_ge(s.topk_ready, 1)
            mm(B[6][:], as_r(ONES_R[0:EXPERTS, :]), as_r(R16[0:EXPERTS, :])).then_inc(s.slot_mm, 1)
            mm(B[7][:, 0:EXPERTS], IDX4[0:EXPERTS, :], ident[0:EXPERTS, 0:EXPERTS])
            mm(B[7][:, EXPERTS:2 * EXPERTS], VAL4[0:EXPERTS, :], ident[0:EXPERTS, 0:EXPERTS]).then_inc(s.slot_mm, 1)
            pe.wait_ge(s.sel_ready, 1)
            pe.wait_ge(s.ht_low, 4)
            for k in range(KT):
                if k >= 4:
                    pe.wait_ge(s.xs_sb, k - 3)
                for part in (HT_HIGH, HT):
                    for t in range(TT):
                        last = mm(B[k % 4][:], as_r(part[:, t, k * P:(k + 1) * P]), as_r(SEL[:, t, :]),
                                  part is HT_HIGH and t == 0, part is HT and t == TT - 1)
                last.then_inc(s.xs_mm, 1)

            pe.wait_ge(s.slots_ready, 1)
            clear(2)
            clear(3)
            pe.wait_ge(s.xs_sb, KT)
            def expert(e):
                def expert_block(b):
                    if isinstance(e, int):
                        if b in EXTRA:
                            pe.wait_ge(s.extra_in, 32 * len(EXTRA))
                            return AHEAD[EXTRA.index(b)]
                        blk = first_expert_block(b)
                        pe.wait_ge(ring_loaded[blk % RING], uses(blk))
                    else:
                        blk = EXP_BASE + b
                        pe.wait_ge(ring_loaded[blk % RING], e * (16 * EXP_BLOCKS // RING) + uses(blk))
                    return ring[:, blk % RING, 0:DEXP], ring[:, blk % RING, DEXP:2 * DEXP]

                pe.wait_ge(s.xse_ready, e + 1)
                for half, bank in ((0, B[0]), (1, B[1])):
                    for b in range(4):
                        block_in = expert_block(4 * half + b)
                        for kk in range(2):
                            k = 2 * b + kk
                            for j in range(4):
                                last = mm(bank[32 * j:32 * j + 32, :], XSE[:, k, :], block_in[kk][:, j * 512:(j + 1) * 512],
                                          k == 0, k == KT - 1)
                        if not (isinstance(e, int) and 4 * half + b in EXTRA):
                            last.then_inc(s.ring_used, 1)
                pe.wait_ge(s.hid_ready, e + 1)
                for q in range(4):
                    last = nc.tensor.transpose(B[0][:, q * P:(q + 1) * P], HID[:, q * P:(q + 1) * P], ident)
                last.then_inc(s.hid_tr, 1)
                pe.wait_ge(s.hidt_sb, e + 1)
                for c in range(4):
                    block_in = expert_block(8 + c)
                    for half in range(2):
                        for j in range(4):
                            at = j % 2 * DM + half * 512
                            last = mm(B[2 + half][32 * j:32 * j + 32, :], HIDT[:, c * P + 32 * j:c * P + 32 * j + 32],
                                      block_in[j // 2][:, at:at + 512], c == 0, c == 3)
                    last.then_inc(s.ring_used, 1)
                pe.wait_ge(s.selt_ready, e + 1)
                pe.wait_ge(s.y_low, e + 1)
                pe.wait_ge(s.y_high, e + 1)
                for k in range(KT):
                    last = nc.tensor.matmul(B[4 + k // 2][:, (k % 2) * SEQ:(k % 2 + 1) * SEQ], YE[:, k * P:(k + 1) * P],
                                            SELT[:], start=False, stop=False)
                last.then_inc(s.acc_done, 1)

            expert(0)
            with pe.Fori(1, EXPERTS) as e:
                expert(e)
            for q in range(4):
                last = mm(B[4 + q][:], ZERO[0:1, 0:P], ZERO[0:1, :], False, True)
            last.then_inc(s.acc_done, 1)
            column_sums(4, bank=3)
            tensor_block2(pe, mm, dense_unit, column_sum, column_sums)
            tensor_block3(pe, mm, dense_unit, dense_tokens, column_sum, column_sums)

        @block.scalar
        def _(act):
            steps = [0]

            def link(ins):
                steps[0] += 1
                ins.then_inc(s.act_step, 1)
                act.wait_ge(s.act_step, steps[0])

            units_done = [0]

            def unit_done(block_no, ends):
                if ends:
                    act.wait_ge(s.ring_used, block_no + 1)
                else:
                    units_done[0] += 1
                    act.wait_ge(s.dense_mm, units_done[0])

            def fn(o, i, f, **kw):
                return nc.scalar.activation(o, i, f, **kw)

            def square(k, src):
                fn(SQ[:, k, :], src, ACT.Square).then_inc(s.norm_squared, 1)

            def squares_of_x(ready, count, after=None):
                for k in range(KT):
                    act.wait_ge(ready, count + k + 1)
                    square(k, X[:, k, :])
                    if after:
                        after(k)

            splits = [0]

            def split_high(high, full, shift=None):
                splits[0] += 1
                act.wait_ge(s.act_full, splits[0])
                high = as_r(high) if high.dtype == F32 else high
                if shift is None:
                    fn(high, full, ACT.Copy).then_inc(s.act_high, 1)
                else:
                    fn(high, full, ACT.Identity, bias=shift).then_inc(s.act_high, 1)

            def splits_passed(n):
                splits[0] += n

            def weight_high(n):
                if n >= D1_UNITS + D2_UNITS:
                    return
                blk, sub = unit_place(n)
                if n < UNITS // 2:
                    act.wait_ge(s.first_units, 16)
                else:
                    act.wait_ge(ring_loaded[blk % RING], uses(blk))
                fn(w_high[:, n % HIGHS, :], unit_weights(blk, sub), ACT.Copy).then_inc(s.w_high, 1)

            def root_table(i):
                fn(ROOT_WARM[:, i:i + 1], ones[:, 0:1], ACT.Sqrt)

            def root(i, bank=7):
                act.wait_ge(s.norm_summed, i + 1)
                fn(RS[:, i % 2, :], B[bank][:, 0:SEQ], ACT.Sqrt, scale=1.0 / DM, bias=EPS_COL).then_inc(s.norm_root, 1)

            act.dma_start(params[:], d["params"]).then_inc(s.params_in, 16)
            act.dma_start(CTXR, d["ctx"]).then_inc(s.ctx_in, 16)
            act.dma_start(X[:, :, :], d["x"]).then_inc(s.x_in, 16)
            act.dma_start(consts[:, 0:SHARED_COLS + EARLY_COLS], d["consts"]).then_inc(s.consts_in, 16)

            act.wait_ge(s.params_in, 16)
            act.wait_ge(s.zeros_ready, 1)
            fn(C2[:, :, 0:2], par("cc").rearrange("p (k m) -> p k m", m=2), ACT.Silu).then_inc(s.c_ready, 1)
            link(fn(LT, par("decay"), ACT.Abs))
            link(fn(LT, LT, ACT.Exp, scale=-1.0))
            fn(LT, LT, ACT.Ln, bias=1.0).then_inc(s.decay_soft, 1)
            link(fn(LAMT, par("lru_lam"), ACT.Abs))
            link(fn(LAMT, LAMT, ACT.Exp, scale=-1.0))
            fn(LAMT, LAMT, ACT.Ln, bias=1.0).then_inc(s.lam_soft, 1)
            fn(NEGA, par("a_log"), ACT.Exp).then_inc(s.a_exp, 1)
            act.wait_ge(s.ctx_in, 16)
            for k in range(KT):
                square(k, CTXR[:, k, :])
            act.wait_ge(s.ones_ready, 2)
            root_table(0)
            root(0)
            act.wait_ge(s.x_in, 16)
            for k in range(KT):
                square(k, X[:, k, :])
            root(1)
            act.dma_start(STARTERS, d["starters"]).then_inc(s.start_in, 16)

            def ada_copy(r):
                act.wait_ge(s.ring_used, ada_block(4 * r + 3) + 1)
                fn(ADA[r], B[ADA_BANK[r]][:], ACT.Copy).then_inc(s.ada_sb, 1)

            ada_copy(0)
            for k in range(KT):
                split_high(CTXR[:, k, :], HC[:, k, :], MOD[:, k, 1:2])
                if k < UNITS:
                    weight_high(k)
            for k in range(KT):
                split_high(HH[:, k, :], H[:, k, :], MOD[:, k, 0:1])
            for pu, (unit, a, t) in enumerate(DENSE1):
                if unit == 12:
                    act.wait_ge(s.toep_stored, 32)
                unit_done(d1_block(unit), job_ends(unit, a, t))
                src, i = B[pu % 4][:, 0:SEQ], unit % 4
                if t is not None:
                    src = B[pu % 4][:]
                    dst = tiles((28 if unit == 0 else 24 if a == "x" else 32) + 2 * t, 2)
                else:
                    dst = (KQ[:, i, :], None, KQ[:, 4 + i, :], G_[:, i, :], C_[:, i, :], XI_[:, i, :], B_[:, i, :])[unit // 4]
                fn(dst, src, ACT.Copy, scale=float(P) ** -0.5 if unit < 4 else 1.0).then_inc(s.dense_sb, 1)
                if a == "x" and unit < 4:
                    weight_high(unit + UNITS)
                if a == "x" and unit == 4 and t == TT - 1:
                    for n in range(AHEAD1):
                        weight_high(8 + n)
                if unit >= 8:
                    weight_high(unit + AHEAD1)
                if pu in (13, JOBS1 - 1):
                    ada_copy(1 if pu == 13 else 2)
                if pu == 1:
                    for kind in range(2):
                        act.wait_ge(s.toep_mm, kind + 1)
                        fn(TW[0:AH, kind, 0:TOEP], B[4 + kind][0:AH, 0:TOEP], ACT.Copy).then_inc(s.toep_sb, 1)
                    act.wait_ge(s.toep_sb, 2)
                    for kind in range(2):
                        act.dma_start(d["toep"][kind * AH:(kind + 1) * AH, :, 0:TOEP],
                                      spread(TW[0:AH, kind, 0:TOEP], 1, P)).then_inc(s.toep_stored, 16)
                    act.wait_ge(s.ramp_ready, 1)
                if pu == 6:
                    act.wait_ge(s.consts_in, 16)
                    fn(tiles(60, 8), tiles(60, 8), ACT.Exp).then_inc(s.dmat_ready, 1)
                if 6 <= pu < 6 + HEADS1:
                    h = pu - 6
                    fn(QFB[:, h, :], con("row"), ACT.Exp, scale=LG[:, h:h + 1], bias=LG[:, h:h + 1])
                    fn(QFB[:, 4 + h, :], con("row_rev"), ACT.Exp, scale=LG[:, 4 + h:5 + h])
                    fn(WFB[:, :, h], con("tok_rev"), ACT.Exp, scale=LG[:, h:h + 1])
                    fn(WFB[:, :, 4 + h], con("tok"), ACT.Exp, scale=LG[:, 4 + h:5 + h]).then_inc(s.xi_ready, 1)
                if pu == STATES_AFTER - 1:
                    act.wait_ge(s.dense_sb, pu + 1)
                    fn(tiles(36, 4), tiles(36, 4), ACT.Silu).then_inc(s.g_silu, 1)
                if pu == STATES_AFTER:
                    for a in range(2):
                        act.wait_ge(s.state_mm, a + 1)
                        fn(SFB[:, a].rearrange("p h c -> p (h c)"), B[6 + a][:], ACT.Copy).then_inc(s.state_sb, 1)
                if pu in (STATES_AFTER + 2, STATES_AFTER + 4):
                    for h in (0, 1) if pu == STATES_AFTER + 2 else (2, 3):
                        act.wait_ge(s.y_mm, h + 1)
                        fn(Y[:, h, :], B[SCORE_BANK[h]][:, 0:SEQ], ACT.Copy).then_inc(s.y_sb, 1)
                if pu == STATES_AFTER + 5:
                    act.wait_ge(s.yc_ready, 1)
                    fn(tiles(16, 4), tiles(20, 4), ACT.Square).then_inc(s.ysq_ready, 1)
                if pu == STATES_AFTER + 8:
                    act.wait_ge(s.yvar_ready, 1)
                    fn(tiles(52, 4), tiles(52, 4), ACT.Sqrt).then_inc(s.yrstd_ready, 1)
                if pu >= JOBS1 - 2:
                    split_high(MIX_HIGH[:, pu - (JOBS1 - 2), :], MIX[:, pu - (JOBS1 - 2), :])
            for k in range(2, KT):
                split_high(MIX_HIGH[:, k, :], MIX[:, k, :])
            for i in range(8):
                unit_done(d1_block(28 + i), block_ends(28 + i))
                square(i, B[(JOBS1 + i) % 4][:, 0:SEQ])
                fn(MO[:, i, :], B[(JOBS1 + i) % 4][:, 0:SEQ], ACT.Copy).then_inc(s.dense_sb, 1)
                if i == KT - 2:
                    root_table(2)
                if 28 + i + AHEAD1 < D1_UNITS:
                    weight_high(28 + i + AHEAD1)
            root(2)
            squares_of_x(s.x_ready, 0)
            root(3)
            for k in range(KT):
                act.wait_ge(s.h2_scaled, k + 1)
                fn(H[:, k, :], H[:, k, :], ACT.Identity, bias=MOD[:, 24 + k, 0:1]).then_inc(s.h2_ready, 1)
            fn(as_r(ONES_R), ones[:], ACT.Copy)
            act.wait_ge(s.logit_shift, 1)
            fn(LOGIT, LOGIT, ACT.Exp).then_inc(s.aff_exp, 1)
            for n in range(4):
                act.wait_ge(s.ht_tr, n + 1)
                spot = slice((n % 2) * 512, (n % 2 + 1) * 512)
                fn(as_r(HT_HIGH[:, n // 2, spot]), B[n][:], ACT.Copy)
                fn(HT[:, n // 2, spot], B[n][:], ACT.Copy).then_inc(s.ht_sb, 1)
            for k in range(KT):
                act.wait_ge(s.xs_mm, k + 1)
                fn(XS[:, k, 0:EXPERTS * CAP], B[k % 4][:], ACT.Copy).then_inc(s.xs_sb, 1)
            def expert(e, gates):
                act.wait_ge(s.ring_used, e * EXP_BLOCKS + gates)
                fn(SG, B[0][:], ACT.Silu).then_inc(s.silu_sb, 1)
                act.wait_ge(s.hid_tr, e + 1)
                fn(HIDT, B[0][:], ACT.Copy).then_inc(s.hidt_sb, 1)
                act.wait_ge(s.ring_used, e * EXP_BLOCKS + (EXP_BASE + 12))
                fn(YE[:, 0:512], B[2][:], ACT.Copy).then_inc(s.y_low, 1)

            expert(0, first_expert_block(3) + 1)
            with act.Fori(1, EXPERTS) as e:
                expert(e, EXP_BASE + 4)
            root_table(4)
            act.wait_ge(s.acc_done, EXPERTS + 1)
            act.dma_start(consts[:, SHARED_COLS:SHARED_COLS + LATE_COLS], d["late"]).then_inc(s.late_in, 16)
            for q in range(4):
                fn(SQ[:, 2 * q:2 * q + 2, :].rearrange("p k t -> p (k t)"), B[4 + q][:], ACT.Square).then_inc(s.norm_squared, 2)
            for q in range(4):
                last = fn(FO[:, 2 * q:2 * q + 2, :].rearrange("p k t -> p (k t)"), B[4 + q][:], ACT.Copy)
            last.then_inc(s.ffn_sb, 1)
            root(4, bank=3)
            for unit in range(AHEAD2):
                weight_high(D1_UNITS + unit)
            scalar_block2(act, fn, link, square, squares_of_x, root_table, root, unit_done, units_done, weight_high, split_high, splits_passed)
            scalar_block3(act, fn, link, squares_of_x, root_table, root, unit_done, weight_high, split_high)

        @block.vector
        def _(dve):
            steps = [0]
            v = nc.vector

            def link(ins):
                steps[0] += 1
                ins.then_inc(s.dve_step, 1)
                dve.wait_ge(s.dve_step, steps[0])

            def mark(ins):
                steps[0] += 1
                ins.then_inc(s.dve_step, 1)
                return steps[0]

            splits = [0]

            def split_low(full, high):
                splits[0] += 1
                dve.wait_ge(s.act_high, splits[0])
                v.tensor_tensor(as_r(full), full, as_r(high) if high.dtype == F32 else high,
                                ALU.subtract).then_inc(s.act_low, 1)

            def splits_passed(n):
                splits[0] += n

            def norm_invert(i):
                dve.wait_ge(s.norm_root, i + 1)
                v.reciprocal(RS[:, i % 2, :], RS[:, i % 2, :]).then_inc(s.norm_inverted, 1)
                dve.wait_ge(s.norm_inverted, i + 1)

            def times_rstd(i, dst, src, gain, k):
                return v.scalar_tensor_tensor(out=dst[:, k, :], in0=src[:, k, :], scalar=gain[:, k:k + 1],
                                              in1=RS[:, i % 2, :], op0=ALU.mult, op1=ALU.mult)

            def norm_to(i, dst, src, gain, high):
                for k in range(KT + 1):
                    if k < KT:
                        times_rstd(i, dst, src, gain, k).then_inc(s.act_full, 1)
                    if k:
                        split_low(dst[:, k - 1, :], high[:, k - 1, :])

            def final_norm(i, gain):
                for k in range(KT):
                    times_rstd(i, X, X, gain, k).then_inc(s.out_ready, 1)

            def norm_shifted(i, dst, src, gain, shift, high):
                for k in range(KT + 1):
                    if k < KT:
                        times_rstd(i, dst, src, gain, k).then_inc(s.act_full, 1)
                    if k:
                        splits[0] += 1
                        dve.wait_ge(s.act_high, splits[0])
                        hi = high[:, k - 1, :]
                        v.scalar_tensor_tensor(out=as_r(dst[:, k - 1, :]), in0=dst[:, k - 1, :], scalar=shift[:, k - 1:k],
                                               in1=as_r(hi) if hi.dtype == F32 else hi, op0=ALU.add,
                                               op1=ALU.subtract).then_inc(s.act_low, 1)

            def add_normed(i, src, gain):
                scaled = mark(times_rstd(i, src, src, gain, 0))
                for k in range(KT):
                    done = scaled
                    if k + 1 < KT:
                        scaled = mark(times_rstd(i, src, src, gain, k + 1))
                    dve.wait_ge(s.dve_step, done)
                    v.tensor_tensor(X[:, k, :], X[:, k, :], src[:, k, :], ALU.add).then_inc(s.x_ready, 1)

            v.memset(ones[:], 1.0).then_inc(s.ones_ready, 1)
            v.memset(EPS_COL, EPS).then_inc(s.ones_ready, 1)
            v.memset(small(0, KT * 32), 0.0).then_inc(s.zeros_ready, 1)
            dve.wait_ge(s.params_in, 16)
            dve.wait_ge(s.decay_soft, 1)
            v.scalar_tensor_tensor(out=LG, in0=par("decay"), scalar=0.0, in1=LT, op0=ALU.min,
                                   op1=ALU.subtract).then_inc(s.decay_ready, 1)
            def modulation(r):
                dve.wait_ge(s.ada_tr, r + 1)
                bias = par("b_ada", 16 * r, 16 * r + 16).rearrange("p (j q) -> p j q", j=4)
                v.tensor_tensor(MOD[:, 16 * r:16 * r + 16, :].rearrange("p (j q) s -> p j q s", j=4),
                                B[ADA_BANK[r] + 1][:].rearrange("p (q j m) -> p j q m", q=4, j=4)[:, :, :, 0:2],
                                spread(bias, 3, 2), ALU.add).then_inc(s.mod_ready, 1)
                dve.wait_ge(s.mod_ready, r + 1)

            def plus_one_times(o, scale, gain):
                link(v.scalar_tensor_tensor(out=o, in0=scale, scalar=1.0, in1=gain, op0=ALU.add, op1=ALU.mult))

            norm_invert(0)
            norm_invert(1)
            modulation(0)
            for a in range(2):
                plus_one_times(A1[:, a, :], MOD[:, 8:16, a], par("pre_mix_g"))
            norm_shifted(0, HC, CTXR, A1[:, 1, :], MOD[:, 0:8, 1], CTXR)
            norm_shifted(1, H, X, A1[:, 0, :], MOD[:, 0:8, 0], HH)
            dve.wait_ge(s.decay_ready, 1)
            dve.wait_ge(s.start_in, 16)
            for h in range(HEADS1):
                ramp = DM_[:, h].rearrange("p m n -> p (m n)")
                link(v.tensor_scalar(ramp, start_con("ahead"), LG[:, h:h + 1], None, ALU.mult))
                last = v.scalar_tensor_tensor(out=ramp, in0=start_con("behind"), scalar=LG[:, 4 + h:5 + h], in1=ramp,
                                              op0=ALU.mult, op1=ALU.add)
            last.then_inc(s.ramp_ready, 1)

            dve.wait_ge(s.consts_in, 16)
            dve.wait_ge(s.dense_sb, 2)
            rot = ROT.rearrange("p (t h c) -> p t h c", t=TT, h=HEADS1)
            half = P // 2
            cos = spread(con("cos_t").rearrange("p (t c) -> p t c", t=TT), 2, HEADS1)
            sin = spread(con("sin_t").rearrange("p (t c) -> p t c", t=TT), 2, HEADS1)
            ta = tiles(54, 2).rearrange("p (t h c) -> p t h c", t=TT, h=HEADS1)
            tb = tiles(56, 2).rearrange("p (t h c) -> p t h c", t=TT, h=HEADS1)
            k1, k2 = KC[:, :, :, 0:half], KC[:, :, :, half:P]
            v.tensor_tensor(rot[:, :, :, 0:half], k1, cos, ALU.mult)
            link(v.tensor_tensor(ta, k2, sin, ALU.mult))
            v.tensor_tensor(rot[:, :, :, 0:half], rot[:, :, :, 0:half], ta, ALU.subtract)
            v.tensor_tensor(rot[:, :, :, half:P], k1, sin, ALU.mult)
            link(v.tensor_tensor(tb, k2, cos, ALU.mult))
            link(v.tensor_tensor(rot[:, :, :, half:P], rot[:, :, :, half:P], tb, ALU.add))
            dve.wait_ge(s.xi_ready, HEADS1)
            for a in range(2):
                v.tensor_tensor(KW[:, a].rearrange("p t (h c) -> p t h c", h=HEADS1), rot,
                                spread(WFB[:, :, 4 * a:4 * a + 4], 3, P), ALU.mult).then_inc(s.kw_ready, 1)
            modulation(1)
            link(v.tensor_tensor(G1P, MOD[:, 16:24, 0], par("post_mix_g"), ALU.mult))
            dve.wait_ge(s.dense_sb, 14)
            link(v.tensor_tensor(KQR, KQ, spread(con("cos_c"), 1, 8), ALU.mult))
            for i in range(4):
                dve.wait_ge(s.rot_mm, i + 1)
                t2 = tiles3(2 * i, 2)
                link(v.tensor_tensor(t2, B[6 + i % 2][:].rearrange("p (k t) -> p k t", k=2), spread(con("sin_c"), 1, 2), ALU.mult))
                v.tensor_tensor(KQR[:, 2 * i:2 * i + 2, :], KQR[:, 2 * i:2 * i + 2, :], t2, ALU.add).then_inc(s.qk_rot, 1)
            dve.wait_ge(s.qk_rot, 4)
            v.tensor_tensor(QFB[:, 0:4, :], QFB[:, 0:4, :], KQR[:, 4:8, :], ALU.mult)
            v.tensor_tensor(QFB[:, 4:8, :], QFB[:, 4:8, :], KQR[:, 4:8, :], ALU.mult).then_inc(s.qfb_ready, 1)
            dve.wait_ge(s.dmat_ready, 1)
            for h in range(HEADS1):
                dve.wait_ge(s.score_mm, h + 1)
                dm = DM_[:, h].rearrange("p m n -> p (m n)")
                v.tensor_tensor(dm, B[SCORE_BANK[h]][:], dm, ALU.mult).then_inc(s.sd_ready, 1)
            grid = lambda ap: ap.rearrange("p (r w) -> p r w", w=64)

            def convolution(i):
                dve.wait_ge(s.dense_sb, JOBS1 - 7 + i)
                link(v.tensor_tensor(C_[:, i, :], C_[:, i, :], XI_[:, i, :], ALU.mult))
                w = par("conv_w", 3 * i, 3 * i + 3)
                o, u = grid(XI_[:, i, :]), grid(C_[:, i, :])
                link(v.tensor_scalar(XI_[:, i, :], C_[:, i, :], w[:, 1:2], par("conv_b", i, i + 1), ALU.mult, ALU.add))
                link(v.scalar_tensor_tensor(out=o[:, :, 1:64], in0=u[:, :, 0:63], scalar=w[:, 0:1], in1=o[:, :, 1:64],
                                            op0=ALU.mult, op1=ALU.add))
                link(v.scalar_tensor_tensor(out=o[:, :, 0:63], in0=u[:, :, 1:64], scalar=w[:, 2:3], in1=o[:, :, 0:63],
                                            op0=ALU.mult, op1=ALU.add))

            def convolution_gate(i):
                dve.wait_ge(s.dense_sb, JOBS1 - 3 + i)
                v.tensor_tensor(MIX[:, i, :], XI_[:, i, :], B_[:, i, :], ALU.mult).then_inc(s.act_full, 1)

            convolution(0)
            dve.wait_ge(s.y_sb, 4)
            for i in range(2):
                dve.wait_ge(s.mean_mm, i + 1)
                last = v.scalar_tensor_tensor(out=tiles(20 + 2 * i, 2), in0=B[6 + i][:], scalar=-1.0 / P, in1=tiles(16 + 2 * i, 2),
                                              op0=ALU.mult, op1=ALU.add)
            last.then_inc(s.yc_ready, 1)
            convolution(1)
            for i in range(2):
                dve.wait_ge(s.var_mm, i + 1)
                link(v.tensor_scalar(tiles(52 + 2 * i, 2), B[6 + i][:], 1.0 / P, EPS, ALU.mult, ALU.add))
            v.reciprocal(tiles(52, 4), tiles(52, 4)).then_inc(s.yvar_ready, 1)
            convolution(2)
            convolution(3)
            dve.wait_ge(s.yrstd_ready, 1)
            link(v.tensor_tensor(YC, YC, R4, ALU.mult))
            for i in range(3):
                convolution_gate(i)
            split_low(MIX[:, 0, :], MIX_HIGH[:, 0, :])
            convolution_gate(3)
            dve.wait_ge(s.g_silu, 1)
            for h in range(HEADS1):
                v.scalar_tensor_tensor(out=MIX[:, 4 + h, :], in0=YC[:, h, :], scalar=par("ret_norm_g", h, h + 1),
                                       in1=G_[:, h, :], op0=ALU.mult, op1=ALU.mult).then_inc(s.act_full, 1)
            for k in range(1, KT):
                split_low(MIX[:, k, :], MIX_HIGH[:, k, :])

            modulation(2)
            plus_one_times(A2, MOD[:, 32:40, 0], par("pre_ffn_g"))
            link(v.tensor_tensor(G2P, MOD[:, 40:48, 0], par("post_ffn_g"), ALU.mult))
            norm_invert(2)
            dve.wait_ge(s.dense_sb, JOBS1 + 8)
            add_normed(2, MO, G1P)
            norm_invert(3)
            for k in range(KT):
                times_rstd(3, H, X, A2, k).then_inc(s.h2_scaled, 1)
            v.memset(ZERO[0:1, :], 0.0)
            v.memset(XS[:, :, EXPERTS * CAP:], 0.0)

            dve.wait_ge(s.router_mm, 1)
            v.tensor_tensor(LOGIT[:, 0, :], B[4][:, 0:EXPERTS], par("b_router"), ALU.add)
            link(v.tensor_tensor(LOGIT[:, 1, :], B[5][:, 0:EXPERTS], par("b_router"), ALU.add))
            link(v.tensor_reduce(RMAX, LOGIT, AXX, ALU.max))
            v.tensor_tensor(LOGIT, LOGIT, spread(RMAX, 2, EXPERTS), ALU.subtract).then_inc(s.logit_shift, 1)
            dve.wait_ge(s.aff_exp, 1)
            link(v.tensor_reduce(RSUM, LOGIT, AXX, ALU.add))
            link(v.reciprocal(RSUM, RSUM))
            v.tensor_tensor(LOGIT, LOGIT, spread(RSUM, 2, EXPERTS), ALU.mult).then_inc(s.aff_ready, 1)
            dve.wait_ge(s.aff_tr, 1)
            at = AT[0:EXPERTS, :]
            link(v.tensor_copy(at, B[7][0:EXPERTS, 0:SEQ]))
            for r in range(CAP // 8):
                best = VAL[0:EXPERTS, 8 * r:8 * r + 8]
                link(v.max(best, at))
                link(v.max_index(idx_u[:, 8 * r:8 * r + 8], best, at))
                link(v.match_replace(at, best, at, -1.0))
            link(v.tensor_copy(IDXF[0:EXPERTS, :], idx_u[:]))
            e16 = EXPERTS
            v.tensor_tensor(as_r(R16[0:e16, :].rearrange("p (e c) -> p e c", e=e16)), spread(IDXF[0:e16, :], 1, e16),
                            spread(ident[0:e16, 0:e16], 2, CAP), ALU.mult)
            v.tensor_copy(IDX4[0:e16, :].rearrange("p (j c) -> p j c", j=4), spread(IDXF[0:e16, :], 1, 4))
            v.tensor_copy(VAL4[0:e16, :].rearrange("p (j c) -> p j c", j=4), spread(VAL[0:e16, :], 1, 4)).then_inc(s.topk_ready, 1)
            dve.wait_ge(s.slot_mm, 1)
            for t in range(TT):
                last = v.tensor_scalar(as_r(SEL[:, t, :]), B[6][:], con("tok")[:, t:t + 1], None, ALU.is_equal)
            last.then_inc(s.sel_ready, 1)
            dve.wait_ge(s.slot_mm, 2)
            v.tensor_copy(small(460, 32), B[7][:, 0:32]).then_inc(s.slots_ready, 1)

            dve.wait_ge(s.xs_sb, KT)
            dve.wait_ge(s.slots_ready, 1)
            v.tensor_copy(XSE, XS[:, :, 0:CAP]).then_inc(s.xse_ready, 1)
            def expert(e):
                dve.wait_ge(s.ring_used, e * EXP_BLOCKS + (EXP_BASE + 8))
                dve.wait_ge(s.silu_sb, e + 1)
                v.tensor_tensor(HID, SG, B[1][:], ALU.mult).then_inc(s.hid_ready, 1)
                v.tensor_copy(XSE, XS[:, :, bass.ds(e * CAP + CAP, CAP)]).then_inc(s.xse_ready, 1)
                v.tensor_scalar(SELT, con("row"), SLOT_TOK[:, bass.ds(e, 1)], SLOT_GATE[:, bass.ds(e, 1)],
                                ALU.is_equal, ALU.mult).then_inc(s.selt_ready, 1)
                dve.wait_ge(s.ring_used, e * EXP_BLOCKS + (EXP_BASE + 12))
                v.tensor_copy(YE[:, 512:1024], B[3][:]).then_inc(s.y_high, 1)

            expert(0)
            with dve.Fori(1, EXPERTS) as e:
                expert(e)
            dve.wait_ge(s.ffn_sb, 1)
            norm_invert(4)
            add_normed(4, FO, G2P)
            vector_block2(dve, v, link, norm_invert, norm_to, add_normed, split_low, splits_passed)
            vector_block3(dve, v, link, norm_invert, norm_to, final_norm, split_low)


def bucket_table():
    dist = 2 * P - 1 - np.arange(TOEP)
    n = np.maximum(dist, 0)
    ratio = np.log(np.maximum(n, 1).astype(np.float32) / np.float32(REL_EXACT)) / np.float32(math.log(REL_DIST / REL_EXACT))
    large = np.minimum(REL_EXACT + (ratio * np.float32(REL_BUCKETS - REL_EXACT)).astype(np.int32), REL_BUCKETS - 1)
    bucket = np.where(n < REL_EXACT, n, large)
    out = np.zeros((P, 2, TOEP), np.float32)
    for kind, limit in enumerate((P, SEQ)):
        row = np.where((dist >= 0) & (dist < limit), bucket, REL_BUCKETS)
        out[row, kind, np.arange(TOEP)] = 1.0
    return out.reshape(P, 2 * TOEP)


def const_table():
    f = np.float32
    p, n = np.arange(P), np.arange(SEQ)
    shared, late, start = (np.zeros((P, n), f) for n in (SHARED_COLS + EARLY_COLS, LATE_COLS, START_COLS))

    def put(name, a):
        t, (at, cols) = ((late, LATE_AT[name]) if name in LATE_AT else (start, START_AT[name]) if name in START_AT
                         else (shared, C_AT[name]))
        a = np.asarray(a, f)
        t[:, at:at + cols] = np.broadcast_to(a.reshape(a.shape[0], -1) if a.ndim > 1 else a[None], (P, cols))

    put("ident", np.eye(P))
    swap = np.zeros((P, P), f)
    swap[np.arange(64) + 64, np.arange(64)] = -1.0
    swap[np.arange(64), np.arange(64) + 64] = 1.0
    put("swap", swap)
    half = P // 2
    inv = f(1.0) / np.power(f(10000.0), np.arange(half, dtype=f) / f(half))
    ang = (SEQ + n).astype(f)[None, :] * inv[p % half][:, None]
    put("cos_c", np.cos(ang)), put("sin_c", np.sin(ang))
    pos = p[:, None] + P * np.arange(TT)[None, :]
    ang = pos.astype(f)[:, :, None] * inv[None, None, :]
    put("cos_t", np.cos(ang)), put("sin_t", np.sin(ang))
    rel = n[None, None, :] - pos[:, :, None]
    put("ahead", np.maximum(rel, 0)), put("behind", np.maximum(-rel, 0))
    put("row_rev", SEQ - n), put("row", n)
    put("tok", pos), put("tok_rev", SEQ - 1 - pos)
    c = p // 32
    starts = n % CHUNK == 0
    put("ssd_reset", ~(starts[None] & ((n // CHUNK)[None] >= c[:, None]) & ((n // CHUNK)[None] <= c[:, None] + 1)))
    chunk_of = (pos // CHUNK).T
    put("chunk_rows", c[:, None, None] == chunk_of[None])
    put("head_rows", (p % 32)[:, None] == np.arange(SSM_H)[None])
    causal = pos[:, :, None] <= n[None, None, :]
    put("causal", np.concatenate([causal[:, 0], causal[:, 1, P:]], 1))
    put("gla_reset", ~starts)
    put("gla_mask", (p[:, None] // CHUNK == p[None] // CHUNK) & (p[:, None] <= p[None]))
    put("half", np.stack([p < 64, p >= 64], 1))
    put("buckets", bucket_table())
    return shared, late, start


def kernel(**inputs):
    import concourse.bacc as bacc
    from concourse.bass_utils import run_bass_kernel_spmd

    f = np.float32
    i = {k: np.asarray(v) for k, v in inputs.items()}
    cols = lambda a: np.asarray(a).reshape(-1, P).T
    taps = lambda w: w.reshape(w.shape[0], -1, P).transpose(2, 1, 0).reshape(P, -1)
    every = lambda a: np.broadcast_to(np.asarray(a).reshape(1, -1), (P, np.asarray(a).size))

    def rows(a, at=(0,)):
        o = np.zeros((P, a.shape[1]), f)
        for r in at:
            o[r:r + a.shape[0]] = a
        return o

    pairs = np.arange(2 * FT).reshape(2, FT).T.ravel()
    by_tile = lambda a: a.reshape(a.shape[0], -1, P)[:, pairs].reshape(a.shape[0], -1)
    chunks = range(0, P, 32)
    values = {
        "cc": np.stack([cols(i["c"][0]), cols(i["c_ctx"])], -1).reshape(P, -1),
        "b_ada": cols(i["b_ada"][0]), "pre_mix_g": cols(i["pre_mix_g"][0]), "post_mix_g": cols(i["post_mix_g"][0]),
        "pre_ffn_g": cols(i["pre_ffn_g"][0]), "post_ffn_g": cols(i["post_ffn_g"][0]),
        "conv_w": taps(i["conv_w"][0]), "conv_b": cols(i["conv_b"][0]), "decay": every(i["ret_decay_logit"][0]),
        "ret_norm_g": cols(i["ret_norm_g"][0]), "b_router": every(i["b_router"][0]),
        "w_router": i["w_router"][0].reshape(KT, P, EXPERTS).transpose(1, 0, 2).reshape(P, -1),
        "mix_pre": cols(i["mix_pre_norm_2"][0]), "mix_post": cols(i["mix_post_norm_2"][0]),
        "ssm_conv_w": taps(i["ssm_conv_w_2"][0]), "ssm_conv_b": cols(i["ssm_conv_b_2"][0]),
        "dt_bias": rows(i["ssm_dt_bias_2"][0][:, None], chunks), "a_log": rows(i["ssm_a_log_2"][0][:, None], chunks),
        "ssm_d": cols(np.repeat(i["ssm_d_2"][0], SSM_P)), "ssm_norm": cols(i["ssm_norm_2"][0]),
        "lru_conv_w": taps(i["lru_conv_w_2"][0]), "lru_conv_b": cols(i["lru_conv_b_2"][0]),
        "lru_br": cols(i["lru_br_2"][0].ravel()), "lru_bi": cols(i["lru_bi_2"][0].ravel()), "lru_lam": cols(i["lru_lambda_2"][0]),
        "gate_b": cols(i["gate_b_2"][0].ravel()), "ffn_pre": cols(i["ffn_pre_norm_2"][0]), "ffn_post": cols(i["ffn_post_norm_2"][0]),
        "ffn_conv_w": taps(by_tile(i["ffn_conv_w_2"][0])), "ffn_conv_b": cols(by_tile(i["ffn_conv_b_2"])[0]),
        "norm_gain": cols(i["norm_gain_3"].ravel()), "final_gain": cols(i["final_gain_3"]),
        "gla_b_up": cols(i["gla_b_up_3"][0]), "gla_gain": cols(i["gla_norm_gain_3"][0]), "sinks": every(i["swa_sinks_3"][0]),
        "rel": rows(np.concatenate([i["rel_bias_3"], np.full((1, AH), -1e30, f)])),
        "gla_w_up": rows(i["gla_w_up_3"][0]),
    }
    params = np.zeros((P, P_COLS), f)
    for name, (at, n) in P_AT.items():
        params[:, at:at + n] = values[name]

    def units(w, pick=None):
        w = w if pick is None else w[:, pick]
        return w.reshape(KT, P, -1, P).transpose(2, 1, 0, 3)

    def blocks(parts):
        u = np.concatenate(parts)
        return np.ascontiguousarray(u.reshape(-1, UNITS, P, KT * P).transpose(0, 2, 1, 3)).reshape(-1, P, BLK)

    r = lambda a, b: np.arange(a, b)
    w1 = i["w_in"][0]
    dense1 = blocks([units(w1, np.concatenate([r(2048, 3072), r(1536, 2048), r(3072, 3584), r(512, 1536), r(0, 512)])), units(i["w_out"][0])])

    w2 = i["w_in_2"][0]
    z, xbc = r(0, 1024), r(1024, 2560)
    dt = np.zeros((DM, P), f)
    for a in chunks:
        dt[:, a:a + SSM_H] = w2[:, 2560:2576]
    w3 = i["w_in_even_3"][0]
    splits = np.cumsum([0, 256, 256, 512, 16, 512, 512, 128, 128, 512])
    aq, ak, av, ad, ag, bq, bk, bv, bg = (r(a, b) for a, b in zip(splits[:-1], splits[1:]))
    pair = (r(0, 512).reshape(2, 4, 64).transpose(1, 0, 2)).ravel()
    down_rank = np.zeros((DM, P), f)
    down_rank[:, 0:16] = w3[:, ad]
    we = i["w_out_even_3"][0][np.concatenate([r(0, 512), 512 + pair])]
    w4 = i["w_in_odd_3"][0]
    wd = i["w_ffn_down_2"][0].reshape(3, KT, P, KT, P).transpose(3, 0, 2, 1, 4).reshape(-1, P, KT, P)
    dense2 = blocks([
        units(w2, xbc), units(dt), units(w2, np.concatenate([r(3600, 4624), r(2576, 3600), z, r(4624, 6672)])),
        units(i["w_proj_lru_2"][0]), units(i["w_proj_ssm_2"][0]), units(i["w_out_2"][0]),
        units(i["w_ffn_up_2"][0].reshape(DM, -1, P)[:, pairs].reshape(DM, -1)), wd,
        units(down_rank), units(w3, np.concatenate([aq, ak, bq[pair], bk, bv, av, ag, bg[pair]])),
        units(we), units(w4), units(i["w_out_odd_3"][0])])
    lru = np.zeros((2, KT, P, P), f)
    for n, name in enumerate(("lru_wr_2", "lru_wi_2")):
        w = i[name][0].reshape(KT, 2, 64, 64)
        for b in range(2):
            lru[n, :, 64 * b:64 * b + 64, 64 * b:64 * b + 64] = w[:, b]
    by_channel = lambda a: np.ascontiguousarray(a.reshape(SEQ, KT, P).transpose(2, 1, 0))
    arrays = {
        "in_x": by_channel(i["x"][0]), "in_ctx": by_channel(i["ctx"][0]), "in_params": params,
        "in_lru_w": np.ascontiguousarray(lru.transpose(2, 0, 1, 3)).reshape(P, -1), "in_w_ada": i["w_ada"][0],
        "in_dense1": dense1, "in_dense2": dense2, "in_w_gate": i["w_gate"][0].reshape(-1, DEXP),
        "in_w_up": i["w_up"][0].reshape(-1, DEXP), "in_w_down": i["w_down"][0].reshape(-1, DM),
    }
    arrays["in_consts"], arrays["in_late"], arrays["in_starters"] = const_table()
    nc = bacc.Bacc("TRN2", target_bir_lowering=False, num_devices=1)
    d = {n[3:]: nc.dram_tensor(n, a.shape, F32, kind="ExternalInput").ap() for n, a in arrays.items()}
    d["toep"] = nc.dram_tensor("bias_diagonals", (2 * AH, P, TPITCH), F32).ap()
    out = nc.dram_tensor("out_x", (P, KT, SEQ), F32, kind="ExternalOutput").ap()
    program(nc, d, out)
    got = run_bass_kernel_spmd(nc, [arrays], core_ids=[0]).results[0]["out_x"]
    return np.ascontiguousarray(got.transpose(2, 1, 0)).reshape(1, SEQ, DM)
```
